# Optimizing a Trainium2 kernel written in Bass

```python
import math
import jax, jax.numpy as jnp
from jax import lax
import numpy as np

D_MODEL = 1024
BATCH = 1
SEQ = 512
DEPTH = 1
DEC_BATCH = 8
DEC_SEQ = 8
PAST_LEN = 2048
PAGE_SIZE = 128

H_A = 8
DH_A = D_MODEL // 16
A_W = H_A * DH_A
MOBA_BLOCK = 256
MOBA_TOPK = 3
MOBA_Q_CHUNK = 64
ROT_DIMS = DH_A // 4
ROPE_THETA = 500000.0
H_M = 4
DH_M = D_MODEL // 8
M_W = H_M * DH_M
MLSTM_CHUNK = 128
FORGET_BIAS_LO = 3.0
FORGET_BIAS_HI = 6.0
D_FF = 4 * D_MODEL
RMS_EPS = 1e-6
SPLIT_SIZES = (A_W, A_W, A_W, M_W, M_W, M_W, M_W, H_M, H_M, D_MODEL, D_MODEL)
D_IN = sum(SPLIT_SIZES)

kernel_name = 'moba_mlstm_gated_hybrid_step'

def _rmsnorm(x, g):
    xf = x.astype(jnp.float32)
    y = xf * lax.rsqrt(jnp.mean(xf * xf, axis=-1, keepdims=True) + RMS_EPS)
    return (y * g.astype(jnp.float32)).astype(x.dtype)

def _rotary(x, pos):
    half = ROT_DIMS // 2
    inv = ROPE_THETA ** (-jnp.arange(half, dtype=jnp.float32) * 2.0 / ROT_DIMS)
    ang = pos[:, None] * inv[None, :]
    cos = jnp.cos(ang)[:, None, :]
    sin = jnp.sin(ang)[:, None, :]
    xf = x.astype(jnp.float32)
    x1 = xf[..., :half]
    x2 = xf[..., half:ROT_DIMS]
    out = jnp.concatenate([x1 * cos - x2 * sin, x2 * cos + x1 * sin, xf[..., ROT_DIMS:]], axis=-1)
    return out.astype(x.dtype)

def _project(x, g_pre_mix, w_in, b_if, pos):
    B, S, _ = x.shape
    h = _rmsnorm(x, g_pre_mix)
    z = h @ w_in
    splits = [int(s) for s in np.cumsum(SPLIT_SIZES)[:-1]]
    qa, ka, va, qm, km, vm, om, ip, fp, ga, gm = jnp.split(z, splits, axis=-1)
    qa = _rotary(qa.reshape(B, S, H_A, DH_A), pos)
    ka = _rotary(ka.reshape(B, S, H_A, DH_A), pos)
    va = va.reshape(B, S, H_A, DH_A)
    qm = qm.reshape(B, S, H_M, DH_M)
    km = km.reshape(B, S, H_M, DH_M) * (DH_M ** -0.5)
    vm = vm.reshape(B, S, H_M, DH_M)
    gates = jnp.concatenate([ip, fp], axis=-1).astype(jnp.float32) + b_if.astype(jnp.float32)
    i_pre = gates[..., :H_M]
    log_f = jax.nn.log_sigmoid(gates[..., H_M:])
    return qa, ka, va, qm, km, vm, om, i_pre, log_f, ga, gm

def _mlstm(q, k, v, o_pre, i_pre, log_f, C0, n0, m0):
    B, S, H, D = q.shape
    f32 = jnp.float32
    L = math.gcd(S, MLSTM_CHUNK)
    n_chunks = S // L

    def to_chunks(a):
        return jnp.moveaxis(a.astype(f32).reshape((B, n_chunks, L) + a.shape[2:]), 1, 0)

    xs = (to_chunks(q), to_chunks(k), to_chunks(v), to_chunks(i_pre), to_chunks(log_f))
    causal = jnp.tril(jnp.ones((L, L), dtype=bool))[None, :, :, None]

    def step(carry, inp):
        C, n, m = carry
        qc, kc, vc, ic, fc = inp
        b = jnp.cumsum(fc, axis=1)
        logD = b[:, :, None, :] - b[:, None, :, :] + ic[:, None, :, :]
        logD = jnp.where(causal, logD, -jnp.inf)
        m_t = jnp.maximum(m[:, None, :] + b, jnp.max(logD, axis=2))
        wD = jnp.exp(logD - m_t[:, :, None, :])
        w_prev = jnp.exp(m[:, None, :] + b - m_t)
        A = jnp.einsum('bthd,bshd->btsh', qc, kc) * wD
        num = jnp.einsum('btsh,bshd->bthd', A, vc) + w_prev[..., None] * jnp.einsum('bhde,bthe->bthd', C, qc)
        den = jnp.sum(A, axis=2) + w_prev * jnp.einsum('bhd,bthd->bth', n, qc)
        hc = num / jnp.maximum(jnp.abs(den), jnp.exp(-m_t))[..., None]
        m_new = m_t[:, -1]
        decay = jnp.exp(m + b[:, -1] - m_new)
        ws = jnp.exp(b[:, -1:, :] - b + ic - m_new[:, None, :])
        C_new = decay[..., None, None] * C + jnp.einsum('bsh,bshd,bshe->bhde', ws, vc, kc)
        n_new = decay[..., None] * n + jnp.einsum('bsh,bshd->bhd', ws, kc)
        return (C_new, n_new, m_new), hc

    init = (C0.astype(f32), n0.astype(f32), m0.astype(f32))
    (C, n, m), hs = lax.scan(step, init, xs)
    h = jnp.moveaxis(hs, 0, 1).reshape(B, S, H, D)
    h = jax.nn.sigmoid(o_pre.astype(f32)).reshape(B, S, H, D) * h
    return h.astype(q.dtype), C, n, m

def _moba_select(q, k_mean, j):
    NB = k_mean.shape[1]
    K = min(MOBA_TOPK, NB)
    s = jnp.einsum('bthd,bnhd->bhtn', q.astype(jnp.float32), k_mean)
    s = jnp.where(jnp.arange(NB) < j, s, -jnp.inf)
    _, idx = lax.top_k(s, K)
    valid = jnp.arange(K) < j
    return idx, valid

def _moba_core(q, k_sel, v_sel, sel_valid, k_own, v_own, own_mask):
    scale = DH_A ** -0.5
    s_own = jnp.einsum('bthd,bohd->bhto', q, k_own).astype(jnp.float32) * scale
    s_own = jnp.where(own_mask[None, None], s_own, -jnp.inf)
    if k_sel is None:
        p = jax.nn.softmax(s_own, axis=-1).astype(v_own.dtype)
        return jnp.einsum('bhto,bohd->bthd', p, v_own)
    B, H, T, K, L, D = k_sel.shape
    s_sel = jnp.einsum('bthd,bhtkld->bhtkl', q, k_sel).astype(jnp.float32) * scale
    s_sel = jnp.where(sel_valid[:, None], s_sel, -jnp.inf).reshape(B, H, T, K * L)
    p = jax.nn.softmax(jnp.concatenate([s_sel, s_own], axis=-1), axis=-1).astype(v_own.dtype)
    out = jnp.einsum('bhtn,bhtnd->bthd', p[..., :K * L], v_sel.reshape(B, H, T, K * L, D))
    return out + jnp.einsum('bhto,bohd->bthd', p[..., K * L:], v_own)

def _moba_prompt(q, k, v):
    B, S, H, D = q.shape
    nb_full = S // MOBA_BLOCK
    nb_tot = -(-S // MOBA_BLOCK)
    pad = nb_tot * MOBA_BLOCK - S
    k_pad = jnp.pad(k, ((0, 0), (0, pad), (0, 0), (0, 0)))
    v_pad = jnp.pad(v, ((0, 0), (0, pad), (0, 0), (0, 0)))
    qc_len = math.gcd(S, MOBA_Q_CHUNK)
    if nb_full > 0:
        kb = k[:, :nb_full * MOBA_BLOCK].reshape(B, nb_full, MOBA_BLOCK, H, D)
        vb = v[:, :nb_full * MOBA_BLOCK].reshape(B, nb_full, MOBA_BLOCK, H, D)
        k_mean = jnp.mean(kb, axis=2, dtype=jnp.float32)
    b_i = jnp.arange(B)[:, None, None, None]
    h_i = jnp.arange(H)[None, :, None, None]

    def chunk(c):
        s0 = c * qc_len
        qc = lax.dynamic_slice_in_dim(q, s0, qc_len, axis=1)
        j = s0 // MOBA_BLOCK
        start = j * MOBA_BLOCK
        k_own = lax.dynamic_slice_in_dim(k_pad, start, MOBA_BLOCK, axis=1)
        v_own = lax.dynamic_slice_in_dim(v_pad, start, MOBA_BLOCK, axis=1)
        own_mask = (start + jnp.arange(MOBA_BLOCK))[None, :] <= (s0 + jnp.arange(qc_len))[:, None]
        if nb_full > 0:
            idx, valid = _moba_select(qc, k_mean, j)
            k_sel = kb[b_i, idx, :, h_i]
            v_sel = vb[b_i, idx, :, h_i]
        else:
            k_sel, v_sel, valid = None, None, None
        return _moba_core(qc, k_sel, v_sel, valid, k_own, v_own, own_mask)

    out = lax.map(chunk, jnp.arange(S // qc_len))
    return jnp.moveaxis(out, 0, 1).reshape(B, S, H, D)

def _moba_sample(q, k, v, cache_k, cache_v, page_table):
    DB, T, H, D = q.shape
    n_pages = page_table.shape[1]
    ps = cache_k.shape[1]
    past = n_pages * ps
    ppb = MOBA_BLOCK // ps
    nb_full = past // MOBA_BLOCK
    r_own = past - nb_full * MOBA_BLOCK
    own_pages = page_table[:, nb_full * ppb:]
    k_own = jnp.concatenate([cache_k[own_pages].reshape(DB, r_own, H, D), k], axis=1)
    v_own = jnp.concatenate([cache_v[own_pages].reshape(DB, r_own, H, D), v], axis=1)
    own_mask = jnp.concatenate([jnp.ones((T, r_own), dtype=bool),
                                jnp.tril(jnp.ones((T, T), dtype=bool))], axis=1)
    if nb_full > 0:
        kb_past = cache_k[page_table[:, :nb_full * ppb]].reshape(DB, nb_full, MOBA_BLOCK, H, D)
        k_mean = jnp.mean(kb_past, axis=2, dtype=jnp.float32)
        idx, valid = _moba_select(q, k_mean, nb_full)
        logical = idx[..., None] * ppb + jnp.arange(ppb)
        phys = page_table[jnp.arange(DB)[:, None, None, None, None], logical]
        h_i = jnp.arange(H)[None, :, None, None, None]
        K = idx.shape[-1]
        k_sel = cache_k[phys, :, h_i].reshape(DB, H, T, K, MOBA_BLOCK, D)
        v_sel = cache_v[phys, :, h_i].reshape(DB, H, T, K, MOBA_BLOCK, D)
    else:
        k_sel, v_sel, valid = None, None, None
    return _moba_core(q, k_sel, v_sel, valid, k_own, v_own, own_mask)

def _merge_mlp(x, att, ml, ga, gm, w_attn_br, w_mlstm_br, w_out, g_post_mix, g_pre_mlp, w_up, w_down, g_post_mlp):
    B, S, _ = x.shape
    ya = att.reshape(B, S, A_W) @ w_attn_br
    ym = ml.reshape(B, S, M_W) @ w_mlstm_br
    u = jax.nn.sigmoid(ga) * ya + jax.nn.sigmoid(gm) * ym
    x = x + _rmsnorm(u @ w_out, g_post_mix)
    h = _rmsnorm(x, g_pre_mlp)
    f = jnp.square(jax.nn.relu(h @ w_up)) @ w_down
    return x + _rmsnorm(f, g_post_mlp)

def setup_inputs(seed: int = 0) -> dict:
    key = jax.random.key(seed)
    ks = jax.random.split(key, 24)
    n_pages = PAST_LEN // PAGE_SIZE
    n_pool = (DEC_BATCH * n_pages * 5) // 4
    nrm = jax.random.normal
    f32 = jnp.float32
    x_prompt = nrm(ks[0], (BATCH, SEQ, D_MODEL), f32)
    x_sample = nrm(ks[1], (DEC_BATCH, DEC_SEQ, D_MODEL), f32)
    cache_k = nrm(ks[2], (n_pool, PAGE_SIZE, H_A, DH_A), f32)
    cache_v = nrm(ks[3], (n_pool, PAGE_SIZE, H_A, DH_A), f32)
    state_C = 0.3 * nrm(ks[4], (DEC_BATCH, H_M, DH_M, DH_M), f32)
    state_n = 0.3 * nrm(ks[5], (DEC_BATCH, H_M, DH_M), f32)
    state_m = nrm(ks[6], (DEC_BATCH, H_M), f32)
    page_table = jax.random.permutation(ks[7], n_pool)[:DEC_BATCH * n_pages].reshape(DEC_BATCH, n_pages).astype(jnp.int32)
    g_pre_mix = 1.0 + 0.05 * nrm(ks[8], (D_MODEL,), f32)
    w_in = nrm(ks[9], (D_MODEL, D_IN), f32) * D_MODEL ** -0.5
    b_if = jnp.concatenate([0.1 * nrm(ks[10], (H_M,), f32),
                            jnp.linspace(FORGET_BIAS_LO, FORGET_BIAS_HI, H_M, dtype=f32) + 0.1 * nrm(ks[11], (H_M,), f32)])
    w_attn_br = nrm(ks[12], (A_W, D_MODEL), f32) * A_W ** -0.5
    w_mlstm_br = nrm(ks[13], (M_W, D_MODEL), f32) * M_W ** -0.5
    w_out = nrm(ks[14], (D_MODEL, D_MODEL), f32) * D_MODEL ** -0.5
    g_post_mix = 1.0 + 0.05 * nrm(ks[15], (D_MODEL,), f32)
    g_pre_mlp = 1.0 + 0.05 * nrm(ks[16], (D_MODEL,), f32)
    w_up = nrm(ks[17], (D_MODEL, D_FF), f32) * D_MODEL ** -0.5
    w_down = nrm(ks[18], (D_FF, D_MODEL), f32) * D_FF ** -0.5
    g_post_mlp = 1.0 + 0.05 * nrm(ks[19], (D_MODEL,), f32)
    return {'x_prompt': x_prompt, 'x_sample': x_sample, 'cache_k': cache_k, 'cache_v': cache_v,
            'state_C': state_C, 'state_n': state_n, 'state_m': state_m, 'page_table': page_table,
            'g_pre_mix': g_pre_mix, 'w_in': w_in, 'b_if': b_if, 'w_attn_br': w_attn_br,
            'w_mlstm_br': w_mlstm_br, 'w_out': w_out, 'g_post_mix': g_post_mix, 'g_pre_mlp': g_pre_mlp,
            'w_up': w_up, 'w_down': w_down, 'g_post_mlp': g_post_mlp}

def reference(x_prompt, x_sample, cache_k, cache_v, state_C, state_n, state_m, page_table,
              g_pre_mix, w_in, b_if, w_attn_br, w_mlstm_br, w_out, g_post_mix, g_pre_mlp,
              w_up, w_down, g_post_mlp):
    f32 = jnp.float32
    Bp, Sp, _ = x_prompt.shape
    pos_p = jnp.arange(Sp, dtype=f32)
    qa, ka_p, va_p, qm, km, vm, om, ip, lf, ga, gm = _project(x_prompt, g_pre_mix, w_in, b_if, pos_p)
    att_p = _moba_prompt(qa, ka_p, va_p)
    C0 = jnp.zeros((Bp, H_M, DH_M, DH_M), f32)
    n0 = jnp.zeros((Bp, H_M, DH_M), f32)
    m0 = jnp.zeros((Bp, H_M), f32)
    ml_p, C_p, n_p, m_p = _mlstm(qm, km, vm, om, ip, lf, C0, n0, m0)
    y_prompt = _merge_mlp(x_prompt, att_p, ml_p, ga, gm, w_attn_br, w_mlstm_br, w_out,
                          g_post_mix, g_pre_mlp, w_up, w_down, g_post_mlp)
    Ds = x_sample.shape[1]
    past = page_table.shape[1] * cache_k.shape[1]
    pos_s = past + jnp.arange(Ds, dtype=f32)
    qa, ka_s, va_s, qm, km, vm, om, ip, lf, ga, gm = _project(x_sample, g_pre_mix, w_in, b_if, pos_s)
    att_s = _moba_sample(qa, ka_s, va_s, cache_k, cache_v, page_table)
    ml_s, C_s, n_s, m_s = _mlstm(qm, km, vm, om, ip, lf, state_C, state_n, state_m)
    y_sample = _merge_mlp(x_sample, att_s, ml_s, ga, gm, w_attn_br, w_mlstm_br, w_out,
                          g_post_mix, g_pre_mlp, w_up, w_down, g_post_mlp)
    return (y_prompt, y_sample, ka_p, va_p, C_p, n_p, m_p, ka_s, va_s, C_s, n_s, m_s)


_drawn_inputs = setup_inputs


def setup_inputs(seed=0):
    import zlib

    import numpy as np

    out = dict(_drawn_inputs(seed))
    spreads = {}
    factors = {}
    for name, (base, spread) in spreads.items():
        noise = np.random.default_rng([zlib.crc32(name.encode()), seed]).standard_normal(out[name].shape)
        drawn = base * np.exp(spread * noise) if base else spread * noise
        out[name] = __import__('jax').numpy.asarray(drawn.astype(out[name].dtype))
    for name, factor in factors.items():
        out[name] = (out[name] * factor).astype(out[name].dtype)
    return out
```

```python
from contextlib import ExitStack, contextmanager

import concourse.bass as bass
from concourse import mybir

ALU = mybir.AluOpType
ACT = mybir.ActivationFunctionType
F32 = mybir.dt.float32
F32R = mybir.dt.float32r
I32 = mybir.dt.int32
X = mybir.AxisListType.X
NEG = -1.0e30

P = 128
D = 1024
KT = D // P
T = 512
PT = T // P
B, S = 8, 8
NS = B * S
NT = T + NS
HALFT = NT // 2
TILES = PT + 1
HA, DH = 8, 64
HP = HA // 2
HM, DM = 4, 128
PAGE, NPAGE = 128, 16
BLOCKS, TOPK = 8, 3
PAST = NPAGE * PAGE
HALF = DH // 8
FF = 4096
EPS = 1e-6
CH = 512
QA, KA, VA, QM, KM, VM, OM = (CH * j for j in range(7))
IF0 = 7 * CH
GA0 = IF0 + 2 * HM
NSLOT = 4
AHEAD = 3
SC = DH ** -0.5
RING = 8


class Count:

    def __init__(self):
        self.base = self.n = self.per = 0
        self.i = None

    def value(self, scale=1, plus=0):
        v = (self.base + self.n) * scale + plus
        return v if self.i is None or not self.per else self.i * (self.per * scale) + v

    def add(self, k=1):
        self.n += k
        return self.value()


class Counts:

    def __init__(self, eng):
        self.eng, self.of = eng, {}

    def __getitem__(self, name):
        return self.of.setdefault(name, Count())

    @contextmanager
    def loop(self, times, per):
        with self.eng.Fori(0, times) as i:
            for name, k in per.items():
                c = self[name]
                c.base, c.n, c.per, c.i = c.base + c.n, 0, k, i
            yield i
            for name, k in per.items():
                c = self[name]
                assert c.n == k, (name, c.n, k)
                c.base, c.n, c.per, c.i = c.base + k * times, 0, 0, None


class Order:

    def __init__(self, eng, sem, count):
        self.eng, self.sem, self.count = eng, sem, count

    def __call__(self, ins):
        ins.then_inc(self.sem, 1)
        self.eng.wait_ge(self.sem, self.count.add())


def moba_mlstm_step(
    nc: bass.Bass, x_prompt, x_sample, cache_k, cache_v, state_C, state_n, state_m, page_table,
    g_pre_mix, w_in, b_if, w_attn_br, w_mlstm_br, w_out, g_post_mix, g_pre_mlp, w_up, w_down, g_post_mlp,
    rotary,
    y_prompt, y_sample, k_prompt, v_prompt, C_prompt, n_prompt, m_prompt,
    k_sample, v_sample, C_sample, n_sample, m_sample,
):
    start = 16512
    R1 = start
    R2 = R1 + 2 * KT * NT * 4
    R3 = R2 + TILES * 7 * CH * 4
    R4 = R3 + 2 * KT * NT * 4
    RW = R4 + TILES * D * 4
    RC = RW + 3 * NSLOT * CH * 4
    at = {"R1": R1, "R2": R2, "R3": R3, "R4": R4, "RW": RW, "RC": RC}
    tops = {"R1": R2, "R2": R3, "R3": R4, "R4": RW, "RW": RC, "RC": nc.sbuf_top}

    def sb(name, shape, dt=F32, region=None, offset=None):
        size = 4
        for s in shape[1:]:
            size *= s
        where = at[region] if offset is None else offset
        if offset is None:
            at[region] = (where + size + 31) // 32 * 32
            assert at[region] <= tops[region], (name, at[region], tops[region])
        return nc.alloc_sbuf_tensor_at(name, shape, dt, offset=where)

    def pair(name, shape, region):
        return sb(name + "_hi", shape, F32R, region), sb(name + "_lo", shape, F32R, region)

    hT = pair("hT", [P, KT, NT], "R1")
    at["R1"] = R1
    attT = pair("attT", [P, HP, NT], "R1")
    mlT = pair("mlT", [P, HM, NT], "R1")
    at["R1"] = R1
    h2T = pair("h2T", [P, KT, NT], "R1")

    tok = sb("tok", [P, TILES, 7 * CH], F32, "R2")
    at["R2"] = R2
    uT = pair("uT", [P, KT, NT], "R2")
    u32 = sb("u32", [P, KT, NT], F32, offset=at["R2"])
    wide = sb("wide", [P, TILES, D], F32, "R2")
    xn = sb("xn", [P, TILES, D], F32, offset=R2 + 2 * KT * NT * 4)
    hole = [R2 + t * 7 * CH * 4 for t in range(PT)]

    sg = sb("sg", [P, 2 * KT * NT], F32, "R3")
    at["R3"] = R3
    hid = pair("hid", [P, KT, NT], "R3")

    x = sb("x", [P, TILES, D], F32, "R4")
    at["R4"] = R4
    qc = sb("qc", [P, PT, P], F32, "R4")
    kc = sb("kc", [P, PT, P], F32, "R4")
    vc = sb("vc", [P, PT, P], F32, "R4")
    QTp = sb("QTp", [P, T], F32, "R4")
    KTp = sb("KTp", [P, T], F32, "R4")
    pr = sb("pr", [P, 3, T], F32, "R4")
    prT = sb("prT", [P, 2, PT * P], F32, "R4")
    at["R4"] = R4
    mq = sb("mq", [P, HM, P], F32, "R4")
    mk = sb("mk", [P, HM, P], F32, "R4")
    mv = sb("mv", [P, HM, DM + 1], F32, "R4")
    mqT = sb("mqT", [P, HM, P], F32, "R4")
    mkT = sb("mkT", [P, HM, P], F32, "R4")
    CTn = sb("CTn", [P, HM, DM + 1], F32, "R4")
    gap = sb("gap", [P, HM, P], F32, "R4")
    wgt = sb("wgt", [P, HM, P], F32, "R4")
    mkw = sb("mkw", [P, HM, P], F32, "R4")
    mA = sb("mA", [P, HM, P], F32, offset=hole[0])
    mnum = sb("mnum", [P, HM, DM + 1], F32, offset=hole[0] + 2048)
    mout = sb("mout", [P, HM, DM], F32, offset=hole[1])
    mdg = sb("mdg", [P, HM, P], F32, offset=hole[1] + 2048)
    Cst = sb("Cst", [P, HM, DM], F32, offset=hole[1] + 4096)
    nst = sb("nst", [HM, DM], F32, offset=hole[2])
    at["R4"] = R4
    kring = sb("kring", [P, RING, CH], F32, "R4")

    base = R2
    sC = sb("sC", [P, B * HM, DM], F32, offset=base)
    sCT = sb("sCT", [P, B * HM, DM + 1], F32, offset=base + 16384)
    skw = sb("skw", [NS, B, DM], F32, offset=base + 32896 + 32)
    sqp = sb("sqp", [P, 2, B * (NS + S)], F32, offset=base + 37120)
    sgap = sb("sgap", [NS, HM, NS], F32, offset=base + 41728)
    swgt = sb("swgt", [NS, HM, NS], F32, offset=base + 42752)
    sA = sb("sA", [NS, HM, NS], F32, offset=base + 43776)
    sdg = sb("sdg", [NS, HM, NS], F32, offset=base + 44800)
    snum = sb("snum", [NS, HM, DM + 1], F32, offset=base + 45824)
    sout = sb("sout", [NS, HM, DM], F32, offset=base + 47904)
    sv = sb("sv", [NS, HM, DM + 1], F32, offset=base + 49952)
    sk = sb("sk", [NS, HM, DM], F32, offset=base + 52032)
    sqT = sb("sqT", [P, HM, NS], F32, offset=base + 54080)
    skT = sb("skT", [P, HM, NS], F32, offset=base + 55104)
    vring = sb("vring", [P, RING, CH], F32, offset=base)
    kT = sb("kT", [P, 2, HP, CH], F32, offset=base + 16384)
    sS = sb("sS", [P, PAST], F32, offset=base + 32768)
    sPT = sb("sPT", [P, 2, 4, P], F32, offset=base + 40960)
    sO = sb("sO", [P, P], F32, offset=base + 45056)
    kb = sb("kb", [P, HP, S], F32, offset=base + 45568)
    assert 56128 <= PT * 7 * CH * 4

    w32 = sb("w32", [P, NSLOT, CH], F32, "RW")
    w_hi, w_lo = pair("w", [P, NSLOT, CH], "RW")

    gB = sb("gB", [P, D], F32, "RC")
    junk = sb("junk", [P, D], F32, "RC")
    snn = sb("snn", [B, HM * DM], F32, offset=at["RC"] - 4 * D)
    ident = sb("ident", [P, P], F32, "RC")
    ones = sb("ones", [P, P], F32, "RC")
    upper = sb("upper", [P, P], F32, "RC")
    causal = sb("causal", [P, P], F32, "RC")
    causalT = sb("causalT", [P, P], F32, "RC")
    lastrow = sb("lastrow", [P, P], F32, "RC")
    same = sb("same", [NS, B, S], F32, "RC")
    supper = sb("supper", [NS, B, S], F32, "RC")
    scausal = sb("scausal", [NS, B, S], F32, "RC")
    scausalT = sb("scausalT", [NS, B, S], F32, "RC")
    slast = sb("slast", [NS, B, S], F32, "RC")
    sameT = sb("sameT", [B, NS], F32, "RC")
    rep8 = sb("rep8", [S, P], F32, "RC")
    own8 = sb("own8", [S, S], F32, "RC")
    earlier = sb("earlier", [P, BLOCKS, BLOCKS], F32, "RC")
    ownmask = sb("ownmask", [P, S], F32, "RC")
    eps = sb("eps", [P, 1], F32, "RC")
    ssq = sb("ssq", [P, TILES], F32, "RC")
    rms = sb("rms", [P, TILES], F32, "RC")
    rinv = sb("rinv", [P, TILES], F32, "RC")
    bif = sb("bif", [2 * HM, 1], F32, "RC")
    gates = sb("gates", [2 * HM, NT], F32, "RC")
    gtok = sb("gtok", [P, TILES, 2 * HM], F32, "RC")
    lf = sb("lf", [P, TILES, HM], F32, "RC")
    lt = sb("lt", [P, TILES, HM], F32, "RC")
    amx = sb("amx", [P, HA], F32, "RC")
    anx = sb("anx", [P, HA], F32, "RC")
    asum = sb("asum", [P, HA], F32, "RC")
    arec = sb("arec", [P, HA], F32, "RC")
    ma = sb("ma", [P, HM], F32, "RC")
    mM = sb("mM", [P, 2, HM], F32, "RC")
    mnM = sb("mnM", [P, HM], F32, "RC")
    mprev = sb("mprev", [P, HM], F32, "RC")
    mex = sb("mex", [P, 4, HM], F32, "RC")
    mev = sb("mev", [P, 4, HM], F32, "RC")
    mlast = sb("mlast", [P, 2, HM], F32, "RC")
    mden = sb("mden", [P, HM], F32, "RC")
    smb = sb("smb", [B, HM], F32, "RC")
    sdecb = sb("sdecb", [NS, B, HM], F32, "RC")
    sdec = sb("sdec", [P, B * HM], F32, "RC")
    smn = sb("smn", [B, 2, HM], F32, "RC")
    mnew = sb("mnew", [NS, 2, HM], F32, "RC")
    pt_sb = sb("pt_sb", [1, B * NPAGE], I32, "RC")
    QTs = sb("QTs", [P, HP, NS], F32, "RC")
    KTs = sb("KTs", [P, HP, NS], F32, "RC")
    qb = sb("qb", [P, HP, 32], F32, "RC")
    ssum = sb("ssum", [P, BLOCKS], F32, "RC")
    smax = sb("smax", [P, BLOCKS + 1], F32, "RC")
    scmp = sb("scmp", [P, BLOCKS, BLOCKS], F32, "RC")
    seq = sb("seq", [P, BLOCKS, BLOCKS], F32, "RC")
    srank = sb("srank", [P, BLOCKS], F32, "RC")
    sneg = sb("sneg", [P, BLOCKS], F32, "RC")
    smx = sb("smx", [P, 1], F32, "RC")
    snx = sb("snx", [P, 1], F32, "RC")
    sbias = sb("sbias", [P, BLOCKS], F32, "RC")
    sown = sb("sown", [P, S], F32, "RC")
    spow = sb("spow", [P, NS], F32, "RC")
    spowT = sb("spowT", [NS, P], F32, "RC")
    srs = sb("srs", [P, BLOCKS + 1], F32, "RC")
    srt = sb("srt", [P, 1], F32, "RC")
    sri = sb("sri", [P, 1], F32, "RC")
    rot = sb("rot", [P, TILES, 2 * HALF], F32, "RC")
    rt = [sb(f"rt{j}", [P, PT, 2 * HA, HALF], F32, offset=R4 + j * 2048) for j in range(4)]

    ps = nc.alloc_psum_tensor("ps", [P, 8, CH], F32)

    def sem(name):
        if name not in names:
            names[name] = stack.enter_context(nc.semaphore(name))
        return names[name]

    names = {}
    stack = ExitStack()

    def rows(t):
        return P if t < PT else NS

    def bank_rows(t):
        return slice(0, P) if t < PT else slice(P - NS, P)

    def tok_cols(t):
        return slice(t * P, (t + 1) * P) if t < PT else slice(NT - P, NT)

    def cols(t):
        return slice(t * P, t * P + rows(t))

    def wide_of(ap, n):
        return ap.unsqueeze(2).broadcast_to([ap.shape[0], ap.shape[1], n])


    def w_load(eng, n, src):
        c = n["w_step"]
        j = (c.base + c.n) % NSLOT
        u = n[f"slot{j}"]
        eng.wait_ge(sem(f"w_split{j}"), u.value())
        eng.dma_start(w32[:, j, 0:src.shape[1]], src).then_inc(sem(f"w_in{j}"), 16)
        u.add()
        c.n += 1

    def w_high(eng, n, width=CH):
        c = n["w_step"]
        j = (c.base + c.n) % NSLOT
        u = n[f"slot{j}"]
        eng.wait_ge(sem(f"w_in{j}"), u.value(16, 16))
        eng.wait_ge(sem(f"w_used{j}"), u.value())
        eng.activation(w_hi[:, j, 0:width], w32[:, j, 0:width], ACT.Copy).then_inc(sem(f"w_high{j}"), 1)
        u.add()
        c.n += 1

    def w_low(eng, n, width=CH):
        c = n["w_step"]
        j = (c.base + c.n) % NSLOT
        u = n[f"slot{j}"]
        eng.wait_ge(sem(f"w_high{j}"), u.value(1, 1))
        eng.tensor_tensor(w_lo[:, j, 0:width], w32[:, j, 0:width], w_hi[:, j, 0:width].bitcast(F32),
                          ALU.subtract).then_inc(sem(f"w_split{j}"), 1)
        u.add()
        c.n += 1

    def take_step(eng, n):
        c = n["w_step"]
        j = (c.base + c.n) % NSLOT
        u = n[f"slot{j}"]
        eng.wait_ge(sem(f"w_split{j}"), u.value(1, 1))
        u.add()
        c.n += 1
        return j

    def steps(k):
        return {"w_step": k} | {f"slot{j}": k // NSLOT for j in range(NSLOT)}

    def banks(*turns):
        free = {f"free{b}": sum(b < t for t in turns) for b in range(max(turns))}
        return free | {f"full{b}": sum(b < t - 1 for t in turns) for b in range(max(turns) - 1)}

    def fill(eng, n, b):
        eng.wait_ge(sem(f"free{b}"), n[f"free{b}"].value())
        n[f"free{b}"].add()

    def filled(ins, n, b):
        ins.then_inc(sem(f"full{b}"), 1)
        n[f"full{b}"].add()

    def drain(eng, n, b, last=False):
        if last:
            eng.wait_ge(sem(f"w_used{NSLOT - 1}"), n[f"slot{NSLOT - 1}"].value())
        else:
            eng.wait_ge(sem(f"full{b}"), n[f"full{b}"].value(1, 1))
            n[f"full{b}"].add()

    def drained(ins, n, b):
        ins.then_inc(sem(f"free{b}"), 1)
        n[f"free{b}"].add()

    def skip(n, b, last=False):
        n[f"free{b}"].add()
        if not last:
            n[f"full{b}"].add()

    THREE = ((0, 0), (0, 1), (1, 0))

    def tokens_chunk(eng, n, left, kt, ready=None):
        w = (w_hi, w_lo)
        for k in range(kt):
            j = take_step(eng, n)
            if ready:
                ready(k)
            for t in range(TILES):
                if k == 0:
                    fill(eng, n, t)
                for a, b in THREE:
                    mm = eng.matmul(ps[:, t, :], left[a][:, k, tok_cols(t)], w[b][:, j, :],
                                    start=(k == 0 and (a, b) == THREE[0]),
                                    stop=(k == kt - 1 and (a, b) == THREE[-1]))
                if k == kt - 1 and t < TILES - 1:
                    filled(mm, n, t)
            mm.then_inc(sem(f"w_used{j}"), 1)

    def features_chunk(eng, n, right, kt, nts=4):
        w = (w_hi, w_lo)
        for k in range(kt):
            j = take_step(eng, n)
            for b in range(2 * nts):
                i, h = b // 2, b % 2
                if k == 0:
                    fill(eng, n, b)
                for c, a in THREE:
                    mm = eng.matmul(ps[:, b, 0:HALFT], w[a][:, j, i * P:(i + 1) * P],
                                    right[c][:, k, h * HALFT:(h + 1) * HALFT],
                                    start=(k == 0 and (c, a) == THREE[0]),
                                    stop=(k == kt - 1 and (c, a) == THREE[-1]))
                if k == kt - 1 and b < 2 * nts - 1:
                    filled(mm, n, b)
            mm.then_inc(sem(f"w_used{j}"), 1)


    def norm_stats(eng, tag, src, ready):
        for t in range(TILES):
            ready(eng, t)
            if t:
                eng.wait_ge(sem("squares"), tag * TILES + t)
            eng.activation(junk[0:rows(t), :], src[0:rows(t), t, :], ACT.Square,
                           accum_out=ssq[0:rows(t), t:t + 1]).then_inc(sem("squares"), 1)
        eng.wait_ge(sem("squares"), tag * TILES + TILES)
        eng.activation(rms[:, :], ssq[:, :], ACT.Sqrt, bias=eps[:, :], scale=1.0 / D).then_inc(sem("rms"), 1)

    def norm_inverse(eng, tag):
        eng.wait_ge(sem("rms"), tag + 1)
        eng.reciprocal(rinv[:, :], rms[:, :]).then_inc(sem("rinv"), 1)
        eng.wait_ge(sem("rinv"), tag + 1)

    def norm_apply(eng, tag, src, dst):
        for t in range(TILES):
            r = rows(t)
            eng.scalar_tensor_tensor(out=dst[0:r, t, :], in0=src[0:r, t, :], scalar=rinv[0:r, t:t + 1],
                                     in1=gB[0:r, :], op0=ALU.mult, op1=ALU.mult).then_inc(sem("normed"), 1)

    def turn_units():
        return [(t, j) for t in range(TILES) for j in range(2)]

    def turn_pe(eng, n, tag):
        for u, (t, j) in enumerate(turn_units()):
            b = u % 8
            eng.wait_ge(sem("normed"), tag * TILES + t + 1)
            fill(eng, n, b)
            for k in range(4):
                c = (4 * j + k) * P
                mm = eng.transpose(ps[:, b, k * P:k * P + rows(t)], xn[0:rows(t), t, c:c + P],
                                   ident[0:rows(t), 0:rows(t)])
            filled(mm, n, b)

    def turned(t, j, dst):
        return dst[:, 4 * j:4 * j + 4, cols(t)]

    def in_bank(t, b):
        return ps[:, b, :].rearrange("p (k c) -> p k c", c=P)[:, :, 0:rows(t)]

    def turn_act(eng, n, tag, dst):
        for u, (t, j) in enumerate(turn_units()):
            drain(eng, n, u % 8)
            eng.activation(turned(t, j, dst[0]), in_bank(t, u % 8), ACT.Copy).then_inc(sem("turned_high"), 1)
            n[f"free{u % 8}"].add()

    def turn_dve(eng, n, tag, dst):
        for u, (t, j) in enumerate(turn_units()):
            eng.wait_ge(sem("turned_high"), (tag and 2 * TILES) + u + 1)
            n[f"full{u % 8}"].add()
            ins = eng.tensor_tensor(turned(t, j, dst[1]), in_bank(t, u % 8),
                                    turned(t, j, dst[0]).bitcast(F32), ALU.subtract)
            drained(ins, n, u % 8)

    def all_out(eng, n):
        for b in range(8):
            eng.wait_ge(sem(f"free{b}"), n[f"free{b}"].value())


    def constants(eng):
        fills = [(ident, 0.0), (ones, 1.0), (upper, 1.0), (causal, 0.0), (causalT, 0.0), (lastrow, 1.0),
                 (same, 1.0), (supper, 1.0), (scausal, 0.0), (scausalT, 0.0), (slast, 1.0), (sameT, 1.0),
                 (rep8, 1.0), (own8, 0.0), (earlier, 1.0), (eps, EPS), (ssq, 1.0), (qb, 0.0),
                 (gtok, 0.0)]
        for buf, v in fills:
            eng.memset(buf[tuple(slice(None) for _ in buf.shape)], v).then_inc(sem("filled"), 1)
        eng.wait_ge(sem("filled"), len(fills))
        batch_rows = [(ALU.is_ge, [[-S, B], [0, S]], 0, 1), (ALU.is_ge, [[S, B], [0, S]], S - 1, -1)]
        upto = (ALU.is_ge, [[S, B], [1, S]], 0, -1)
        downto = (ALU.is_ge, [[-S, B], [-1, S]], 0, 1)
        plan = [
            (ident, 1.0, [(ALU.not_equal, [[-1, P]], 0, 1)]),
            (upper, 0.0, [(ALU.is_ge, [[1, P]], 0, -1)]),
            (causal, NEG, [(ALU.is_ge, [[-1, P]], 0, 1)]),
            (causalT, NEG, [(ALU.is_ge, [[1, P]], 0, -1)]),
            (lastrow, 0.0, [(ALU.is_equal, [[0, P]], 1 - P, 1)]),
            (same, 0.0, batch_rows),
            (supper, 0.0, batch_rows + [upto]),
            (scausal, NEG, batch_rows + [downto]),
            (scausalT, NEG, batch_rows + [upto]),
            (slast, 0.0, [(ALU.is_equal, [[S, B], [0, S]], S - 1, -1)]),
            (sameT, 0.0, [(ALU.is_ge, [[1, NS]], 0, -S), (ALU.is_ge, [[-1, NS]], S - 1, S)]),
            (rep8, 0.0, [(ALU.is_equal, [[0, P // S], [-1, S]], 0, 1)]),
            (own8, NEG, [(ALU.is_ge, [[-1, S]], 0, 1)]),
            (earlier, 0.0, [(ALU.is_ge, [[1, BLOCKS], [-1, BLOCKS]], -1, 0)]),
        ]
        order = Order(eng, sem("masked"), n_masks)
        for buf, fill_with, cuts in plan:
            whole = buf[tuple(slice(None) for _ in buf.shape)]
            for op, pattern, first, by_row in cuts:
                if len(pattern) == 2 and len(buf.shape) == 2:
                    whole = buf[:, :].rearrange("p (a b) -> p a b", b=pattern[1][1])
                order(eng.affine_select(out=whole, in_=whole, compare_op=op, fill=fill_with, base=first,
                                        pattern=pattern, channel_multiplier=by_row))
        assert n_masks.value() == MASKS

    n_masks = Count()
    MASKS = 22

    def constants_ready(eng):
        eng.wait_ge(sem("masked"), MASKS)

    def load_x(eng, tag, after=None):
        if after is not None:
            after()
        for t in range(PT):
            eng.dma_start(x[:, t, :], x_prompt[0, t * P:(t + 1) * P, :]).then_inc(sem(f"{tag}{t}"), 16)
        eng.dma_start(x[0:NS, PT, :], x_sample.rearrange("b s d -> (b s) d")).then_inc(sem(f"{tag}{PT}"), 16)

    def load_g(eng, g, name="g_in"):
        eng.dma_start(gB[:, :], g.rearrange("(a n) -> a n", a=1).broadcast_to([P, D])).then_inc(sem(name), 16)


    ALL8 = steps(8)

    def sp_project(eng, n):
        def w_rows(k, first, width=CH):
            return w_in[k * P:(k + 1) * P, first:first + width]
        with n.loop(7, ALL8) as c:
            for k in range(KT):
                w_load(eng, n, w_in[k * P:(k + 1) * P, bass.ds(c * CH, CH)])
        for k in range(KT):
            w_load(eng, n, w_rows(k, IF0, P))
        with n.loop(4, ALL8) as c:
            for k in range(KT):
                w_load(eng, n, w_in[k * P:(k + 1) * P, bass.ds(c * CH + GA0, CH)])

    def pe_project(eng, n):
        with n.loop(7, ALL8 | banks(TILES)):
            tokens_chunk(eng, n, hT, KT)
        features_chunk(eng, n, hT, KT, 1)
        with n.loop(4, ALL8 | banks(8)):
            features_chunk(eng, n, hT, KT)

    def copy_tokens(eng, n, dst, mine):
        for t in range(TILES):
            if t % 2 != mine:
                skip(n, t, t == TILES - 1)
                continue
            drain(eng, n, t, t == TILES - 1)
            out, src = dst(t), ps[bank_rows(t), t, :]
            ins = eng.activation(out, src, ACT.Copy) if mine == 0 else eng.tensor_copy(out, src)
            drained(ins, n, t)

    def act_project(eng, n):
        with n.loop(7, ALL8 | banks(TILES)) as c:
            for _ in range(KT):
                w_high(eng, n)
            copy_tokens(eng, n, lambda t: tok[0:rows(t), t, bass.ds(c * CH, CH)], 0)
        for _ in range(KT):
            w_high(eng, n)
        for h in range(2):
            if h == 0:
                eng.wait_ge(sem("small_in"), 64)
            drain(eng, n, h, h == 1)
            drained(eng.activation(gates[:, h * HALFT:(h + 1) * HALFT], ps[0:2 * HM, h, 0:HALFT],
                                   ACT.Identity, bias=bif[:, :]), n, h)
        with n.loop(4, ALL8 | banks(8)) as c:
            for _ in range(KT):
                w_high(eng, n)
            for b in range(8):
                drain(eng, n, b, b == 7)
                dst = sg[:, bass.ds(c * (4 * NT) + (b // 2) * NT + (b % 2) * HALFT, HALFT)]
                drained(eng.activation(dst, ps[:, b, 0:HALFT], ACT.Sigmoid), n, b)
        projected(eng)
        for t, r in ((slice(0, PT), P), (slice(PT, TILES), NS)):
            eng.activation(tok[0:r, t, KM:KM + CH], tok[0:r, t, KM:KM + CH], ACT.Copy,
                           scale=DM ** -0.5).then_inc(sem("km_scaled"), 1)
            eng.activation(tok[0:r, t, OM:OM + CH], tok[0:r, t, OM:OM + CH],
                           ACT.Sigmoid).then_inc(sem("km_scaled"), 1)

    def dve_project(eng, n):
        with n.loop(7, ALL8 | banks(TILES)) as c:
            for _ in range(KT):
                w_low(eng, n)
            copy_tokens(eng, n, lambda t: tok[0:rows(t), t, bass.ds(c * CH, CH)], 1)
        for _ in range(KT):
            w_low(eng, n)
        for h in range(2):
            skip(n, h, h == 1)
        with n.loop(4, ALL8 | banks(8)):
            for _ in range(KT):
                w_low(eng, n)
            for b in range(8):
                skip(n, b, b == 7)

    def projected(eng, n_chunks=7):
        for t in range(TILES):
            eng.wait_ge(sem(f"free{t}"), FREE0[t] + n_chunks)

    FREE0 = [2, 2, 1, 1, 1, 1, 1, 1]

    def pool_rotary(eng):
        projected(eng)
        eng.wait_ge(sem("small_in"), 64)
        order = Order(eng, sem("rotated"), Count())
        for t, nt, r in ((slice(0, PT), PT, P), (slice(PT, TILES), 1, NS)):
            if nt == 1:
                heads = tok[0:r, PT, QA:QA + 2 * CH].rearrange("p (h d) -> p h d", d=DH)
                x1, x2 = heads[:, :, 0:HALF], heads[:, :, HALF:2 * HALF]
                shape = [r, 2 * HA, HALF]
                cos = rot[0:r, PT, 0:HALF].unsqueeze(1).broadcast_to(shape)
                sin = rot[0:r, PT, HALF:2 * HALF].unsqueeze(1).broadcast_to(shape)
                y = [b[0:r, 0, :, :] for b in rt]
            else:
                heads = tok[:, t, QA:QA + 2 * CH].rearrange("p t (h d) -> p t h d", d=DH)
                x1, x2 = heads[:, :, :, 0:HALF], heads[:, :, :, HALF:2 * HALF]
                shape = [r, PT, 2 * HA, HALF]
                cos = rot[0:r, t, 0:HALF].unsqueeze(2).broadcast_to(shape)
                sin = rot[0:r, t, HALF:2 * HALF].unsqueeze(2).broadcast_to(shape)
                y = [b[0:r, :, :, :] for b in rt]
            order(eng.tensor_tensor(y[0], x1, sin, ALU.mult))
            order(eng.tensor_tensor(y[1], x2, sin, ALU.mult))
            order(eng.tensor_tensor(y[2], x1, cos, ALU.mult))
            order(eng.tensor_tensor(y[3], x2, cos, ALU.mult))
            order(eng.tensor_tensor(x1, y[2], y[1], ALU.subtract))
            order(eng.tensor_tensor(x2, y[3], y[0], ALU.add))
        for dst, c in ((k_prompt, KA), (v_prompt, VA)):
            eng.dma_start(dst[0].rearrange("(t p) h d -> p t (h d)", p=P),
                          tok[:, 0:PT, c:c + CH]).then_inc(sem("kv_out"), 16)
        for dst, c in ((k_sample, KA), (v_sample, VA)):
            eng.dma_start(dst.rearrange("b s h d -> (b s) (h d)"),
                          tok[0:NS, PT, c:c + CH]).then_inc(sem("kv_out"), 16)

    ROTATED = 12


    def pool_heads(eng):
        with eng.Fori(0, HP) as i:
            eng.wait_ge(sem("a_turned"), i * 2)
            eng.tensor_copy(qc[:, :, :], tok[:, 0:PT, bass.ds(i * P + QA, P)]).then_inc(sem("a_copied"), 1)
            eng.tensor_copy(kc[:, :, :], tok[:, 0:PT, bass.ds(i * P + KA, P)]).then_inc(sem("a_copied"), 1)
            eng.wait_ge(sem("a_pv"), i * 8)
            eng.tensor_copy(vc[:, :, :], tok[:, 0:PT, bass.ds(i * P + VA, P)]).then_inc(sem("a_copied"), 1)

    units = [(h2, qt) for h2 in range(2) for qt in range(PT)]

    def back(i, u, k):
        return i * 8 + max(u - k + 1, 0)

    def pe_prompt(eng):
        eng.wait_ge(sem("s_qk"), 2)
        eng.wait_ge(sem("g_steps"), 4)
        with eng.Fori(0, HP) as i:
            for which, (src, b) in enumerate(((qc, 0), (kc, 1))):
                eng.wait_ge(sem("a_copied"), i * 3 + which + 1)
                eng.wait_ge(sem("a_qT" if b == 0 else "a_kT"), i)
                for t in range(PT):
                    mm = eng.transpose(ps[:, b, t * P:(t + 1) * P], src[:, t, :], ident[:, :])
                mm.then_inc(sem("a_turned"), 1)

            def scores(u):
                h2, qt = units[u]
                g = slice(h2 * DH, (h2 + 1) * DH)
                eng.wait_ge(sem("a_exp"), back(i, u, 3))
                w = (qt + 1) * P
                eng.matmul(ps[:, 2 + u % 3, 0:w], QTp[g, qt * P:(qt + 1) * P], KTp[g, 0:w],
                           start=True, stop=True).then_inc(sem("a_scores"), 1)

            eng.wait_ge(sem("a_qT"), i + 1)
            eng.wait_ge(sem("a_kT"), i + 1)
            for u in range(3):
                scores(u)
            for u in range(9):
                if u < 8:
                    h2, qt = units[u]
                    eng.wait_ge(sem("a_norm"), i * 8 + u + 1)
                    eng.wait_ge(sem("a_prT"), back(i, u, 2))
                    for k in range(qt + 1):
                        mm = eng.transpose(ps[:, 5 + u % 2, k * P:(k + 1) * P],
                                           pr[:, u % 3, k * P:(k + 1) * P], ident[:, :])
                    mm.then_inc(sem("a_prT_ps"), 1)
                if u + 3 < 8:
                    scores(u + 3)
                if u >= 1:
                    v = u - 1
                    h2, qt = units[v]
                    eng.wait_ge(sem("a_prT"), i * 8 + v + 1)
                    if v == 0:
                        eng.wait_ge(sem("a_copied"), i * 3 + 3)
                        eng.wait_ge(sem("a_out"), i)
                    for k in range(qt + 1):
                        mm = eng.matmul(ps[h2 * DH:(h2 + 1) * DH, 7, qt * P:(qt + 1) * P],
                                        vc[:, k, h2 * DH:(h2 + 1) * DH], prT[:, v % 2, k * P:(k + 1) * P],
                                        start=(k == 0), stop=(k == qt))
                    mm.then_inc(sem("a_pv"), 1)

    def act_prompt(eng):
        with eng.Fori(0, HP) as i:
            eng.wait_ge(sem("a_turned"), i * 2 + 1)
            eng.wait_ge(sem("a_scores"), i * 8)
            eng.activation(QTp[:, :], ps[:, 0, :], ACT.Copy).then_inc(sem("a_qT"), 1)
            for u in range(9):
                if u < 8:
                    w = (units[u][1] + 1) * P
                    eng.wait_ge(sem("a_max"), i * 8 + u + 1)
                    eng.wait_ge(sem("a_prT_ps"), back(i, u, 3))
                    eng.activation(pr[:, u % 3, 0:w], ps[:, 2 + u % 3, 0:w], ACT.Exp, bias=anx[:, u:u + 1],
                                   scale=SC, accum_out=asum[:, u:u + 1]).then_inc(sem("a_exp"), 1)
                if u >= 1:
                    v = u - 1
                    w = (units[v][1] + 1) * P
                    eng.wait_ge(sem("a_prT_ps"), i * 8 + v + 1)
                    eng.wait_ge(sem("a_pv"), back(i, v, 2))
                    eng.activation(prT[:, v % 2, 0:w], ps[:, 5 + v % 2, 0:w], ACT.Copy).then_inc(sem("a_prT"), 1)
            eng.wait_ge(sem("a_pv"), i * 8 + 8)
            eng.activation(attT_flat[0][:, bass.ds(i * NT, T)], ps[:, 7, :], ACT.Copy).then_inc(sem("a_high"), 1)

    def dve_prompt(eng):
        order = Order(eng, sem("a_steps"), Count())
        order.count.per = 24
        with eng.Fori(0, HP) as i:
            order.count.i = i
            eng.wait_ge(sem("a_turned"), i * 2 + 2)
            eng.wait_ge(sem("a_scores"), i * 8)
            eng.tensor_copy(KTp[:, :], ps[:, 1, :]).then_inc(sem("a_kT"), 1)
            for u in range(9):
                if u < 8:
                    qt = units[u][1]
                    own = ps[:, 2 + u % 3, qt * P:(qt + 1) * P]
                    eng.wait_ge(sem("a_scores"), i * 8 + u + 1)
                    order(eng.tensor_tensor(own, own, causal[:, :], ALU.add))
                    order(eng.tensor_reduce(amx[:, u:u + 1], ps[:, 2 + u % 3, 0:(qt + 1) * P], X, ALU.max))
                    eng.tensor_scalar(anx[:, u:u + 1], amx[:, u:u + 1], -SC, None, ALU.mult)\
                       .then_inc(sem("a_max"), 1)
                if u >= 1:
                    v = u - 1
                    w = (units[v][1] + 1) * P
                    eng.wait_ge(sem("a_exp"), i * 8 + v + 1)
                    order(eng.reciprocal(arec[:, v:v + 1], asum[:, v:v + 1]))
                    eng.tensor_scalar(pr[:, v % 3, 0:w], pr[:, v % 3, 0:w], arec[:, v:v + 1], None, ALU.mult)\
                       .then_inc(sem("a_norm"), 1)
            eng.wait_ge(sem("a_high"), i + 1)
            eng.tensor_tensor(attT_flat[1][:, bass.ds(i * NT, T)], ps[:, 7, :],
                              attT_flat[0][:, bass.ds(i * NT, T)].bitcast(F32), ALU.subtract)\
               .then_inc(sem("a_out"), 1)
            assert order.count.n == 24

    attT_flat = [a[:, :, :].rearrange("p h n -> p (h n)") for a in attT]
    mlT_flat = [a[:, :, :].rearrange("p h n -> p (h n)") for a in mlT]


    VIEWS = ((P, slice(0, PT)), (NS, slice(PT, TILES)))

    def pe_gates(eng):
        for t in range(TILES):
            mm = eng.transpose(ps[0:rows(t), 2, t * 8:t * 8 + 8], gates[:, cols(t)], ident[0:8, 0:8])
        mm.then_inc(sem("g_turned"), 1)
        eng.wait_ge(sem("rotated"), ROTATED)
        for b, c0 in ((0, QA), (1, KA)):
            for h in range(HP):
                mm = eng.transpose(ps[:, b, h * NS:(h + 1) * NS], tok[0:NS, PT, c0 + h * P:c0 + (h + 1) * P],
                                   ident[0:NS, 0:NS])
            mm.then_inc(sem("s_turned"), 1)

    def dve_gates(eng):
        eng.wait_ge(sem("g_turned"), 1)
        order = Order(eng, sem("g_steps"), Count())
        order(eng.tensor_copy(gtok[:, 0:PT, :], ps[:, 2, 0:PT * 8].rearrange("p (t g) -> p t g", g=8)))
        order(eng.tensor_copy(gtok[0:NS, PT, :], ps[0:NS, 2, PT * 8:PT * 8 + 8]))
        f = gtok[:, :, HM:2 * HM]
        order(eng.scalar_tensor_tensor(out=lf[:, :, :], in0=f, scalar=-1.0, in1=f, op0=ALU.mult, op1=ALU.min))
        eng.tensor_scalar(lt[:, :, :], f, 0.0, None, ALU.min).then_inc(sem("g_abs"), 1)
        eng.wait_ge(sem("g_ln"), 2)
        order(eng.tensor_tensor(lf[:, :, :], lt[:, :, :], lf[:, :, :], ALU.subtract))
        eng.wait_ge(sem("s_turned"), 2)
        eng.tensor_copy(QTs[:, :, :], ps[:, 0, 0:HP * NS].rearrange("p (h n) -> p h n", n=NS))\
           .then_inc(sem("s_qk"), 1)
        eng.tensor_copy(KTs[:, :, :], ps[:, 1, 0:HP * NS].rearrange("p (h n) -> p h n", n=NS))\
           .then_inc(sem("s_qk"), 1)

    def act_gates(eng):
        eng.wait_ge(sem("g_abs"), 1)
        eng.activation(lf[:, :, :], lf[:, :, :], ACT.Exp).then_inc(sem("g_ln"), 1)
        eng.wait_ge(sem("g_ln"), 1)
        eng.activation(lf[:, :, :], lf[:, :, :], ACT.Ln, bias=ones[:, 0:1]).then_inc(sem("g_ln"), 1)


    def pool_mlstm(eng):
        eng.wait_ge(sem("a_copied"), 3 * HP)
        eng.wait_ge(sem("a_out"), HP)
        eng.wait_ge(sem("km_scaled"), 4)
        eng.memset(mv[:, :, DM:DM + 1], 1.0).then_inc(sem("m_set"), 1)
        eng.memset(CTn[:, :, :], 0.0).then_inc(sem("m_set"), 1)
        eng.memset(mprev[:, :], 0.0).then_inc(sem("m_set"), 1)
        with eng.Fori(0, PT) as c:
            eng.wait_ge(sem("m_update"), c)
            row = lambda c0: tok_flat[:, bass.ds(c * (7 * CH) + c0, CH)].rearrange("p (h d) -> p h d", d=DM)
            eng.tensor_copy(mq[:, :, :], row(QM)).then_inc(sem("m_copied"), 1)
            eng.tensor_copy(mk[:, :, :], row(KM)).then_inc(sem("m_copied"), 1)
            eng.tensor_copy(mv[:, :, 0:DM], row(VM)).then_inc(sem("m_copied"), 1)

    tok_flat = tok[:, :, :].rearrange("p t n -> p (t n)")
    lf_flat = lf[:, :, :].rearrange("p t g -> p (t g)")
    gt_flat = gtok[:, :, :].rearrange("p t g -> p (t g)")

    def two(b, h, r=P, w=DM + 1):
        return ps[0:r, b + h // 2, (h % 2) * (DM + 1):(h % 2) * (DM + 1) + w]

    def pe_mlstm(eng):
        eng.wait_ge(sem("m_set"), 3)
        eng.wait_ge(sem("a_out"), HP)
        with eng.Fori(0, PT) as c:
            eng.wait_ge(sem("m_copied"), c * 3 + 1)
            eng.wait_ge(sem("m_num"), c)
            for h in range(HM):
                mm = eng.transpose(ps[:, 0, h * P:(h + 1) * P], mq[:, h, :], ident[:, :])
            mm.then_inc(sem("m_qT_ps"), 1)
            eng.wait_ge(sem("m_copied"), c * 3 + 2)
            for h in range(HM):
                mm = eng.transpose(ps[:, 1, h * P:(h + 1) * P], mk[:, h, :], ident[:, :])
            mm.then_inc(sem("m_kT_ps"), 1)
            eng.wait_ge(sem("m_state"), c)
            eng.matmul(ps[:, 2, 0:HM], upper[:, :], lf_flat[:, bass.ds(c * HM, HM)],
                       start=True, stop=True).then_inc(sem("m_b_ps"), 1)
            eng.wait_ge(sem("m_diag_a"), c + 1)
            eng.matmul(ps[:, 3, :], ones[:, :], mdg[:, :, :].rearrange("p h n -> p (h n)"),
                       start=True, stop=True).then_inc(sem("m_a_ps"), 1)
            eng.wait_ge(sem("m_qT"), c + 1)
            eng.wait_ge(sem("m_kT"), c + 1)
            eng.wait_ge(sem("m_low"), c)
            for h in range(HM):
                mm = eng.matmul(ps[:, 5, h * P:(h + 1) * P], mkT[:, h, :], mqT[:, h, :], start=True, stop=True)
            mm.then_inc(sem("m_qk_ps"), 1)
            for h in range(HM):
                mm = eng.matmul(two(0, h), mqT[:, h, :], CTn[:, h, :], start=True, stop=True)
            eng.wait_ge(sem("m_diag_M"), c + 1)
            eng.matmul(ps[:, 4, :], ones[:, :], mdg[:, :, :].rearrange("p h n -> p (h n)"),
                       start=True, stop=True).then_inc(sem("m_M_ps"), 1)
            eng.matmul(ps[:, 2, 8:8 + 2 * HM], lastrow[:, :], mM[:, :, :].rearrange("p a h -> p (a h)"),
                       start=True, stop=True).then_inc(sem("m_last_ps"), 1)
            eng.wait_ge(sem("m_A"), c + 1)
            eng.wait_ge(sem("m_copied"), c * 3 + 3)
            for h in range(HM):
                mm = eng.matmul(two(6, h), mA[:, h, :], mv[:, h, :], start=True, stop=True)
            mm.then_inc(sem("m_num_ps"), 1)
            eng.wait_ge(sem("m_kw"), c + 1)
            for h in range(HM):
                mm = eng.matmul(two(3, h), mkw[:, h, :], mv[:, h, :], start=True, stop=True)
            mm.then_inc(sem("m_update"), 1)
            eng.wait_ge(sem("m_h"), c + 1)
            for h in range(HM):
                mm = eng.transpose(ps[:, 5, h * P:(h + 1) * P], mout[:, h, :], ident[:, :])
            mm.then_inc(sem("m_hT_ps"), 1)
        eng.wait_ge(sem("m_state"), PT)
        for h in range(HM):
            eng.transpose(ps[:, 0, h * P:(h + 1) * P], CTn[:, h, 0:DM], ident[:, :])
        eng.transpose(ps[0:HM, 1, 0:P], CTn[:, :, DM], ident[:, :]).then_inc(sem("m_C_ps"), 1)

    def act_mlstm(eng):
        with eng.Fori(0, PT) as c:
            eng.wait_ge(sem("m_qT_ps"), c + 1)
            eng.wait_ge(sem("m_num"), c)
            eng.activation(mqT[:, :, :], ps[:, 0, :].rearrange("p (h n) -> p h n", n=P),
                           ACT.Copy).then_inc(sem("m_qT"), 1)
            eng.wait_ge(sem("m_gap"), c + 1)
            for h in range(HM):
                eng.activation(wgt[:, h, :], gap[:, h, :], ACT.Exp, bias=ma[:, h:h + 1])\
                   .then_inc(sem("m_wD"), 1)
            eng.wait_ge(sem("m_exponents"), c + 1)
            eng.activation(mev[:, :, :], mex[:, :, :], ACT.Exp).then_inc(sem("m_exps"), 1)
            eng.wait_ge(sem("m_hT_ps"), c + 1)
            eng.activation(ml_at(mlT, c)[0], ps[:, 5, :].rearrange("p (h n) -> p h n", n=P), ACT.Copy)\
               .then_inc(sem("m_high"), 1)

    def ml_at(dst, c):
        return [a[:, :, bass.ds(c * P, P)] for a in dst]

    M_STEPS = 20

    def dve_mlstm(eng):
        order = Order(eng, sem("m_steps"), Count())
        per = order.count.per = M_STEPS
        eng.wait_ge(sem("kv_out"), 64)
        eng.wait_ge(sem("m_set"), 3)
        eng.wait_ge(sem("km_scaled"), 4)
        with eng.Fori(0, PT) as c:
            order.count.i = c
            eng.wait_ge(sem("m_kT_ps"), c + 1)
            eng.tensor_copy(mkT[:, :, :], ps[:, 1, :].rearrange("p (h n) -> p h n", n=P)).then_inc(sem("m_kT"), 1)
            eng.wait_ge(sem("m_b_ps"), c + 1)
            order(eng.tensor_copy(mM[:, 1, :], ps[:, 2, 0:HM]))
            order(eng.tensor_tensor(ma[:, :], gt_flat[:, bass.ds(c * 8, HM)], mM[:, 1, :], ALU.subtract))
            idb = ident[:, :].unsqueeze(1).broadcast_to([P, HM, P])
            eng.tensor_tensor(mdg[:, :, :], idb, wide_of(ma[:, :], P), ALU.mult).then_inc(sem("m_diag_a"), 1)
            eng.wait_ge(sem("m_a_ps"), c + 1)
            order(eng.tensor_tensor(gap[:, :, :], ps[:, 3, :].rearrange("p (h n) -> p h n", n=P),
                                    causal[:, :].unsqueeze(1).broadcast_to([P, HM, P]), ALU.add))
            order(eng.tensor_reduce(mden[:, :], gap[:, :, :], X, ALU.max))
            order(eng.tensor_tensor(mM[:, 0, :], mden[:, :], mprev[:, :], ALU.max))
            order(eng.tensor_scalar(mnM[:, :], mM[:, 0, :], -1.0, None, ALU.mult))
            eng.tensor_tensor(mdg[:, :, :], idb, wide_of(mnM[:, :], P), ALU.mult).then_inc(sem("m_diag_M"), 1)
            eng.wait_ge(sem("m_M_ps"), c + 1)
            eng.tensor_tensor(gap[:, :, :], ps[:, 4, :].rearrange("p (h n) -> p h n", n=P),
                              causalT[:, :].unsqueeze(1).broadcast_to([P, HM, P]), ALU.add)\
               .then_inc(sem("m_gap"), 1)
            eng.wait_ge(sem("m_last_ps"), c + 1)
            order(eng.tensor_copy(mlast[:, :, :], ps[:, 2, 8:8 + 2 * HM].rearrange("p (a h) -> p a h", h=HM)))
            order(eng.tensor_tensor(mex[:, 0, :], mprev[:, :], mM[:, 0, :], ALU.subtract))
            order(eng.scalar_tensor_tensor(out=mex[:, 1, :], in0=mM[:, 0, :], scalar=-1.0, in1=mM[:, 1, :],
                                           op0=ALU.mult, op1=ALU.subtract))
            order(eng.tensor_tensor(mex[:, 2, :], ma[:, :], mlast[:, 0, :], ALU.subtract))
            eng.tensor_tensor(mex[:, 3, :], mprev[:, :], mlast[:, 0, :], ALU.subtract)\
               .then_inc(sem("m_exponents"), 1)
            eng.wait_ge(sem("m_qk_ps"), c + 1)
            eng.wait_ge(sem("m_wD"), c * HM + HM)
            eng.tensor_tensor(mA[:, :, :], ps[:, 5, :].rearrange("p (h n) -> p h n", n=P), wgt[:, :, :],
                              ALU.mult).then_inc(sem("m_A"), 1)
            eng.wait_ge(sem("m_exps"), c + 1)
            eng.tensor_tensor(mkw[:, :, :], mk[:, :, :], wide_of(mev[:, 2, :], P), ALU.mult)\
               .then_inc(sem("m_kw"), 1)
            eng.wait_ge(sem("m_num_ps"), c + 1)
            for h in range(0, HM, 2):
                order(eng.tensor_copy(mnum[:, h:h + 2, :], ps[:, 6 + h // 2, 0:2 * (DM + 1)]
                                      .rearrange("p (h n) -> p h n", n=DM + 1)))
            for h in range(HM):
                ins = eng.scalar_tensor_tensor(out=mnum[:, h, :], in0=two(0, h), scalar=mev[:, 0, h:h + 1],
                                               in1=mnum[:, h, :], op0=ALU.mult, op1=ALU.add)
                if h < HM - 1:
                    order(ins)
            ins.then_inc(sem("m_num"), 1)
            eng.wait_ge(sem("m_num"), c + 1)
            order(eng.scalar_tensor_tensor(out=mden[:, :], in0=mnum[:, :, DM], scalar=-1.0, in1=mnum[:, :, DM],
                                           op0=ALU.mult, op1=ALU.max))
            order(eng.tensor_tensor(mden[:, :], mden[:, :], mev[:, 1, :], ALU.max))
            order(eng.reciprocal(mden[:, :], mden[:, :]))
            for h in range(HM):
                ins = eng.scalar_tensor_tensor(
                    out=mout[:, h, :], in0=mnum[:, h, 0:DM], scalar=mden[:, h:h + 1],
                    in1=tok_flat[:, bass.ds(c * (7 * CH) + OM + h * DM, DM)], op0=ALU.mult, op1=ALU.mult)
            ins.then_inc(sem("m_h"), 1)
            eng.wait_ge(sem("m_update"), c + 1)
            for h in range(HM):
                order(eng.scalar_tensor_tensor(out=CTn[:, h, :], in0=CTn[:, h, :], scalar=mev[:, 3, h:h + 1],
                                               in1=two(3, h), op0=ALU.mult, op1=ALU.add)) if h < 2 else \
                    eng.scalar_tensor_tensor(out=CTn[:, h, :], in0=CTn[:, h, :], scalar=mev[:, 3, h:h + 1],
                                             in1=two(3, h), op0=ALU.mult, op1=ALU.add)
            eng.tensor_tensor(mprev[:, :], mlast[:, 0, :], mlast[:, 1, :], ALU.add).then_inc(sem("m_state"), 1)
            eng.wait_ge(sem("m_state"), c + 1)
            eng.wait_ge(sem("m_high"), c + 1)
            eng.tensor_tensor(ml_at(mlT, c)[1], ps[:, 5, :].rearrange("p (h n) -> p h n", n=P),
                              ml_at(mlT, c)[0].bitcast(F32), ALU.subtract).then_inc(sem("m_low"), 1)
            assert order.count.n == per, order.count.n
        eng.wait_ge(sem("m_C_ps"), 1)
        eng.tensor_copy(Cst[:, :, :], ps[:, 0, :].rearrange("p (h n) -> p h n", n=P)).then_inc(sem("m_Cout"), 1)
        eng.tensor_copy(nst[:, :], ps[0:HM, 1, 0:P]).then_inc(sem("m_Cout"), 1)

    def pool_mlstm_out(eng):
        eng.wait_ge(sem("m_Cout"), 2)
        eng.wait_ge(sem("m_state"), PT)
        eng.dma_start(C_prompt[0].rearrange("h d e -> d h e"), Cst[:, :, :]).then_inc(sem("m_out"), 16)
        eng.dma_start(n_prompt[0], nst[:, :]).then_inc(sem("m_out"), 16)
        eng.dma_start(m_prompt, mprev[0:1, :]).then_inc(sem("m_out"), 16)


    def sp_states(eng):
        eng.wait_ge(sem("m_copied"), 3 * PT)
        eng.wait_ge(sem("m_low"), PT)
        eng.wait_ge(sem("m_out"), 48)
        eng.dma_start(sC[:, :, :], state_C.rearrange("b h d e -> d (b h) e")).then_inc(sem("d_C_in"), 16)
        eng.dma_start(snn[:, :], state_n.rearrange("b h e -> b (h e)")).then_inc(sem("d_n_in"), 16)

    def pool_states(eng):
        eng.wait_ge(sem("m_copied"), 3 * PT)
        eng.wait_ge(sem("m_low"), PT)
        eng.wait_ge(sem("m_out"), 48)
        row = lambda c0: tok[0:NS, PT, c0:c0 + CH].rearrange("p (h d) -> p h d", d=DM)
        eng.memset(sv[:, :, DM:DM + 1], 1.0).then_inc(sem("m_set"), 1)
        eng.tensor_copy(sv[:, :, 0:DM], row(VM)).then_inc(sem("m_set"), 1)
        eng.tensor_copy(sk[:, :, :], row(KM)).then_inc(sem("m_set"), 1)
        eng.memset(sqp[:, :, :], 0.0).then_inc(sem("m_set"), 1)

    def pe_sample(eng):
        eng.wait_ge(sem("m_Cout"), 2)
        eng.wait_ge(sem("m_low"), PT)
        eng.wait_ge(sem("small_in"), 64)
        eng.matmul(ps[0:NS, 2, 0:HM], sameT[:, :], smb[:, :], start=True, stop=True)
        eng.matmul(ps[0:NS, 2, 8:8 + HM], supper[:, :, :].rearrange("p b s -> p (b s)"), lf[0:NS, PT, :],
                   start=True, stop=True).then_inc(sem("m_b_ps"), 1)
        for b, c0 in ((0, QM), (1, KM)):
            for h in range(HM):
                mm = eng.transpose(ps[:, b, h * NS:(h + 1) * NS], tok[0:NS, PT, c0 + h * DM:c0 + (h + 1) * DM],
                                   ident[0:NS, 0:NS])
            mm.then_inc(sem("m_qT_ps"), 1)
        eng.wait_ge(sem("m_diag_a"), PT + 1)
        eng.matmul(ps[0:NS, 5, 0:HM * NS], ones[0:NS, 0:NS], sdg[:, :, :].rearrange("p h n -> p (h n)"),
                   start=True, stop=True).then_inc(sem("m_a_ps"), 1)
        eng.wait_ge(sem("d_n_in"), 16)
        for h in range(HM):
            mm = eng.transpose(ps[:, 6, h * B:(h + 1) * B], snn[:, h * DM:(h + 1) * DM], ident[0:B, 0:B])
        mm.then_inc(sem("m_kT_ps"), 1)
        eng.wait_ge(sem("d_C_in"), 16)
        for g in range(B):
            if g >= 2:
                eng.wait_ge(sem("d_CT"), g - 1)
            for h in range(HM):
                mm = eng.transpose(ps[:, 3 + g % 2, h * P:(h + 1) * P], sC[:, g * HM + h, :], ident[:, :])
            mm.then_inc(sem("d_CT_ps"), 1)
        eng.wait_ge(sem("m_qT"), PT + 2)
        for h in range(HM):
            mm = eng.matmul(ps[0:NS, 7, h * NS:(h + 1) * NS], skT[:, h, :], sqT[:, h, :], start=True, stop=True)
        mm.then_inc(sem("m_qk_ps"), 1)
        eng.wait_ge(sem("m_diag_M"), PT + 1)
        eng.matmul(ps[0:NS, 5, 0:HM * NS], ones[0:NS, 0:NS], sdg[:, :, :].rearrange("p h n -> p (h n)"),
                   start=True, stop=True).then_inc(sem("m_M_ps"), 1)
        eng.matmul(ps[0:NS, 2, 64:64 + 2 * HM], slast[:, :, :].rearrange("p b s -> p (b s)"),
                   mM[0:NS, :, :].rearrange("p a h -> p (a h)"), start=True, stop=True)\
           .then_inc(sem("m_last_ps"), 1)
        eng.wait_ge(sem("d_CT"), B)
        for h in range(HM):
            eng.wait_ge(sem("d_qp"), h + 1)
            for b in range(B):
                mm = eng.matmul(two(3, h, NS), sqp[:, h % 2, b * NS:(b + 1) * NS], sCT[:, b * HM + h, :],
                                start=(b == 0), stop=(b == B - 1))
            mm.then_inc(sem("d_qC_ps"), 1)
        eng.wait_ge(sem("m_A"), PT + 1)
        for h in range(HM):
            mm = eng.matmul(two(0, h, NS), sA[:, h, :], sv[:, h, :], start=True, stop=True)
        mm.then_inc(sem("m_num_ps"), 1)
        eng.wait_ge(sem("d_decb"), 1)
        eng.matmul(ps[0:B, 2, 80:80 + 2 * HM], slast[:, :, 0], mnew[:, :, :].rearrange("p a h -> p (a h)"),
                   start=True, stop=True)
        eng.matmul(ps[:, 2, 96:96 + B * HM], ones[0:NS, :], sdecb[:, :, :].rearrange("p b h -> p (b h)"),
                   start=True, stop=True).then_inc(sem("d_dec_ps"), 1)
        eng.wait_ge(sem("m_kw"), PT + 1)
        eng.matmul(ps[0:B, 7, :], same[:, :, 0], sk[:, :, :].rearrange("p h d -> p (h d)"),
                   start=True, stop=True).then_inc(sem("d_n_ps"), 1)
        for h in range(HM):
            eng.wait_ge(sem("d_kwb"), h + 1)
            eng.wait_ge(sem("d_C"), h)
            for k in range(2):
                mm = eng.matmul(ps[:, 5 + k, :], tok[0:NS, PT, VM + h * DM:VM + (h + 1) * DM],
                                skw[:, 4 * k:4 * k + 4, :].rearrange("p b d -> p (b d)"), start=True, stop=True)
            mm.then_inc(sem("m_update"), 1)
        eng.wait_ge(sem("m_h"), PT + 1)
        for h in range(HM):
            mm = eng.transpose(ps[:, 0, h * NS:(h + 1) * NS], sout[:, h, :], ident[0:NS, 0:NS])
        mm.then_inc(sem("m_hT_ps"), 1)

    def act_sample(eng):
        eng.wait_ge(sem("m_qT_ps"), PT + 1)
        eng.activation(sqT[:, :, :], ps[:, 0, 0:HM * NS].rearrange("p (h n) -> p h n", n=NS), ACT.Copy)\
           .then_inc(sem("m_qT"), 1)
        for g in range(B):
            eng.wait_ge(sem("d_CT_ps"), g + 1)
            eng.activation(sCT[:, g * HM:(g + 1) * HM, 0:DM], ps[:, 3 + g % 2, :].rearrange("p (h n) -> p h n", n=P),
                           ACT.Copy).then_inc(sem("d_CT"), 1)
        eng.wait_ge(sem("m_gap"), PT + 1)
        for h in range(HM):
            eng.activation(swgt[:, h, :], sgap[:, h, :], ACT.Exp, bias=ma[0:NS, h:h + 1]).then_inc(sem("m_wD"), 1)
        eng.wait_ge(sem("m_exponents"), PT + 1)
        eng.activation(mev[0:NS, :, :], mex[0:NS, :, :], ACT.Exp).then_inc(sem("m_exps"), 1)
        eng.wait_ge(sem("m_hT_ps"), PT + 1)
        eng.activation(mlT[0][:, :, T:NT], ps[:, 0, 0:HM * NS].rearrange("p (h n) -> p h n", n=NS), ACT.Copy)\
           .then_inc(sem("m_high"), 1)

    def dve_sample(eng):
        order = Order(eng, sem("m_steps"), Count())
        order.count.base = M_STEPS * PT
        r = slice(0, NS)
        eng.wait_ge(sem("m_out"), 48)
        eng.wait_ge(sem("m_set"), 3 + 4)
        eng.wait_ge(sem("m_b_ps"), PT + 1)
        order(eng.tensor_copy(mprev[r, :], ps[r, 2, 0:HM]))
        order(eng.tensor_copy(mM[r, 1, :], ps[r, 2, 8:8 + HM]))
        order(eng.tensor_tensor(ma[r, :], gtok[r, PT, 0:HM], mM[r, 1, :], ALU.subtract))
        idb = ident[r, 0:NS].unsqueeze(1).broadcast_to([NS, HM, NS])
        eng.tensor_tensor(sdg[:, :, :], idb, wide_of(ma[r, :], NS), ALU.mult).then_inc(sem("m_diag_a"), 1)
        eng.wait_ge(sem("m_qT_ps"), PT + 2)
        eng.tensor_copy(skT[:, :, :], ps[:, 1, 0:HM * NS].rearrange("p (h n) -> p h n", n=NS))\
           .then_inc(sem("m_qT"), 1)
        eng.wait_ge(sem("m_kT_ps"), PT + 1)
        sn = sCT[:, :, DM].rearrange("p (b h) -> p h b", h=HM)
        order(eng.tensor_copy(sn, ps[:, 6, 0:HM * B].rearrange("p (h b) -> p h b", b=B)))

        def mask3(m):
            return m[:, :, :].rearrange("p b s -> p (b s)").unsqueeze(1).broadcast_to([NS, HM, NS])

        def bank3(b):
            return ps[r, b, 0:HM * NS].rearrange("p (h n) -> p h n", n=NS)

        eng.wait_ge(sem("m_a_ps"), PT + 1)
        order(eng.tensor_tensor(sgap[:, :, :], bank3(5), mask3(scausal), ALU.add))
        order(eng.tensor_reduce(mden[r, :], sgap[:, :, :], X, ALU.max))
        order(eng.tensor_tensor(mM[r, 0, :], mden[r, :], mprev[r, :], ALU.max))
        order(eng.tensor_scalar(mnM[r, :], mM[r, 0, :], -1.0, None, ALU.mult))
        eng.tensor_tensor(sdg[:, :, :], idb, wide_of(mnM[r, :], NS), ALU.mult).then_inc(sem("m_diag_M"), 1)
        eng.wait_ge(sem("m_M_ps"), PT + 1)
        eng.tensor_tensor(sgap[:, :, :], bank3(5), mask3(scausalT), ALU.add).then_inc(sem("m_gap"), 1)
        eng.wait_ge(sem("m_qT"), PT + 2)
        for h in range(2):
            eng.tensor_copy(sqp[:, h % 2, :].rearrange("p (b k) -> p b k", k=NS + S)[:, :, 0:S], sqT[:, h, :].rearrange("p (b s) -> p b s", s=S))\
               .then_inc(sem("d_qp"), 1)
        eng.wait_ge(sem("m_last_ps"), PT + 1)
        order(eng.tensor_copy(mlast[r, :, :], ps[r, 2, 64:64 + 2 * HM].rearrange("p (a h) -> p a h", h=HM)))
        order(eng.tensor_tensor(mex[r, 0, :], mprev[r, :], mM[r, 0, :], ALU.subtract))
        order(eng.scalar_tensor_tensor(out=mex[r, 1, :], in0=mM[r, 0, :], scalar=-1.0, in1=mM[r, 1, :],
                                       op0=ALU.mult, op1=ALU.subtract))
        order(eng.tensor_tensor(mex[r, 2, :], ma[r, :], mlast[r, 0, :], ALU.subtract))
        eng.tensor_tensor(mex[r, 3, :], mprev[r, :], mlast[r, 0, :], ALU.subtract).then_inc(sem("m_exponents"), 1)
        order(eng.tensor_tensor(mnew[:, 1, :], mlast[r, 0, :], mlast[r, 1, :], ALU.add))
        eng.wait_ge(sem("m_qk_ps"), PT + 1)
        eng.wait_ge(sem("m_wD"), PT * HM + HM)
        eng.tensor_tensor(sA[:, :, :], bank3(7), swgt[:, :, :], ALU.mult).then_inc(sem("m_A"), 1)
        eng.wait_ge(sem("m_exps"), PT + 1)
        order(eng.tensor_copy(mnew[:, 0, :], mev[r, 3, :]))
        eng.tensor_tensor(sdecb[:, :, :], slast[:, :, 0:1].broadcast_to([NS, B, HM]),
                          mev[r, 3, :].unsqueeze(1).broadcast_to([NS, B, HM]), ALU.mult).then_inc(sem("d_decb"), 1)
        eng.tensor_tensor(sk[:, :, :], sk[:, :, :], wide_of(mev[r, 2, :], DM), ALU.mult).then_inc(sem("m_kw"), 1)
        for h in range(2, HM):
            eng.wait_ge(sem("d_qC_ps"), h - 1)
            eng.tensor_copy(sqp[:, h % 2, :].rearrange("p (b k) -> p b k", k=NS + S)[:, :, 0:S], sqT[:, h, :].rearrange("p (b s) -> p b s", s=S))\
               .then_inc(sem("d_qp"), 1)
        eng.wait_ge(sem("m_kw"), PT + 1)
        eng.wait_ge(sem("d_dec_ps"), 1)
        order(eng.tensor_copy(smn[:, :, :], ps[0:B, 2, 80:80 + 2 * HM].rearrange("p (a h) -> p a h", h=HM)))
        order(eng.tensor_copy(sdec[:, :], ps[:, 2, 96:96 + B * HM]))
        eng.wait_ge(sem("d_n_ps"), 1)
        for h in range(HM):
            ins = eng.scalar_tensor_tensor(out=snn[:, h * DM:(h + 1) * DM], in0=snn[:, h * DM:(h + 1) * DM],
                                           scalar=smn[:, 0, h:h + 1], in1=ps[0:B, 7, h * DM:(h + 1) * DM],
                                           op0=ALU.mult, op1=ALU.add)
        ins.then_inc(sem("d_n"), 1)
        for h in range(HM):
            if h:
                eng.wait_ge(sem("m_update"), PT + h)
            eng.tensor_tensor(skw[:, :, :], sk[:, h, :].unsqueeze(1).broadcast_to([NS, B, DM]),
                              same[:, :, 0:1].broadcast_to([NS, B, DM]), ALU.mult).then_inc(sem("d_kwb"), 1)
            eng.wait_ge(sem("m_update"), PT + h + 1)
            for b in range(B):
                j = b * HM + h
                ins = eng.scalar_tensor_tensor(out=sC[:, j, :], in0=sC[:, j, :], scalar=sdec[:, j:j + 1],
                                               in1=ps[:, 5 + b // 4, (b % 4) * DM:(b % 4 + 1) * DM],
                                               op0=ALU.mult, op1=ALU.add)
            ins.then_inc(sem("d_C"), 1)
        eng.wait_ge(sem("m_num_ps"), PT + 1)
        eng.wait_ge(sem("d_qC_ps"), HM)
        for h in range(0, HM, 2):
            order(eng.tensor_copy(snum[:, h:h + 2, :], ps[r, h // 2, 0:2 * (DM + 1)]
                                  .rearrange("p (h n) -> p h n", n=DM + 1)))
        for h in range(HM):
            order(eng.scalar_tensor_tensor(out=snum[:, h, :], in0=two(3, h, NS), scalar=mev[r, 0, h:h + 1],
                                           in1=snum[:, h, :], op0=ALU.mult, op1=ALU.add))
        order(eng.scalar_tensor_tensor(out=mden[r, :], in0=snum[:, :, DM], scalar=-1.0, in1=snum[:, :, DM],
                                       op0=ALU.mult, op1=ALU.max))
        order(eng.tensor_tensor(mden[r, :], mden[r, :], mev[r, 1, :], ALU.max))
        order(eng.reciprocal(mden[r, :], mden[r, :]))
        for h in range(HM):
            ins = eng.scalar_tensor_tensor(out=sout[:, h, :], in0=snum[:, h, 0:DM], scalar=mden[r, h:h + 1],
                                           in1=tok[r, PT, OM + h * DM:OM + (h + 1) * DM],
                                           op0=ALU.mult, op1=ALU.mult)
        ins.then_inc(sem("m_h"), 1)
        eng.wait_ge(sem("m_high"), PT + 1)
        eng.tensor_tensor(mlT[1][:, :, T:NT], ps[:, 0, 0:HM * NS].rearrange("p (h n) -> p h n", n=NS),
                          mlT[0][:, :, T:NT].bitcast(F32), ALU.subtract).then_inc(sem("m_low"), 1)

    def act_states_out(eng):
        eng.wait_ge(sem("d_C"), HM)
        eng.wait_ge(sem("d_n"), 1)
        eng.dma_start(C_sample.rearrange("b h d e -> d (b h) e"), sC[:, :, :]).then_inc(sem("d_out"), 16)
        eng.dma_start(n_sample.rearrange("b h e -> b (h e)"), snn[:, :]).then_inc(sem("d_out"), 16)
        eng.dma_start(m_sample, smn[:, 1, :]).then_inc(sem("d_out"), 16)


    GROUPS = NPAGE // 4

    def pages(eng, pool, ring, arrived, free, b):
        flat = pool.rearrange("n p h d -> n p (h d)")
        for g in range(GROUPS):
            for j in range(4):
                page = eng.value_load(pt_sb[0:1, bass.ds(b * NPAGE + g * 4 + j, 1)],
                                      min_val=0, max_val=pool.shape[0] - 1)
                slot = (g % 2) * 4 + j
                if j == 0:
                    eng.wait_ge(sem(free), b * GROUPS + g + 1)
                eng.dma_start(ring[:, slot, :], flat[bass.ds(page, 1), :, :].rearrange("a p n -> (a p) n"))\
                   .then_inc(sem(f"{arrived}{g % 2}"), 16)

    def group_in(eng, arrived, b, g):
        eng.wait_ge(sem(f"{arrived}{g % 2}"), b * 128 + 64 * (g // 2) + 64)

    def sp_keys(eng):
        eng.wait_ge(sem("small_in"), 64)
        with eng.Fori(0, B) as b:
            pages(eng, cache_k, kring, "k_in", "k_free", b)

    def pool_values(eng):
        eng.wait_ge(sem("m_C_ps"), 1)
        eng.wait_ge(sem("m_Cout"), 2)
        for half in range(2):
            eng.memset(spow[:, half * (NS // 2):(half + 1) * (NS // 2)], 0.0).then_inc(sem("k_free"), 1)
        pool_states(eng)
        eng.wait_ge(sem("m_low"), PT + 1)
        eng.wait_ge(sem("d_C"), HM)
        eng.wait_ge(sem("d_out"), 48)
        for half in range(2):
            eng.memset(spowT[:, half * (P // 2):(half + 1) * (P // 2)], 0.0).then_inc(sem("v_free"), 1)
        eng.wait_ge(sem("small_in"), 64)
        with eng.Fori(0, B) as b:
            pages(eng, cache_v, vring, "v_in", "v_free", b)

    def pe_decode(eng):
        eng.wait_ge(sem("m_low"), PT + 1)
        eng.wait_ge(sem("d_C"), HM)
        eng.wait_ge(sem("v_free"), 2)
        eng.matmul(ps[:, 6, 0:S], rep8[:, :], own8[:, :], start=True, stop=True).then_inc(sem("p_mask_ps"), 1)
        with eng.Fori(0, B) as b:
            def turn(g):
                group_in(eng, "k_in", b, g)
                for h in range(HP):
                    eng.wait_ge(sem("p_kT_act" if h % 2 == 0 else "p_kT_dve"),
                                b * 8 + max(2 * (g - 1) + h // 2 + 1, 0))
                    for j in range(4):
                        mm = eng.transpose(ps[:, h, j * P:(j + 1) * P],
                                           kring[:, (g % 2) * 4 + j, h * P:(h + 1) * P], ident[:, :])
                    if h < HP - 1:
                        mm.then_inc(sem("p_kT_ps"), 1)
                mm.then_inc(sem("k_free"), 1)

            def score(g):
                eng.wait_ge(sem("p_kT_act"), b * 8 + 2 * g + 2)
                eng.wait_ge(sem("p_kT_dve"), b * 8 + 2 * g + 2)
                if g == 0:
                    eng.wait_ge(sem("p_q"), b * 3 + 3)
                eng.wait_ge(sem("p_S"), b * GROUPS + max(g - 1, 0))
                for h in range(HP):
                    mm = eng.matmul(ps[32 * h:32 * h + 32, 4 + g % 2, :], qb[:, h, :], kT[:, g % 2, h, :],
                                    start=True, stop=True)
                mm.then_inc(sem("p_S_ps"), 1)

            turn(0)
            eng.wait_ge(sem("p_q"), b * 3 + 3)
            eng.wait_ge(sem("p_low"), b * 2)
            eng.wait_ge(sem("p_mask"), 1)
            for h in range(HP):
                mm = eng.matmul(ps[32 * h:32 * h + 32, 6, 0:S], qb[:, h, :], kb[:, h, :],
                                start=True, stop=True)
            mm.then_inc(sem("p_own_ps"), 1)
            for g in range(GROUPS):
                if g + 1 < GROUPS:
                    turn(g + 1)
                score(g)

            def turn_probs(g):
                eng.wait_ge(sem("p_exp"), b * BLOCKS + 2 * g + 2)
                if g == 0:
                    eng.wait_ge(sem("p_S"), b * GROUPS + GROUPS)
                else:
                    eng.wait_ge(sem("p_PT"), b * GROUPS + max(g - 1, 0))
                for j in range(4):
                    c = (4 * g + j) * P
                    if g == 0 and j == 3:
                        eng.wait_ge(sem("p_own"), b + 1)
                    mm = eng.transpose(ps[:, 4 + g % 2, j * P:(j + 1) * P], sS[:, c:c + P], ident[:, :])
                mm.then_inc(sem("p_PT_ps"), 1)

            turn_probs(0)
            eng.transpose(ps[0:NS, 6, P:2 * P], spow[:, :], ident[:, :]).then_inc(sem("p_ownT_ps"), 1)
            for g in range(GROUPS):
                if g + 1 < GROUPS:
                    turn_probs(g + 1)
                group_in(eng, "v_in", b, g)
                eng.wait_ge(sem("p_PT"), b * GROUPS + g + 1)
                for j in range(4):
                    if g == GROUPS - 1 and j == 3:
                        eng.wait_ge(sem("p_ownT"), b + 1)
                    for h in range(HP):
                        mm = eng.matmul(ps[32 * h:32 * h + 32, 7, 0:P], sPT[:, g % 2, j, 32 * h:32 * h + 32],
                                        vring[:, (g % 2) * 4 + j, h * P:(h + 1) * P],
                                        start=(g == 0 and j == 0), stop=False)
                mm.then_inc(sem("v_free"), 1)
            for h in range(HP):
                mm = eng.matmul(ps[32 * h:32 * h + 32, 7, 0:P], spowT[:, 32 * h:32 * h + 32],
                                tok[0:NS, PT, VA + h * P:VA + (h + 1) * P], start=False, stop=True)
            mm.then_inc(sem("p_O_ps"), 1)
            eng.wait_ge(sem("p_O"), b + 1)
            eng.transpose(ps[:, 6, 2 * P:3 * P], sO[:, :], ident[:, :]).then_inc(sem("p_OT_ps"), 1)
        eng.wait_ge(sem("p_low"), 2 * B)

    def act_decode(eng):
        eng.wait_ge(sem("v_free"), 2)
        with eng.Fori(0, B) as b:
            def keys(g):
                for h in (0, 2):
                    eng.wait_ge(sem("p_kT_ps"), b * 12 + 3 * g + h + 1)
                    eng.wait_ge(sem("p_S_ps"), b * GROUPS + max(g - 1, 0))
                    eng.activation(kT[:, g % 2, h, :], ps[:, h, :], ACT.Copy).then_inc(sem("p_kT_act"), 1)

            def scores(g):
                eng.wait_ge(sem("p_S_ps"), b * GROUPS + g + 1)
                if g == 0:
                    eng.wait_ge(sem("p_PT_ps"), b * GROUPS)
                eng.activation(sS[:, g * CH:(g + 1) * CH], ps[:, 4 + g % 2, :], ACT.Copy).then_inc(sem("p_S"), 1)

            for g in range(GROUPS):
                keys(g)
                if g:
                    scores(g - 1)
            scores(GROUPS - 1)
            eng.wait_ge(sem("p_bias"), b + 1)
            for n in range(BLOCKS):
                c = slice(n * 2 * PAGE, (n + 1) * 2 * PAGE)
                eng.activation(sS[:, c], sS[:, c], ACT.Exp, bias=sbias[:, n:n + 1], scale=SC,
                               accum_out=srs[:, n:n + 1]).then_inc(sem("p_exp"), 1)
                if n == 1:
                    eng.activation(spow[:, bass.ds(b * S, S)], sown[:, :], ACT.Exp, bias=snx[:, :], scale=SC,
                                   accum_out=srs[:, BLOCKS:BLOCKS + 1]).then_inc(sem("p_own"), 1)
                if n % 2 == 1 and n > 1:
                    probs(eng, b, n // 2 - 1)
            probs(eng, b, GROUPS - 1)
            eng.wait_ge(sem("p_OT_ps"), b + 1)
            for k in range(2):
                g = slice(k * DH, (k + 1) * DH)
                eng.activation(out_cols(attT[0], b, g), turned_out(k), ACT.Copy).then_inc(sem("p_high"), 1)

    def probs(eng, b, g):
        eng.wait_ge(sem("p_PT_ps"), b * GROUPS + g + 1)
        if g >= 2:
            eng.wait_ge(sem("v_free"), b * GROUPS + g - 1 + 2)
        eng.activation(sPT[:, g % 2, :, :], ps[:, 4 + g % 2, :].rearrange("p (j n) -> p j n", n=P), ACT.Copy)\
           .then_inc(sem("p_PT"), 1)

    def out_cols(dst, b, g):
        return dst[g, :, bass.ds(b * S + T, S)]

    def turned_out(k):
        g = slice(k * DH, (k + 1) * DH)
        return ps[g, 6, 2 * P:3 * P].rearrange("p (h n) -> p h n", n=32)[:, :, k * S:(k + 1) * S]

    def dve_decode(eng):
        order = Order(eng, sem("p_steps"), Count())
        per = order.count.per = 22
        eng.wait_ge(sem("v_free"), 2)
        eng.wait_ge(sem("p_mask_ps"), 1)
        eng.tensor_copy(ownmask[:, :], ps[:, 6, 0:S]).then_inc(sem("p_mask"), 1)
        eng.wait_ge(sem("p_mask"), 1)
        with eng.Fori(0, B) as b:
            order.count.i = b
            eng.wait_ge(sem("p_S_ps"), b * GROUPS)
            eng.wait_ge(sem("p_own_ps"), b)
            for k in range(2):
                g = slice(k * DH, (k + 1) * DH)
                eng.tensor_copy(qb[g, :, k * S:(k + 1) * S], QTs[g, :, bass.ds(b * S, S)]).then_inc(sem("p_q"), 1)
            eng.tensor_copy(kb[:, :, :], KTs[:, :, bass.ds(b * S, S)]).then_inc(sem("p_q"), 1)

            def keys(g):
                for h in (1, 3):
                    if h == 1:
                        eng.wait_ge(sem("p_kT_ps"), b * 12 + 3 * g + 2)
                    else:
                        eng.wait_ge(sem("k_free"), b * GROUPS + g + 1 + 2)
                    eng.wait_ge(sem("p_S_ps"), b * GROUPS + max(g - 1, 0))
                    eng.tensor_copy(kT[:, g % 2, h, :], ps[:, h, :]).then_inc(sem("p_kT_dve"), 1)

            def reduce(g):
                s = sS[:, g * CH:(g + 1) * CH].rearrange("p (n k) -> p n k", k=2 * PAGE)
                eng.wait_ge(sem("p_S"), b * GROUPS + g + 1)
                order(eng.tensor_reduce(ssum[:, 2 * g:2 * g + 2], s, X, ALU.add))
                order(eng.tensor_reduce(smax[:, 2 * g:2 * g + 2], s, X, ALU.max))

            for g in range(GROUPS):
                keys(g)
                if g == 1:
                    eng.wait_ge(sem("p_own_ps"), b + 1)
                    order(eng.tensor_tensor(sown[:, :], ps[:, 6, 0:S], ownmask[:, :], ALU.add))
                    order(eng.tensor_reduce(smax[:, BLOCKS:BLOCKS + 1], sown[:, :], X, ALU.max))
                if g:
                    reduce(g - 1)
            reduce(GROUPS - 1)
            full = [P, BLOCKS, BLOCKS]
            of_n = ssum[:, :].unsqueeze(2).broadcast_to(full)
            of_m = ssum[:, :].unsqueeze(1).broadcast_to(full)
            order(eng.tensor_tensor(seq[:, :, :], of_m, of_n, ALU.is_equal))
            order(eng.tensor_tensor(seq[:, :, :], seq[:, :, :], earlier[:, :, :], ALU.mult))
            order(eng.tensor_tensor(scmp[:, :, :], of_m, of_n, ALU.is_gt))
            order(eng.tensor_tensor(scmp[:, :, :], scmp[:, :, :], seq[:, :, :], ALU.add))
            order(eng.tensor_reduce(srank[:, :], scmp[:, :, :], X, ALU.add))
            order(eng.tensor_scalar(sneg[:, :], srank[:, :], TOPK - 0.5, NEG, ALU.is_gt, ALU.mult))
            order(eng.tensor_tensor(smax[:, 0:BLOCKS], smax[:, 0:BLOCKS], sneg[:, :], ALU.add))
            order(eng.tensor_reduce(smx[:, :], smax[:, :], X, ALU.max))
            order(eng.tensor_scalar(snx[:, :], smx[:, :], -SC, None, ALU.mult))
            order(eng.memset(spow[:, :], 0.0))
            eng.tensor_scalar(sbias[:, :], sneg[:, :], snx[:, :], None, ALU.add).then_inc(sem("p_bias"), 1)
            eng.wait_ge(sem("p_ownT_ps"), b + 1)
            eng.tensor_copy(spowT[:, :], ps[0:NS, 6, P:2 * P]).then_inc(sem("p_ownT"), 1)
            eng.wait_ge(sem("p_exp"), b * BLOCKS + BLOCKS)
            eng.wait_ge(sem("p_own"), b + 1)
            order(eng.tensor_reduce(srt[:, :], srs[:, :], X, ALU.add))
            order(eng.reciprocal(sri[:, :], srt[:, :]))
            eng.wait_ge(sem("p_O_ps"), b + 1)
            eng.tensor_scalar(sO[:, :], ps[:, 7, 0:P], sri[:, :], None, ALU.mult).then_inc(sem("p_O"), 1)
            eng.wait_ge(sem("p_high"), b * 2 + 2)
            for k in range(2):
                g = slice(k * DH, (k + 1) * DH)
                eng.tensor_tensor(out_cols(attT[1], b, g), turned_out(k), out_cols(attT[0], b, g).bitcast(F32),
                                  ALU.subtract).then_inc(sem("p_low"), 1)
            assert order.count.n == per, order.count.n


    MERGE = steps(8) | banks(8, 8)

    def merge_rows(k, c):
        w = w_attn_br if k < 4 else w_mlstm_br
        return w[(k % 4) * P:(k % 4 + 1) * P, c * CH:(c + 1) * CH]

    def sp_merge_first(eng, n):
        for k in range(AHEAD):
            w_load(eng, n, merge_rows(k, 0))

    def sp_merge_rest(eng, n):
        for c in range(2):
            for k in range(AHEAD if c == 0 else 0, 8):
                w_load(eng, n, merge_rows(k, c))
        with n.loop(2, ALL8) as c:
            for k in range(KT):
                w_load(eng, n, w_out[k * P:(k + 1) * P, bass.ds(c * CH, CH)])

    def pe_merge(eng, n):
        with n.loop(2, MERGE):
            features_chunk(eng, n, attT, HP)
            features_chunk(eng, n, mlT, HM)
        eng.wait_ge(sem("u_low"), 16)
        with n.loop(2, ALL8 | banks(TILES)):
            tokens_chunk(eng, n, uT, KT)

    def u_at(dst, c, b):
        return dst[:, bass.ds(c * (4 * NT) + (b // 2) * NT + (b % 2) * HALFT, HALFT)]

    uT_flat = [a[:, :, :].rearrange("p k n -> p (k n)") for a in uT]
    u32_flat = u32[:, :, :].rearrange("p k n -> p (k n)")
    sgm = sg[:, KT * NT:2 * KT * NT]

    def act_merge(eng, n):
        with n.loop(2, MERGE) as c:
            for _ in range(4):
                w_high(eng, n)
            for b in range(8):
                skip(n, b, b == 7)
            for _ in range(4):
                w_high(eng, n)
            for b in range(8):
                skip(n, b, b == 7)
                eng.wait_ge(sem("u_sum"), c * 8 + b + 1)
                eng.activation(u_at(uT_flat[0], c, b), u_at(u32_flat, c, b), ACT.Copy).then_inc(sem("u_high"), 1)
        with n.loop(2, ALL8 | banks(TILES)) as c:
            for _ in range(KT):
                w_high(eng, n)
            copy_tokens(eng, n, lambda t: wide[0:rows(t), t, bass.ds(c * CH, CH)], 0)
        merged_norm_act(eng, n)

    def dve_merge(eng, n):
        with n.loop(2, MERGE) as c:
            for _ in range(4):
                w_low(eng, n)
            for b in range(8):
                drain(eng, n, b, b == 7)
                drained(eng.tensor_tensor(u_at(u32_flat, c, b), ps[:, b, 0:HALFT], u_at(sg, c, b), ALU.mult), n, b)
            for _ in range(4):
                w_low(eng, n)
            for b in range(8):
                drain(eng, n, b, b == 7)
                drained(eng.tensor_tensor(u_at(sgm, c, b), ps[:, b, 0:HALFT], u_at(sgm, c, b), ALU.mult), n, b)
                eng.wait_ge(sem(f"free{b}"), n[f"free{b}"].value())
                eng.tensor_tensor(u_at(u32_flat, c, b), u_at(u32_flat, c, b), u_at(sgm, c, b), ALU.add)\
                   .then_inc(sem("u_sum"), 1)
            for b in range(8):
                eng.wait_ge(sem("u_high"), c * 8 + b + 1)
                eng.tensor_tensor(u_at(uT_flat[1], c, b), u_at(u32_flat, c, b),
                                  u_at(uT_flat[0], c, b).bitcast(F32), ALU.subtract).then_inc(sem("u_low"), 1)
        with n.loop(2, ALL8 | banks(TILES)) as c:
            for _ in range(KT):
                w_low(eng, n)
            copy_tokens(eng, n, lambda t: wide[0:rows(t), t, bass.ds(c * CH, CH)], 1)
        merged_norm_dve(eng, n)

    def wide_whole(eng, n):
        for t in range(TILES):
            eng.wait_ge(sem(f"free{t}"), n[f"free{t}"].value())

    def merged_norm_act(eng, n):
        wide_whole(eng, n)
        norm_stats(eng, 1, wide, lambda e, t: None)
        norm_stats(eng, 2, x, lambda e, t: e.wait_ge(sem("x_sum"), t + 1))
        turn_act(eng, n, 2, h2T)

    def merged_norm_dve(eng, n):
        wide_whole(eng, n)
        norm_inverse(eng, 1)
        eng.wait_ge(sem("g_in"), 16)
        norm_apply(eng, 1, wide, wide)
        for t in range(TILES):
            eng.wait_ge(sem("normed"), 1 * TILES + t + 1)
            eng.wait_ge(sem(f"x_in{t}"), 32)
            r = rows(t)
            eng.tensor_tensor(x[0:r, t, :], x[0:r, t, :], wide[0:r, t, :], ALU.add).then_inc(sem("x_sum"), 1)
        norm_inverse(eng, 2)
        eng.wait_ge(sem("g_in"), 32)
        norm_apply(eng, 2, x, xn)
        turn_dve(eng, n, 2, h2T)
        eng.memset(wide[:, :, :], 0.0).then_inc(sem("y_zero"), 1)


    FB = FF // D
    MLP = steps(32) | banks(8, 8, TILES, TILES)
    rl = sb("rl", [P, 8, HALFT], F32, offset=R2)

    def mlp_passes(eng, n, counts, body):
        with n.loop(FB - 1, counts) as i:
            body(i, False)
        body(FB - 1, True)

    def sp_mlp(eng, n):
        def body(i, last):
            for c in range(2):
                for k in range(KT):
                    w_load(eng, n, w_up[k * P:(k + 1) * P, bass.ds(i * D + c * CH, CH)])
            for c in range(2):
                for k in range(KT):
                    w_load(eng, n, w_down[bass.ds(i * D + k * P, P), c * CH:(c + 1) * CH])
        mlp_passes(eng, n, steps(32), body)

    def pe_mlp(eng, n):
        def body(i, last):
            for c in range(2):
                features_chunk(eng, n, h2T, KT)
            tokens_chunk(eng, n, hid, KT, lambda k: eng.wait_ge(sem("hid_low"), i * 16 + 2 * k + 2))
            tokens_chunk(eng, n, hid, KT)
        all_out(eng, n)
        mlp_passes(eng, n, MLP, body)

    def act_mlp(eng, n):
        def body(i, last):
            for c in range(2):
                for _ in range(KT):
                    w_high(eng, n)
                for b in range(9):
                    if b < 8:
                        drain(eng, n, b, b == 7)
                        eng.wait_ge(sem("hid_low"), i * 16 + 8 * c)
                        drained(eng.activation(rl[:, b, :], ps[:, b, 0:HALFT], ACT.Relu), n, b)
                    if b >= 1:
                        u = b - 1
                        eng.wait_ge(sem("hid_sq"), i * 16 + 8 * c + u + 1)
                        k = 4 * c + u // 2
                        eng.activation(hid[0][:, k, (u % 2) * HALFT:(u % 2 + 1) * HALFT], rl[:, u, :], ACT.Copy)\
                           .then_inc(sem("hid_high"), 1)
            for c in range(2):
                for _ in range(KT - (AHEAD if last and c == 1 else 0)):
                    w_high(eng, n)
                for t in range(TILES):
                    skip(n, t, t == TILES - 1)
        mlp_passes(eng, n, MLP, body)

    def dve_mlp(eng, n):
        def body(i, last):
            for c in range(2):
                for _ in range(KT):
                    w_low(eng, n)
                for b in range(9):
                    if b < 8:
                        eng.wait_ge(sem(f"free{b}"), n[f"free{b}"].value(1, 1))
                        skip(n, b, b == 7)
                        eng.tensor_tensor(rl[:, b, :], rl[:, b, :], rl[:, b, :], ALU.mult).then_inc(sem("hid_sq"), 1)
                    if b >= 1:
                        u = b - 1
                        eng.wait_ge(sem("hid_high"), i * 16 + 8 * c + u + 1)
                        k = 4 * c + u // 2
                        half = slice((u % 2) * HALFT, (u % 2 + 1) * HALFT)
                        eng.tensor_tensor(hid[1][:, k, half], rl[:, u, :], hid[0][:, k, half].bitcast(F32),
                                          ALU.subtract).then_inc(sem("hid_low"), 1)
            for c in range(2):
                for _ in range(KT - (AHEAD if last and c == 1 else 0)):
                    w_low(eng, n)
                for t in range(TILES):
                    drain(eng, n, t, t == TILES - 1)
                    y = wide[0:rows(t), t, c * CH:(c + 1) * CH]
                    drained(eng.tensor_tensor(y, ps[bank_rows(t), t, :], y, ALU.add), n, t)
        eng.wait_ge(sem("y_zero"), 1)
        mlp_passes(eng, n, MLP, body)


    def act_out(eng, n):
        wide_whole(eng, n)
        norm_stats(eng, 3, wide, lambda e, t: None)

    def dve_out(eng, n):
        wide_whole(eng, n)
        norm_inverse(eng, 3)
        eng.wait_ge(sem("g_in"), 48)
        norm_apply(eng, 3, wide, wide)
        for t in range(TILES):
            eng.wait_ge(sem("normed"), 3 * TILES + t + 1)
            r = rows(t)
            eng.tensor_tensor(x[0:r, t, :], x[0:r, t, :], wide[0:r, t, :], ALU.add).then_inc(sem("x_sum"), 1)

    def sp_out(eng):
        for t in range(PT):
            eng.wait_ge(sem("x_sum"), TILES + t + 1)
            eng.dma_start(y_prompt[0, t * P:(t + 1) * P, :], x[:, t, :]).then_inc(sem("y_out"), 16)
        eng.wait_ge(sem("x_sum"), 2 * TILES)
        eng.dma_start(y_sample.rearrange("b s d -> (b s) d"), x[0:NS, PT, :]).then_inc(sem("y_out"), 16)
        eng.wait_ge(sem("y_out"), 16 * TILES)
        eng.wait_ge(sem("kv_out"), 64)
        eng.wait_ge(sem("m_out"), 48)
        eng.wait_ge(sem("d_out"), 48)


    with stack:
        block = stack.enter_context(nc.Block())

        @block.sync
        def _(eng):
            n = Counts(eng)
            load_x(eng, "x_in")
            sp_project(eng, n)
            sp_merge_first(eng, n)
            sp_states(eng)
            sp_keys(eng)
            eng.wait_ge(sem("k_free"), 2 + B * GROUPS)
            load_x(eng, "x_in")
            sp_merge_rest(eng, n)
            sp_mlp(eng, n)
            sp_out(eng)

        @block.gpsimd
        def _(eng):
            constants(eng)
            eng.wait_ge(sem("normed"), TILES)
            load_g(eng, g_post_mix)
            pool_rotary(eng)
            pool_heads(eng)
            pool_mlstm(eng)
            pool_mlstm_out(eng)
            pool_values(eng)
            eng.wait_ge(sem("normed"), 2 * TILES)
            load_g(eng, g_pre_mlp)
            eng.wait_ge(sem("normed"), 3 * TILES)
            load_g(eng, g_post_mlp)

        @block.scalar
        def _(eng):
            n = Counts(eng)
            load_g(eng, g_pre_mix, "g_first")
            eng.dma_start(bif[:, :], b_if.rearrange("(p a) -> p a", a=1)).then_inc(sem("small_in"), 16)
            eng.dma_start(rot[:, :, :], rotary.rearrange("(t p) n -> p t n", p=P)).then_inc(sem("small_in"), 16)
            eng.dma_start(pt_sb[:, :], page_table.rearrange("(a b) n -> a (b n)", a=1)).then_inc(sem("small_in"), 16)
            eng.dma_start(smb[:, :], state_m).then_inc(sem("small_in"), 16)
            constants_ready(eng)
            norm_stats(eng, 0, x, lambda e, t: e.wait_ge(sem(f"x_in{t}"), 16))
            for _ in range(AHEAD):
                w_high(eng, n)
            turn_act(eng, n, 0, hT)
            act_project(eng, n)
            act_gates(eng)
            act_prompt(eng)
            act_mlstm(eng)
            act_sample(eng)
            act_states_out(eng)
            act_decode(eng)
            act_merge(eng, n)
            act_mlp(eng, n)
            act_out(eng, n)

        @block.vector
        def _(eng):
            n = Counts(eng)
            constants_ready(eng)
            norm_inverse(eng, 0)
            eng.wait_ge(sem("g_first"), 16)
            norm_apply(eng, 0, x, xn)
            for _ in range(AHEAD):
                w_low(eng, n)
            turn_dve(eng, n, 0, hT)
            dve_project(eng, n)
            dve_gates(eng)
            dve_prompt(eng)
            dve_mlstm(eng)
            dve_sample(eng)
            dve_decode(eng)
            dve_merge(eng, n)
            dve_mlp(eng, n)
            dve_out(eng, n)

        @block.tensor
        def _(eng):
            n = Counts(eng)
            constants_ready(eng)
            turn_pe(eng, n, 0)
            all_out(eng, n)
            pe_project(eng, n)
            all_out(eng, n)
            pe_gates(eng)
            pe_prompt(eng)
            pe_mlstm(eng)
            pe_sample(eng)
            pe_decode(eng)
            pe_merge(eng, n)
            turn_pe(eng, n, 2)
            pe_mlp(eng, n)



def rotary_table():
    import numpy as np
    half = HALF
    inv = (np.float32(500000.0) ** (-np.arange(half, dtype=np.float32) * np.float32(2.0) / np.float32(2 * half)))
    pos = np.zeros(TILES * P, np.float32)
    pos[:T] = np.arange(T)
    pos[T:NT] = PAST + np.arange(NS) % S
    ang = (pos[:, None] * inv[None, :].astype(np.float32)).astype(np.float32).astype(np.float64)
    return np.concatenate([np.cos(ang), np.sin(ang)], axis=1).astype(np.float32)


_INS = ["x_prompt", "x_sample", "cache_k", "cache_v", "state_C", "state_n", "state_m", "page_table",
        "g_pre_mix", "w_in", "b_if", "w_attn_br", "w_mlstm_br", "w_out", "g_post_mix", "g_pre_mlp",
        "w_up", "w_down", "g_post_mlp"]
_OUTS = [(1, T, D), (B, S, D), (1, T, HA, DH), (1, T, HA, DH), (1, HM, DM, DM), (1, HM, DM), (1, HM),
         (B, S, HA, DH), (B, S, HA, DH), (B, HM, DM, DM), (B, HM, DM), (B, HM)]


def kernel(**inputs):
    import numpy as _np
    import concourse.bacc as _bacc
    from concourse.bass_utils import run_bass_kernel_spmd as _run

    nc = _bacc.Bacc("TRN2", target_bir_lowering=False, num_devices=1)
    arrays, args = {}, []
    for name, a in [(k, _np.ascontiguousarray(inputs[k])) for k in _INS] + [("rotary", rotary_table())]:
        arrays[f"in_{name}_dram"] = a
        args.append(nc.dram_tensor(f"in_{name}_dram", a.shape, mybir.dt.from_np(a.dtype), kind="ExternalInput").ap())
    for i, shape in enumerate(_OUTS):
        args.append(nc.dram_tensor(f"out_{i}_dram", shape, F32, kind="ExternalOutput").ap())
    moba_mlstm_step(nc, *args)
    r = _run(nc, [arrays], core_ids=[0])
    return tuple(r.results[0][f"out_{i}_dram"] for i in range(len(_OUTS)))
```

```python
from contextlib import ExitStack, contextmanager

import concourse.bass as bass
from concourse import mybir

ALU = mybir.AluOpType
ACT = mybir.ActivationFunctionType
F32 = mybir.dt.float32
F32R = mybir.dt.float32r
I32 = mybir.dt.int32
X = mybir.AxisListType.X
NEG = -1.0e30

P = 128
D = 1024
KT = D // P
T = 512
PT = T // P
B, S = 8, 8
NS = B * S
NT = T + NS
HALFT = NT // 2
TILES = PT + 1
HA, DH = 8, 64
HP = HA // 2
HM, DM = 4, 128
PAGE, NPAGE = 128, 16
BLOCKS, TOPK = 8, 3
PAST = NPAGE * PAGE
HALF = DH // 8
FF = 4096
EPS = 1e-6
CH = 512
QA, KA, VA, QM, KM, VM, OM = (CH * j for j in range(7))
IF0 = 7 * CH
GA0 = IF0 + 2 * HM
NSLOT = 4
AHEAD = 3
SC = DH ** -0.5
RING = 8


class Count:

    def __init__(self):
        self.base = self.n = self.per = 0
        self.i = None

    def value(self, scale=1, plus=0):
        v = (self.base + self.n) * scale + plus
        return v if self.i is None or not self.per else self.i * (self.per * scale) + v

    def add(self, k=1):
        self.n += k
        return self.value()


class Counts:

    def __init__(self, eng):
        self.eng, self.of = eng, {}

    def __getitem__(self, name):
        return self.of.setdefault(name, Count())

    @contextmanager
    def loop(self, times, per):
        with self.eng.Fori(0, times) as i:
            for name, k in per.items():
                c = self[name]
                c.base, c.n, c.per, c.i = c.base + c.n, 0, k, i
            yield i
            for name, k in per.items():
                c = self[name]
                assert c.n == k, (name, c.n, k)
                c.base, c.n, c.per, c.i = c.base + k * times, 0, 0, None


class Order:

    def __init__(self, eng, sem, count):
        self.eng, self.sem, self.count = eng, sem, count

    def __call__(self, ins):
        ins.then_inc(self.sem, 1)
        self.eng.wait_ge(self.sem, self.count.add())


def moba_mlstm_step(
    nc: bass.Bass, x_prompt, x_sample, cache_k, cache_v, state_C, state_n, state_m, page_table,
    g_pre_mix, w_in, b_if, w_attn_br, w_mlstm_br, w_out, g_post_mix, g_pre_mlp, w_up, w_down, g_post_mlp,
    rotary,
    y_prompt, y_sample, k_prompt, v_prompt, C_prompt, n_prompt, m_prompt,
    k_sample, v_sample, C_sample, n_sample, m_sample,
):
    start = 16512
    R1 = start
    R2 = R1 + 2 * KT * NT * 4
    R3 = R2 + TILES * 7 * CH * 4
    R4 = R3 + 2 * KT * NT * 4
    RW = R4 + TILES * D * 4
    RC = RW + 3 * NSLOT * CH * 4
    at = {"R1": R1, "R2": R2, "R3": R3, "R4": R4, "RW": RW, "RC": RC}
    tops = {"R1": R2, "R2": R3, "R3": R4, "R4": RW, "RW": RC, "RC": nc.sbuf_top}

    def sb(name, shape, dt=F32, region=None, offset=None):
        size = 4
        for s in shape[1:]:
            size *= s
        where = at[region] if offset is None else offset
        if offset is None:
            at[region] = (where + size + 31) // 32 * 32
            assert at[region] <= tops[region], (name, at[region], tops[region])
        return nc.alloc_sbuf_tensor_at(name, shape, dt, offset=where)

    def pair(name, shape, region):
        return sb(name + "_hi", shape, F32R, region), sb(name + "_lo", shape, F32R, region)

    hT = pair("hT", [P, KT, NT], "R1")
    at["R1"] = R1
    attT = pair("attT", [P, HP, NT], "R1")
    mlT = pair("mlT", [P, HM, NT], "R1")
    at["R1"] = R1
    h2T = pair("h2T", [P, KT, NT], "R1")

    tok = sb("tok", [P, TILES, 7 * CH], F32, "R2")
    at["R2"] = R2
    uT = pair("uT", [P, KT, NT], "R2")
    u32 = sb("u32", [P, KT, NT], F32, offset=at["R2"])
    wide = sb("wide", [P, TILES, D], F32, "R2")
    xn = sb("xn", [P, TILES, D], F32, offset=R2 + 2 * KT * NT * 4)
    hole = [R2 + t * 7 * CH * 4 for t in range(PT)]

    sg = sb("sg", [P, 2 * KT * NT], F32, "R3")
    at["R3"] = R3
    hid = pair("hid", [P, KT, NT], "R3")

    x = sb("x", [P, TILES, D], F32, "R4")
    at["R4"] = R4
    qc = sb("qc", [P, PT, P], F32, "R4")
    kc = sb("kc", [P, PT, P], F32, "R4")
    vc = sb("vc", [P, PT, P], F32, "R4")
    QTp = sb("QTp", [P, T], F32, "R4")
    KTp = sb("KTp", [P, T], F32, "R4")
    pr = sb("pr", [P, 3, T], F32, "R4")
    prT = sb("prT", [P, 2, PT * P], F32, "R4")
    at["R4"] = R4
    mq = sb("mq", [P, HM, P], F32, "R4")
    mk = sb("mk", [P, HM, P], F32, "R4")
    mv = sb("mv", [P, HM, DM + 1], F32, "R4")
    mqT = sb("mqT", [P, HM, P], F32, "R4")
    mkT = sb("mkT", [P, HM, P], F32, "R4")
    CTn = sb("CTn", [P, HM, DM + 1], F32, "R4")
    gap = sb("gap", [P, HM, P], F32, "R4")
    wgt = sb("wgt", [P, HM, P], F32, "R4")
    mkw = sb("mkw", [P, HM, P], F32, "R4")
    mA = sb("mA", [P, HM, P], F32, offset=hole[0])
    mnum = sb("mnum", [P, HM, DM + 1], F32, offset=hole[0] + 2048)
    mout = sb("mout", [P, HM, DM], F32, offset=hole[1])
    mdg = sb("mdg", [P, HM, P], F32, offset=hole[1] + 2048)
    Cst = sb("Cst", [P, HM, DM], F32, offset=hole[1] + 4096)
    nst = sb("nst", [HM, DM], F32, offset=hole[2])
    at["R4"] = R4
    kring = sb("kring", [P, RING, CH], F32, "R4")

    base = R2
    sC = sb("sC", [P, B * HM, DM], F32, offset=base)
    sCT = sb("sCT", [P, B * HM, DM + 1], F32, offset=base + 16384)
    skw = [sb("skw0", [NS, B, DM], F32, offset=base + 32896 + 32),
           sb("skw1", [NS, B, DM], F32, offset=R4 + RING * CH * 4)]
    sqp = sb("sqp", [P, 2, B * (NS + S)], F32, offset=base + 37120)
    sgap = sb("sgap", [NS, HM, NS], F32, offset=base + 41728)
    swgt = sb("swgt", [NS, HM, NS], F32, offset=base + 42752)
    sA = sb("sA", [NS, HM, NS], F32, offset=base + 43776)
    sdg = sb("sdg", [NS, HM, NS], F32, offset=base + 44800)
    snum = sb("snum", [NS, HM, DM + 1], F32, offset=base + 45824)
    sout = sb("sout", [NS, HM, DM], F32, offset=base + 47904)
    sv = sb("sv", [NS, HM, DM + 1], F32, offset=base + 49952)
    sk = sb("sk", [NS, HM, DM], F32, offset=base + 52032)
    sqT = sb("sqT", [P, HM, NS], F32, offset=base + 54080)
    skT = sb("skT", [P, HM, NS], F32, offset=base + 55104)
    vrings = (sb("vring0", [P, RING, CH], F32, offset=RW + NSLOT * CH * 4),
              sb("vring1", [P, RING, CH], F32, offset=base))
    kT = sb("kT", [P, 2, HP, CH], F32, offset=base + 16384)
    sS = sb("sS", [P, PAST], F32, offset=base + 32768)
    sPT = sb("sPT", [P, 2, 4, P], F32, offset=base + 40960)
    sO = sb("sO", [P, P], F32, offset=base + 45056)
    kb = sb("kb", [P, HP, S], F32, offset=base + 45568)
    assert 56128 <= PT * 7 * CH * 4

    w32 = sb("w32", [P, NSLOT, CH], F32, "RW")
    w_hi, w_lo = pair("w", [P, NSLOT, CH], "RW")

    gB = sb("gB", [P, D], F32, "RC")
    junk = sb("junk", [P, D], F32, "RC")
    snn = sb("snn", [B, HM * DM], F32, offset=at["RC"] - 4 * D)
    ident = sb("ident", [P, P], F32, "RC")
    ones = sb("ones", [P, P], F32, "RC")
    upper = sb("upper", [P, P], F32, "RC")
    causal = sb("causal", [P, P], F32, "RC")
    causalT = sb("causalT", [P, P], F32, "RC")
    lastrow = sb("lastrow", [P, P], F32, "RC")
    same = sb("same", [NS, B, S], F32, "RC")
    supper = sb("supper", [NS, B, S], F32, "RC")
    scausal = sb("scausal", [NS, B, S], F32, "RC")
    scausalT = sb("scausalT", [NS, B, S], F32, "RC")
    slast = sb("slast", [NS, B, S], F32, "RC")
    sameT = sb("sameT", [B, NS], F32, "RC")
    rep8 = sb("rep8", [S, P], F32, "RC")
    own8 = sb("own8", [S, S], F32, "RC")
    earlier = sb("earlier", [P, BLOCKS, BLOCKS], F32, "RC")
    ownmask = sb("ownmask", [P, S], F32, "RC")
    eps = sb("eps", [P, 1], F32, "RC")
    ssq = sb("ssq", [P, TILES], F32, "RC")
    rms = sb("rms", [P, TILES], F32, "RC")
    rinv = sb("rinv", [P, TILES], F32, "RC")
    bif = sb("bif", [2 * HM, 1], F32, "RC")
    gates = sb("gates", [2 * HM, NT], F32, "RC")
    gtok = sb("gtok", [P, TILES, 2 * HM], F32, "RC")
    lf = sb("lf", [P, TILES, HM], F32, "RC")
    lt = sb("lt", [P, TILES, HM], F32, "RC")
    amx = sb("amx", [P, HA], F32, "RC")
    anx = sb("anx", [P, HA], F32, "RC")
    asum = sb("asum", [P, HA], F32, "RC")
    arec = sb("arec", [P, HA], F32, "RC")
    ma = sb("ma", [P, HM], F32, "RC")
    mM = sb("mM", [P, 2, HM], F32, "RC")
    mnM = sb("mnM", [P, HM], F32, "RC")
    mprev = sb("mprev", [P, HM], F32, "RC")
    mex = sb("mex", [P, 4, HM], F32, "RC")
    mev = sb("mev", [P, 4, HM], F32, "RC")
    mlast = sb("mlast", [P, 2, HM], F32, "RC")
    mden = sb("mden", [P, HM], F32, "RC")
    smb = sb("smb", [B, HM], F32, "RC")
    sdecb = sb("sdecb", [NS, B, HM], F32, "RC")
    sdec = sb("sdec", [P, B * HM], F32, "RC")
    smn = sb("smn", [B, 2, HM], F32, "RC")
    mnew = sb("mnew", [NS, 2, HM], F32, "RC")
    pt_sb = sb("pt_sb", [1, B * NPAGE], I32, "RC")
    QTs = sb("QTs", [P, HP, NS], F32, "RC")
    KTs = sb("KTs", [P, HP, NS], F32, "RC")
    qb = sb("qb", [P, HP, 32], F32, "RC")
    ssum = sb("ssum", [P, BLOCKS], F32, "RC")
    smax = sb("smax", [P, BLOCKS + 1], F32, "RC")
    scmp = sb("scmp", [P, BLOCKS, BLOCKS], F32, "RC")
    seq = sb("seq", [P, BLOCKS, BLOCKS], F32, "RC")
    srank = sb("srank", [P, BLOCKS], F32, "RC")
    sneg = sb("sneg", [P, BLOCKS], F32, "RC")
    smx = sb("smx", [P, 1], F32, "RC")
    snx = sb("snx", [P, 1], F32, "RC")
    sbias = sb("sbias", [P, BLOCKS], F32, "RC")
    sown = sb("sown", [P, S], F32, "RC")
    snext = sb("snext", [P, S], F32, "RC")
    spow = sb("spow", [P, NS], F32, "RC")
    spowT = sb("spowT", [NS, P], F32, "RC")
    srs = sb("srs", [P, BLOCKS + 1], F32, "RC")
    srt = sb("srt", [P, 1], F32, "RC")
    sri = sb("sri", [P, 1], F32, "RC")
    rot = sb("rot", [P, TILES, 2 * HALF], F32, "RC")
    rt = [sb(f"rt{j}", [P, PT, 2 * HA, HALF], F32, offset=R4 + j * 2048) for j in range(4)]

    ps = nc.alloc_psum_tensor("ps", [P, 8, CH], F32)

    def sem(name):
        if name not in names:
            names[name] = stack.enter_context(nc.semaphore(name))
        return names[name]

    names = {}
    stack = ExitStack()

    def rows(t):
        return P if t < PT else NS

    def bank_rows(t):
        return slice(0, P) if t < PT else slice(P - NS, P)

    def tok_cols(t):
        return slice(t * P, (t + 1) * P) if t < PT else slice(NT - P, NT)

    def cols(t):
        return slice(t * P, t * P + rows(t))

    def wide_of(ap, n):
        return ap.unsqueeze(2).broadcast_to([ap.shape[0], ap.shape[1], n])


    def w_load(eng, n, src):
        c = n["w_step"]
        j = (c.base + c.n) % NSLOT
        u = n[f"slot{j}"]
        eng.wait_ge(sem(f"w_split{j}"), u.value())
        eng.dma_start(w32[:, j, 0:src.shape[1]], src).then_inc(sem(f"w_in{j}"), 16)
        u.add()
        c.n += 1

    def w_high(eng, n, width=CH):
        c = n["w_step"]
        j = (c.base + c.n) % NSLOT
        u = n[f"slot{j}"]
        eng.wait_ge(sem(f"w_in{j}"), u.value(16, 16))
        eng.wait_ge(sem(f"w_used{j}"), u.value())
        eng.activation(w_hi[:, j, 0:width], w32[:, j, 0:width], ACT.Copy).then_inc(sem(f"w_high{j}"), 1)
        u.add()
        c.n += 1

    def w_low(eng, n, width=CH):
        c = n["w_step"]
        j = (c.base + c.n) % NSLOT
        u = n[f"slot{j}"]
        eng.wait_ge(sem(f"w_high{j}"), u.value(1, 1))
        eng.tensor_tensor(w_lo[:, j, 0:width], w32[:, j, 0:width], w_hi[:, j, 0:width].bitcast(F32),
                          ALU.subtract).then_inc(sem(f"w_split{j}"), 1)
        u.add()
        c.n += 1

    def take_step(eng, n):
        c = n["w_step"]
        j = (c.base + c.n) % NSLOT
        u = n[f"slot{j}"]
        eng.wait_ge(sem(f"w_split{j}"), u.value(1, 1))
        u.add()
        c.n += 1
        return j

    def steps(k):
        return {"w_step": k} | {f"slot{j}": k // NSLOT for j in range(NSLOT)}

    def banks(*turns):
        free = {f"free{b}": sum(b < t for t in turns) for b in range(max(turns))}
        return free | {f"full{b}": sum(b < t - 1 for t in turns) for b in range(max(turns) - 1)}

    def fill(eng, n, b):
        eng.wait_ge(sem(f"free{b}"), n[f"free{b}"].value())
        n[f"free{b}"].add()

    def filled(ins, n, b):
        ins.then_inc(sem(f"full{b}"), 1)
        n[f"full{b}"].add()

    def drain(eng, n, b, last=False):
        if last:
            eng.wait_ge(sem(f"w_used{NSLOT - 1}"), n[f"slot{NSLOT - 1}"].value())
        else:
            eng.wait_ge(sem(f"full{b}"), n[f"full{b}"].value(1, 1))
            n[f"full{b}"].add()

    def drained(ins, n, b):
        ins.then_inc(sem(f"free{b}"), 1)
        n[f"free{b}"].add()

    def skip(n, b, last=False):
        n[f"free{b}"].add()
        if not last:
            n[f"full{b}"].add()

    THREE = ((0, 0), (0, 1), (1, 0))

    def tokens_chunk(eng, n, left, kt, ready=None):
        w = (w_hi, w_lo)
        for k in range(kt):
            j = take_step(eng, n)
            if ready:
                ready(k)
            for t in range(TILES):
                if k == 0:
                    fill(eng, n, t)
                for a, b in THREE:
                    mm = eng.matmul(ps[:, t, :], left[a][:, k, tok_cols(t)], w[b][:, j, :],
                                    start=(k == 0 and (a, b) == THREE[0]),
                                    stop=(k == kt - 1 and (a, b) == THREE[-1]))
                if k == kt - 1 and t < TILES - 1:
                    filled(mm, n, t)
            mm.then_inc(sem(f"w_used{j}"), 1)

    def features_chunk(eng, n, right, kt, nts=4):
        w = (w_hi, w_lo)
        for k in range(kt):
            j = take_step(eng, n)
            for b in range(2 * nts):
                i, h = b // 2, b % 2
                if k == 0:
                    fill(eng, n, b)
                for c, a in THREE:
                    mm = eng.matmul(ps[:, b, 0:HALFT], w[a][:, j, i * P:(i + 1) * P],
                                    right[c][:, k, h * HALFT:(h + 1) * HALFT],
                                    start=(k == 0 and (c, a) == THREE[0]),
                                    stop=(k == kt - 1 and (c, a) == THREE[-1]))
                if k == kt - 1 and b < 2 * nts - 1:
                    filled(mm, n, b)
            mm.then_inc(sem(f"w_used{j}"), 1)


    def norm_stats(eng, tag, src, ready):
        for t in range(TILES + 1):
            if t:
                r = rows(t - 1)
                eng.wait_ge(sem("squares"), tag * TILES + t)
                eng.activation(rms[0:r, t - 1:t], ssq[0:r, t - 1:t], ACT.Sqrt, bias=eps[0:r, :],
                               scale=1.0 / D).then_inc(sem("rms"), 1)
            if t < TILES:
                ready(eng, t)
                eng.activation(junk[0:rows(t), :], src[0:rows(t), t, :], ACT.Square,
                               accum_out=ssq[0:rows(t), t:t + 1]).then_inc(sem("squares"), 1)

    def norm_tile(eng, tag, t, src, dst):
        r = rows(t)
        eng.wait_ge(sem("rms"), tag * TILES + t + 1)
        eng.reciprocal(rinv[0:r, t:t + 1], rms[0:r, t:t + 1]).then_inc(sem("rinv"), 1)
        eng.wait_ge(sem("rinv"), tag * TILES + t + 1)
        eng.scalar_tensor_tensor(out=dst[0:r, t, :], in0=src[0:r, t, :], scalar=rinv[0:r, t:t + 1],
                                 in1=gB[0:r, :], op0=ALU.mult, op1=ALU.mult).then_inc(sem("normed"), 1)

    def norm_and_turn(eng, n, tag, src, dst):
        for t in range(TILES + 1):
            if t < TILES:
                norm_tile(eng, tag, t, src, xn)
            if t:
                turn_dve(eng, n, tag, dst, t - 1)

    def add_norm(eng, tag):
        for t in range(TILES + 1):
            if t < TILES:
                norm_tile(eng, tag, t, wide, wide)
            if t:
                r = rows(t - 1)
                eng.wait_ge(sem("normed"), tag * TILES + t)
                eng.wait_ge(sem(f"x_in{t - 1}"), 32)
                eng.tensor_tensor(x[0:r, t - 1, :], x[0:r, t - 1, :], wide[0:r, t - 1, :], ALU.add)\
                   .then_inc(sem("x_sum"), 1)

    def turn_units():
        return [(t, j) for t in range(TILES) for j in range(2)]

    def turn_pe(eng, n, tag):
        for u, (t, j) in enumerate(turn_units()):
            b = u % 8
            eng.wait_ge(sem("normed"), tag * TILES + t + 1)
            fill(eng, n, b)
            for k in range(4):
                c = (4 * j + k) * P
                mm = eng.transpose(ps[:, b, k * P:k * P + rows(t)], xn[0:rows(t), t, c:c + P],
                                   ident[0:rows(t), 0:rows(t)])
            filled(mm, n, b)

    def turned(t, j, dst):
        return dst[:, 4 * j:4 * j + 4, cols(t)]

    def in_bank(t, b):
        return ps[:, b, :].rearrange("p (k c) -> p k c", c=P)[:, :, 0:rows(t)]

    def turn_act(eng, n, tag, dst):
        for u, (t, j) in enumerate(turn_units()):
            drain(eng, n, u % 8)
            eng.activation(turned(t, j, dst[0]), in_bank(t, u % 8), ACT.Copy).then_inc(sem("turned_high"), 1)
            n[f"free{u % 8}"].add()

    def turn_dve(eng, n, tag, dst, tile):
        for u, (t, j) in enumerate(turn_units()):
            if t != tile:
                continue
            eng.wait_ge(sem("turned_high"), (tag and 2 * TILES) + u + 1)
            n[f"full{u % 8}"].add()
            ins = eng.tensor_tensor(turned(t, j, dst[1]), in_bank(t, u % 8),
                                    turned(t, j, dst[0]).bitcast(F32), ALU.subtract)
            drained(ins, n, u % 8)

    def all_out(eng, n):
        for b in range(8):
            eng.wait_ge(sem(f"free{b}"), n[f"free{b}"].value())


    def constants(eng):
        fills = [(ident, 0.0), (ones, 1.0), (upper, 1.0), (causal, 0.0), (causalT, 0.0), (lastrow, 1.0),
                 (same, 1.0), (supper, 1.0), (scausal, 0.0), (scausalT, 0.0), (slast, 1.0), (sameT, 1.0),
                 (rep8, 1.0), (own8, 0.0), (earlier, 1.0), (eps, EPS), (ssq, 1.0), (qb, 0.0),
                 (gtok, 0.0)]
        for buf, v in fills:
            eng.memset(buf[tuple(slice(None) for _ in buf.shape)], v).then_inc(sem("filled"), 1)
        eng.wait_ge(sem("filled"), len(fills))
        batch_rows = [(ALU.is_ge, [[-S, B], [0, S]], 0, 1), (ALU.is_ge, [[S, B], [0, S]], S - 1, -1)]
        upto = (ALU.is_ge, [[S, B], [1, S]], 0, -1)
        downto = (ALU.is_ge, [[-S, B], [-1, S]], 0, 1)
        plan = [
            (ident, 1.0, [(ALU.not_equal, [[-1, P]], 0, 1)]),
            (upper, 0.0, [(ALU.is_ge, [[1, P]], 0, -1)]),
            (causal, NEG, [(ALU.is_ge, [[-1, P]], 0, 1)]),
            (causalT, NEG, [(ALU.is_ge, [[1, P]], 0, -1)]),
            (lastrow, 0.0, [(ALU.is_equal, [[0, P]], 1 - P, 1)]),
            (same, 0.0, batch_rows),
            (supper, 0.0, batch_rows + [upto]),
            (scausal, NEG, batch_rows + [downto]),
            (scausalT, NEG, batch_rows + [upto]),
            (slast, 0.0, [(ALU.is_equal, [[S, B], [0, S]], S - 1, -1)]),
            (sameT, 0.0, [(ALU.is_ge, [[1, NS]], 0, -S), (ALU.is_ge, [[-1, NS]], S - 1, S)]),
            (rep8, 0.0, [(ALU.is_equal, [[0, P // S], [-1, S]], 0, 1)]),
            (own8, NEG, [(ALU.is_ge, [[-1, S]], 0, 1)]),
            (earlier, 0.0, [(ALU.is_ge, [[1, BLOCKS], [-1, BLOCKS]], -1, 0)]),
        ]
        order = Order(eng, sem("masked"), n_masks)
        for buf, fill_with, cuts in plan:
            whole = buf[tuple(slice(None) for _ in buf.shape)]
            for op, pattern, first, by_row in cuts:
                if len(pattern) == 2 and len(buf.shape) == 2:
                    whole = buf[:, :].rearrange("p (a b) -> p a b", b=pattern[1][1])
                order(eng.affine_select(out=whole, in_=whole, compare_op=op, fill=fill_with, base=first,
                                        pattern=pattern, channel_multiplier=by_row))
        assert n_masks.value() == MASKS

    n_masks = Count()
    MASKS = 22

    def constants_ready(eng):
        eng.wait_ge(sem("masked"), MASKS)

    def load_x(eng, tag, after=None):
        if after is not None:
            after()
        for t in range(PT):
            eng.dma_start(x[:, t, :], x_prompt[0, t * P:(t + 1) * P, :]).then_inc(sem(f"{tag}{t}"), 16)
        eng.dma_start(x[0:NS, PT, :], x_sample.rearrange("b s d -> (b s) d")).then_inc(sem(f"{tag}{PT}"), 16)

    def load_g(eng, g, name="g_in"):
        eng.dma_start(gB[:, :], g.rearrange("(a n) -> a n", a=1).broadcast_to([P, D])).then_inc(sem(name), 16)


    ALL8 = steps(8)

    def sp_project(eng, n):
        def w_rows(k, first, width=CH):
            return w_in[k * P:(k + 1) * P, first:first + width]
        with n.loop(7, ALL8) as c:
            for k in range(KT):
                w_load(eng, n, w_in[k * P:(k + 1) * P, bass.ds(c * CH, CH)])
        for k in range(KT):
            w_load(eng, n, w_rows(k, IF0, P))
        with n.loop(4, ALL8) as c:
            for k in range(KT):
                w_load(eng, n, w_in[k * P:(k + 1) * P, bass.ds(c * CH + GA0, CH)])

    def pe_project(eng, n):
        with n.loop(7, ALL8 | banks(TILES)):
            tokens_chunk(eng, n, hT, KT)
        features_chunk(eng, n, hT, KT, 1)
        with n.loop(4, ALL8 | banks(8)):
            features_chunk(eng, n, hT, KT)

    def copy_tokens(eng, n, dst, mine):
        for t in range(TILES):
            if t % 2 != mine:
                skip(n, t, t == TILES - 1)
                continue
            drain(eng, n, t, t == TILES - 1)
            out, src = dst(t), ps[bank_rows(t), t, :]
            ins = eng.activation(out, src, ACT.Copy) if mine == 0 else eng.tensor_copy(out, src)
            drained(ins, n, t)

    def act_project(eng, n):
        with n.loop(7, ALL8 | banks(TILES)) as c:
            for _ in range(KT):
                w_high(eng, n)
            copy_tokens(eng, n, lambda t: tok[0:rows(t), t, bass.ds(c * CH, CH)], 0)
        for _ in range(KT):
            w_high(eng, n)
        for h in range(2):
            if h == 0:
                eng.wait_ge(sem("small_in"), 64)
            drain(eng, n, h, h == 1)
            drained(eng.activation(gates[:, h * HALFT:(h + 1) * HALFT], ps[0:2 * HM, h, 0:HALFT],
                                   ACT.Identity, bias=bif[:, :]), n, h)

        def merge_gates(c, ahead):
            for _ in range(KT - AHEAD + ahead):
                w_high(eng, n)
            for b in range(8):
                drain(eng, n, b, b == 7)
                dst = sg[:, bass.ds(c * (4 * NT) + (b // 2) * NT + (b % 2) * HALFT, HALFT)]
                drained(eng.activation(dst, ps[:, b, 0:HALFT], ACT.Sigmoid), n, b)

        with n.loop(3, ALL8 | banks(8)) as c:
            merge_gates(c, AHEAD)
        merge_gates(3, 0)
        projected(eng)
        for t, r in ((slice(0, PT), P), (slice(PT, TILES), NS)):
            eng.activation(tok[0:r, t, KM:KM + CH], tok[0:r, t, KM:KM + CH], ACT.Copy,
                           scale=DM ** -0.5).then_inc(sem("km_scaled"), 1)
            eng.activation(tok[0:r, t, OM:OM + CH], tok[0:r, t, OM:OM + CH],
                           ACT.Sigmoid).then_inc(sem("km_scaled"), 1)

    def dve_project(eng, n):
        with n.loop(7, ALL8 | banks(TILES)) as c:
            for _ in range(KT):
                w_low(eng, n)
            copy_tokens(eng, n, lambda t: tok[0:rows(t), t, bass.ds(c * CH, CH)], 1)
        for _ in range(KT):
            w_low(eng, n)
        for h in range(2):
            skip(n, h, h == 1)

        def merge_gates(ahead):
            for _ in range(KT - AHEAD + ahead):
                w_low(eng, n)
            for b in range(8):
                skip(n, b, b == 7)

        with n.loop(3, ALL8 | banks(8)):
            merge_gates(AHEAD)
        merge_gates(0)

    def projected(eng, n_chunks=7):
        for t in range(TILES):
            eng.wait_ge(sem(f"free{t}"), FREE0[t] + n_chunks)

    FREE0 = [2, 2, 1, 1, 1, 1, 1, 1]

    def pool_rotary(eng):
        projected(eng)
        eng.wait_ge(sem("small_in"), 64)
        order = Order(eng, sem("rotated"), Count())
        for t, nt, r in ((slice(0, PT), PT, P), (slice(PT, TILES), 1, NS)):
            if nt == 1:
                heads = tok[0:r, PT, QA:QA + 2 * CH].rearrange("p (h d) -> p h d", d=DH)
                x1, x2 = heads[:, :, 0:HALF], heads[:, :, HALF:2 * HALF]
                shape = [r, 2 * HA, HALF]
                cos = rot[0:r, PT, 0:HALF].unsqueeze(1).broadcast_to(shape)
                sin = rot[0:r, PT, HALF:2 * HALF].unsqueeze(1).broadcast_to(shape)
                y = [b[0:r, 0, :, :] for b in rt]
            else:
                heads = tok[:, t, QA:QA + 2 * CH].rearrange("p t (h d) -> p t h d", d=DH)
                x1, x2 = heads[:, :, :, 0:HALF], heads[:, :, :, HALF:2 * HALF]
                shape = [r, PT, 2 * HA, HALF]
                cos = rot[0:r, t, 0:HALF].unsqueeze(2).broadcast_to(shape)
                sin = rot[0:r, t, HALF:2 * HALF].unsqueeze(2).broadcast_to(shape)
                y = [b[0:r, :, :, :] for b in rt]
            order(eng.tensor_tensor(y[0], x1, sin, ALU.mult))
            order(eng.tensor_tensor(y[1], x2, sin, ALU.mult))
            order(eng.tensor_tensor(y[2], x1, cos, ALU.mult))
            order(eng.tensor_tensor(y[3], x2, cos, ALU.mult))
            order(eng.tensor_tensor(x1, y[2], y[1], ALU.subtract))
            order(eng.tensor_tensor(x2, y[3], y[0], ALU.add))
        for dst, c in ((k_prompt, KA), (v_prompt, VA)):
            eng.dma_start(dst[0].rearrange("(t p) h d -> p t (h d)", p=P),
                          tok[:, 0:PT, c:c + CH]).then_inc(sem("kv_out"), 16)
        for dst, c in ((k_sample, KA), (v_sample, VA)):
            eng.dma_start(dst.rearrange("b s h d -> (b s) (h d)"),
                          tok[0:NS, PT, c:c + CH]).then_inc(sem("kv_out"), 16)

    ROTATED = 12


    def pool_heads(eng):
        with eng.Fori(0, HP) as i:
            eng.wait_ge(sem("a_turned"), i * 2)
            eng.tensor_copy(qc[:, :, :], tok[:, 0:PT, bass.ds(i * P + QA, P)]).then_inc(sem("a_copied"), 1)
            eng.tensor_copy(kc[:, :, :], tok[:, 0:PT, bass.ds(i * P + KA, P)]).then_inc(sem("a_copied"), 1)
            eng.wait_ge(sem("a_pv"), i * 8)
            eng.tensor_copy(vc[:, :, :], tok[:, 0:PT, bass.ds(i * P + VA, P)]).then_inc(sem("a_copied"), 1)

    units = [(h2, qt) for h2 in range(2) for qt in range(PT)]

    def back(i, u, k):
        return i * 8 + max(u - k + 1, 0)

    def pe_prompt(eng):
        eng.wait_ge(sem("s_qk"), 2)
        eng.wait_ge(sem("g_steps"), 4)
        with eng.Fori(0, HP) as i:
            for which, (src, b) in enumerate(((qc, 0), (kc, 1))):
                eng.wait_ge(sem("a_copied"), i * 3 + which + 1)
                eng.wait_ge(sem("a_qT" if b == 0 else "a_kT"), i)
                for t in range(PT):
                    mm = eng.transpose(ps[:, b, t * P:(t + 1) * P], src[:, t, :], ident[:, :])
                mm.then_inc(sem("a_turned"), 1)

            def scores(u):
                h2, qt = units[u]
                g = slice(h2 * DH, (h2 + 1) * DH)
                eng.wait_ge(sem("a_exp"), back(i, u, 3))
                w = (qt + 1) * P
                eng.matmul(ps[:, 2 + u % 3, 0:w], QTp[g, qt * P:(qt + 1) * P], KTp[g, 0:w],
                           start=True, stop=True).then_inc(sem("a_scores"), 1)

            eng.wait_ge(sem("a_qT"), i + 1)
            eng.wait_ge(sem("a_kT"), i + 1)
            for u in range(3):
                scores(u)
            for u in range(9):
                if u < 8:
                    h2, qt = units[u]
                    eng.wait_ge(sem("a_norm"), i * 8 + u + 1)
                    eng.wait_ge(sem("a_prT"), back(i, u, 2))
                    for k in range(qt + 1):
                        mm = eng.transpose(ps[:, 5 + u % 2, k * P:(k + 1) * P],
                                           pr[:, u % 3, k * P:(k + 1) * P], ident[:, :])
                    mm.then_inc(sem("a_prT_ps"), 1)
                if u + 3 < 8:
                    scores(u + 3)
                if u >= 1:
                    v = u - 1
                    h2, qt = units[v]
                    eng.wait_ge(sem("a_prT"), i * 8 + v + 1)
                    if v == 0:
                        eng.wait_ge(sem("a_copied"), i * 3 + 3)
                        eng.wait_ge(sem("a_out"), i)
                    for k in range(qt + 1):
                        mm = eng.matmul(ps[h2 * DH:(h2 + 1) * DH, 7, qt * P:(qt + 1) * P],
                                        vc[:, k, h2 * DH:(h2 + 1) * DH], prT[:, v % 2, k * P:(k + 1) * P],
                                        start=(k == 0), stop=(k == qt))
                    mm.then_inc(sem("a_pv"), 1)

    def act_prompt(eng):
        with eng.Fori(0, HP) as i:
            eng.wait_ge(sem("a_turned"), i * 2 + 1)
            eng.wait_ge(sem("a_scores"), i * 8)
            eng.activation(QTp[:, :], ps[:, 0, :], ACT.Copy).then_inc(sem("a_qT"), 1)
            for u in range(9):
                if u < 8:
                    w = (units[u][1] + 1) * P
                    eng.wait_ge(sem("a_max"), i * 8 + u + 1)
                    eng.wait_ge(sem("a_prT_ps"), back(i, u, 3))
                    eng.activation(pr[:, u % 3, 0:w], ps[:, 2 + u % 3, 0:w], ACT.Exp, bias=anx[:, u:u + 1],
                                   scale=SC, accum_out=asum[:, u:u + 1]).then_inc(sem("a_exp"), 1)
                if u >= 1:
                    v = u - 1
                    w = (units[v][1] + 1) * P
                    eng.wait_ge(sem("a_prT_ps"), i * 8 + v + 1)
                    eng.wait_ge(sem("a_pv"), back(i, v, 2))
                    eng.activation(prT[:, v % 2, 0:w], ps[:, 5 + v % 2, 0:w], ACT.Copy).then_inc(sem("a_prT"), 1)
            eng.wait_ge(sem("a_pv"), i * 8 + 8)
            eng.activation(attT_flat[0][:, bass.ds(i * NT, T)], ps[:, 7, :], ACT.Copy).then_inc(sem("a_high"), 1)

    def dve_prompt(eng):
        order = Order(eng, sem("a_steps"), Count())
        order.count.per = 24
        with eng.Fori(0, HP) as i:
            order.count.i = i
            eng.wait_ge(sem("a_turned"), i * 2 + 2)
            eng.wait_ge(sem("a_scores"), i * 8)
            eng.tensor_copy(KTp[:, :], ps[:, 1, :]).then_inc(sem("a_kT"), 1)
            for u in range(9):
                if u < 8:
                    qt = units[u][1]
                    own = ps[:, 2 + u % 3, qt * P:(qt + 1) * P]
                    eng.wait_ge(sem("a_scores"), i * 8 + u + 1)
                    order(eng.tensor_tensor(own, own, causal[:, :], ALU.add))
                    order(eng.tensor_reduce(amx[:, u:u + 1], ps[:, 2 + u % 3, 0:(qt + 1) * P], X, ALU.max))
                    eng.tensor_scalar(anx[:, u:u + 1], amx[:, u:u + 1], -SC, None, ALU.mult)\
                       .then_inc(sem("a_max"), 1)
                if u >= 1:
                    v = u - 1
                    w = (units[v][1] + 1) * P
                    eng.wait_ge(sem("a_exp"), i * 8 + v + 1)
                    order(eng.reciprocal(arec[:, v:v + 1], asum[:, v:v + 1]))
                    eng.tensor_scalar(pr[:, v % 3, 0:w], pr[:, v % 3, 0:w], arec[:, v:v + 1], None, ALU.mult)\
                       .then_inc(sem("a_norm"), 1)
            eng.wait_ge(sem("a_high"), i + 1)
            eng.tensor_tensor(attT_flat[1][:, bass.ds(i * NT, T)], ps[:, 7, :],
                              attT_flat[0][:, bass.ds(i * NT, T)].bitcast(F32), ALU.subtract)\
               .then_inc(sem("a_out"), 1)
            assert order.count.n == 24

    attT_flat = [a[:, :, :].rearrange("p h n -> p (h n)") for a in attT]
    mlT_flat = [a[:, :, :].rearrange("p h n -> p (h n)") for a in mlT]


    VIEWS = ((P, slice(0, PT)), (NS, slice(PT, TILES)))

    def pe_gates(eng):
        for t in range(TILES):
            mm = eng.transpose(ps[0:rows(t), 2, t * 8:t * 8 + 8], gates[:, cols(t)], ident[0:8, 0:8])
        mm.then_inc(sem("g_turned"), 1)
        eng.wait_ge(sem("rotated"), ROTATED)
        for b, c0 in ((0, QA), (1, KA)):
            for h in range(HP):
                mm = eng.transpose(ps[:, b, h * NS:(h + 1) * NS], tok[0:NS, PT, c0 + h * P:c0 + (h + 1) * P],
                                   ident[0:NS, 0:NS])
            mm.then_inc(sem("s_turned"), 1)

    def dve_gates(eng):
        eng.wait_ge(sem("g_turned"), 1)
        order = Order(eng, sem("g_steps"), Count())
        order(eng.tensor_copy(gtok[:, 0:PT, :], ps[:, 2, 0:PT * 8].rearrange("p (t g) -> p t g", g=8)))
        order(eng.tensor_copy(gtok[0:NS, PT, :], ps[0:NS, 2, PT * 8:PT * 8 + 8]))
        f = gtok[:, :, HM:2 * HM]
        order(eng.scalar_tensor_tensor(out=lf[:, :, :], in0=f, scalar=-1.0, in1=f, op0=ALU.mult, op1=ALU.min))
        eng.tensor_scalar(lt[:, :, :], f, 0.0, None, ALU.min).then_inc(sem("g_abs"), 1)
        eng.wait_ge(sem("g_ln"), 2)
        order(eng.tensor_tensor(lf[:, :, :], lt[:, :, :], lf[:, :, :], ALU.subtract))
        eng.wait_ge(sem("s_turned"), 2)
        eng.tensor_copy(QTs[:, :, :], ps[:, 0, 0:HP * NS].rearrange("p (h n) -> p h n", n=NS))\
           .then_inc(sem("s_qk"), 1)
        eng.tensor_copy(KTs[:, :, :], ps[:, 1, 0:HP * NS].rearrange("p (h n) -> p h n", n=NS))\
           .then_inc(sem("s_qk"), 1)

    def act_gates(eng):
        eng.wait_ge(sem("g_abs"), 1)
        eng.activation(lf[:, :, :], lf[:, :, :], ACT.Exp).then_inc(sem("g_ln"), 1)
        eng.wait_ge(sem("g_ln"), 1)
        eng.activation(lf[:, :, :], lf[:, :, :], ACT.Ln, bias=ones[:, 0:1]).then_inc(sem("g_ln"), 1)


    def pool_mlstm(eng):
        eng.wait_ge(sem("a_copied"), 3 * HP)
        eng.wait_ge(sem("a_out"), HP)
        eng.wait_ge(sem("km_scaled"), 4)
        eng.memset(mv[:, :, DM:DM + 1], 1.0).then_inc(sem("m_set"), 1)
        eng.memset(CTn[:, :, :], 0.0).then_inc(sem("m_set"), 1)
        eng.memset(mprev[:, :], 0.0).then_inc(sem("m_set"), 1)
        with eng.Fori(0, PT) as c:
            eng.wait_ge(sem("m_update"), c)
            row = lambda c0: tok_flat[:, bass.ds(c * (7 * CH) + c0, CH)].rearrange("p (h d) -> p h d", d=DM)
            eng.tensor_copy(mq[:, :, :], row(QM)).then_inc(sem("m_copied"), 1)
            eng.tensor_copy(mk[:, :, :], row(KM)).then_inc(sem("m_copied"), 1)
            eng.tensor_copy(mv[:, :, 0:DM], row(VM)).then_inc(sem("m_copied"), 1)

    tok_flat = tok[:, :, :].rearrange("p t n -> p (t n)")
    lf_flat = lf[:, :, :].rearrange("p t g -> p (t g)")
    gt_flat = gtok[:, :, :].rearrange("p t g -> p (t g)")

    def two(b, h, r=P, w=DM + 1):
        return ps[0:r, b + h // 2, (h % 2) * (DM + 1):(h % 2) * (DM + 1) + w]

    def pe_mlstm(eng):
        eng.wait_ge(sem("m_set"), 3)
        eng.wait_ge(sem("a_out"), HP)
        with eng.Fori(0, PT) as c:
            eng.wait_ge(sem("m_copied"), c * 3 + 1)
            eng.wait_ge(sem("m_num"), c)
            for h in range(HM):
                mm = eng.transpose(ps[:, 0, h * P:(h + 1) * P], mq[:, h, :], ident[:, :])
            mm.then_inc(sem("m_qT_ps"), 1)
            eng.wait_ge(sem("m_copied"), c * 3 + 2)
            for h in range(HM):
                mm = eng.transpose(ps[:, 1, h * P:(h + 1) * P], mk[:, h, :], ident[:, :])
            mm.then_inc(sem("m_kT_ps"), 1)
            eng.wait_ge(sem("m_state"), c)
            eng.matmul(ps[:, 2, 0:HM], upper[:, :], lf_flat[:, bass.ds(c * HM, HM)],
                       start=True, stop=True).then_inc(sem("m_b_ps"), 1)
            eng.wait_ge(sem("m_diag_a"), c + 1)
            eng.matmul(ps[:, 3, :], ones[:, :], mdg[:, :, :].rearrange("p h n -> p (h n)"),
                       start=True, stop=True).then_inc(sem("m_a_ps"), 1)
            eng.wait_ge(sem("m_qT"), c + 1)
            eng.wait_ge(sem("m_kT"), c + 1)
            eng.wait_ge(sem("m_low"), c)
            for h in range(HM):
                mm = eng.matmul(ps[:, 5, h * P:(h + 1) * P], mkT[:, h, :], mqT[:, h, :], start=True, stop=True)
            mm.then_inc(sem("m_qk_ps"), 1)
            for h in range(HM):
                mm = eng.matmul(two(0, h), mqT[:, h, :], CTn[:, h, :], start=True, stop=True)
            eng.wait_ge(sem("m_diag_M"), c + 1)
            eng.matmul(ps[:, 4, :], ones[:, :], mdg[:, :, :].rearrange("p h n -> p (h n)"),
                       start=True, stop=True).then_inc(sem("m_M_ps"), 1)
            eng.matmul(ps[:, 2, 8:8 + 2 * HM], lastrow[:, :], mM[:, :, :].rearrange("p a h -> p (a h)"),
                       start=True, stop=True).then_inc(sem("m_last_ps"), 1)
            eng.wait_ge(sem("m_A"), c + 1)
            eng.wait_ge(sem("m_copied"), c * 3 + 3)
            for h in range(HM):
                mm = eng.matmul(two(6, h), mA[:, h, :], mv[:, h, :], start=True, stop=True)
            mm.then_inc(sem("m_num_ps"), 1)
            eng.wait_ge(sem("m_kw"), c + 1)
            for h in range(HM):
                mm = eng.matmul(two(3, h), mkw[:, h, :], mv[:, h, :], start=True, stop=True)
            mm.then_inc(sem("m_update"), 1)
            eng.wait_ge(sem("m_h"), c + 1)
            for h in range(HM):
                mm = eng.transpose(ps[:, 5, h * P:(h + 1) * P], mout[:, h, :], ident[:, :])
            mm.then_inc(sem("m_hT_ps"), 1)
        eng.wait_ge(sem("m_state"), PT)
        for h in range(HM):
            eng.transpose(ps[:, 0, h * P:(h + 1) * P], CTn[:, h, 0:DM], ident[:, :])
        eng.transpose(ps[0:HM, 1, 0:P], CTn[:, :, DM], ident[:, :]).then_inc(sem("m_C_ps"), 1)

    def act_mlstm(eng):
        with eng.Fori(0, PT) as c:
            eng.wait_ge(sem("m_qT_ps"), c + 1)
            eng.wait_ge(sem("m_num"), c)
            eng.activation(mqT[:, :, :], ps[:, 0, :].rearrange("p (h n) -> p h n", n=P),
                           ACT.Copy).then_inc(sem("m_qT"), 1)
            eng.wait_ge(sem("m_gap"), c + 1)
            for h in range(HM):
                eng.activation(wgt[:, h, :], gap[:, h, :], ACT.Exp, bias=ma[:, h:h + 1])\
                   .then_inc(sem("m_wD"), 1)
            eng.wait_ge(sem("m_exponents"), c + 1)
            eng.activation(mev[:, :, :], mex[:, :, :], ACT.Exp).then_inc(sem("m_exps"), 1)
            eng.wait_ge(sem("m_hT_ps"), c + 1)
            eng.activation(ml_at(mlT, c)[0], ps[:, 5, :].rearrange("p (h n) -> p h n", n=P), ACT.Copy)\
               .then_inc(sem("m_high"), 1)

    def ml_at(dst, c):
        return [a[:, :, bass.ds(c * P, P)] for a in dst]

    M_STEPS = 20

    def dve_mlstm(eng):
        order = Order(eng, sem("m_steps"), Count())
        per = order.count.per = M_STEPS
        eng.wait_ge(sem("kv_out"), 64)
        eng.wait_ge(sem("m_set"), 3)
        eng.wait_ge(sem("km_scaled"), 4)
        with eng.Fori(0, PT) as c:
            order.count.i = c
            eng.wait_ge(sem("m_kT_ps"), c + 1)
            eng.tensor_copy(mkT[:, :, :], ps[:, 1, :].rearrange("p (h n) -> p h n", n=P)).then_inc(sem("m_kT"), 1)
            eng.wait_ge(sem("m_b_ps"), c + 1)
            order(eng.tensor_copy(mM[:, 1, :], ps[:, 2, 0:HM]))
            order(eng.tensor_tensor(ma[:, :], gt_flat[:, bass.ds(c * 8, HM)], mM[:, 1, :], ALU.subtract))
            idb = ident[:, :].unsqueeze(1).broadcast_to([P, HM, P])
            eng.tensor_tensor(mdg[:, :, :], idb, wide_of(ma[:, :], P), ALU.mult).then_inc(sem("m_diag_a"), 1)
            eng.wait_ge(sem("m_a_ps"), c + 1)
            order(eng.tensor_tensor(gap[:, :, :], ps[:, 3, :].rearrange("p (h n) -> p h n", n=P),
                                    causal[:, :].unsqueeze(1).broadcast_to([P, HM, P]), ALU.add))
            order(eng.tensor_reduce(mden[:, :], gap[:, :, :], X, ALU.max))
            order(eng.tensor_tensor(mM[:, 0, :], mden[:, :], mprev[:, :], ALU.max))
            order(eng.tensor_scalar(mnM[:, :], mM[:, 0, :], -1.0, None, ALU.mult))
            eng.tensor_tensor(mdg[:, :, :], idb, wide_of(mnM[:, :], P), ALU.mult).then_inc(sem("m_diag_M"), 1)
            eng.wait_ge(sem("m_M_ps"), c + 1)
            eng.tensor_tensor(gap[:, :, :], ps[:, 4, :].rearrange("p (h n) -> p h n", n=P),
                              causalT[:, :].unsqueeze(1).broadcast_to([P, HM, P]), ALU.add)\
               .then_inc(sem("m_gap"), 1)
            eng.wait_ge(sem("m_last_ps"), c + 1)
            order(eng.tensor_copy(mlast[:, :, :], ps[:, 2, 8:8 + 2 * HM].rearrange("p (a h) -> p a h", h=HM)))
            order(eng.tensor_tensor(mex[:, 0, :], mprev[:, :], mM[:, 0, :], ALU.subtract))
            order(eng.scalar_tensor_tensor(out=mex[:, 1, :], in0=mM[:, 0, :], scalar=-1.0, in1=mM[:, 1, :],
                                           op0=ALU.mult, op1=ALU.subtract))
            order(eng.tensor_tensor(mex[:, 2, :], ma[:, :], mlast[:, 0, :], ALU.subtract))
            eng.tensor_tensor(mex[:, 3, :], mprev[:, :], mlast[:, 0, :], ALU.subtract)\
               .then_inc(sem("m_exponents"), 1)
            eng.wait_ge(sem("m_qk_ps"), c + 1)
            eng.wait_ge(sem("m_wD"), c * HM + HM)
            eng.tensor_tensor(mA[:, :, :], ps[:, 5, :].rearrange("p (h n) -> p h n", n=P), wgt[:, :, :],
                              ALU.mult).then_inc(sem("m_A"), 1)
            eng.wait_ge(sem("m_exps"), c + 1)
            eng.tensor_tensor(mkw[:, :, :], mk[:, :, :], wide_of(mev[:, 2, :], P), ALU.mult)\
               .then_inc(sem("m_kw"), 1)
            eng.wait_ge(sem("m_num_ps"), c + 1)
            for h in range(0, HM, 2):
                order(eng.tensor_copy(mnum[:, h:h + 2, :], ps[:, 6 + h // 2, 0:2 * (DM + 1)]
                                      .rearrange("p (h n) -> p h n", n=DM + 1)))
            for h in range(HM):
                ins = eng.scalar_tensor_tensor(out=mnum[:, h, :], in0=two(0, h), scalar=mev[:, 0, h:h + 1],
                                               in1=mnum[:, h, :], op0=ALU.mult, op1=ALU.add)
                if h < HM - 1:
                    order(ins)
            ins.then_inc(sem("m_num"), 1)
            eng.wait_ge(sem("m_num"), c + 1)
            order(eng.scalar_tensor_tensor(out=mden[:, :], in0=mnum[:, :, DM], scalar=-1.0, in1=mnum[:, :, DM],
                                           op0=ALU.mult, op1=ALU.max))
            order(eng.tensor_tensor(mden[:, :], mden[:, :], mev[:, 1, :], ALU.max))
            order(eng.reciprocal(mden[:, :], mden[:, :]))
            for h in range(HM):
                ins = eng.scalar_tensor_tensor(
                    out=mout[:, h, :], in0=mnum[:, h, 0:DM], scalar=mden[:, h:h + 1],
                    in1=tok_flat[:, bass.ds(c * (7 * CH) + OM + h * DM, DM)], op0=ALU.mult, op1=ALU.mult)
            ins.then_inc(sem("m_h"), 1)
            eng.wait_ge(sem("m_update"), c + 1)
            for h in range(HM):
                order(eng.scalar_tensor_tensor(out=CTn[:, h, :], in0=CTn[:, h, :], scalar=mev[:, 3, h:h + 1],
                                               in1=two(3, h), op0=ALU.mult, op1=ALU.add)) if h < 2 else \
                    eng.scalar_tensor_tensor(out=CTn[:, h, :], in0=CTn[:, h, :], scalar=mev[:, 3, h:h + 1],
                                             in1=two(3, h), op0=ALU.mult, op1=ALU.add)
            eng.tensor_tensor(mprev[:, :], mlast[:, 0, :], mlast[:, 1, :], ALU.add).then_inc(sem("m_state"), 1)
            eng.wait_ge(sem("m_state"), c + 1)
            eng.wait_ge(sem("m_high"), c + 1)
            eng.tensor_tensor(ml_at(mlT, c)[1], ps[:, 5, :].rearrange("p (h n) -> p h n", n=P),
                              ml_at(mlT, c)[0].bitcast(F32), ALU.subtract).then_inc(sem("m_low"), 1)
            assert order.count.n == per, order.count.n
        eng.wait_ge(sem("m_C_ps"), 1)
        eng.tensor_copy(Cst[:, :, :], ps[:, 0, :].rearrange("p (h n) -> p h n", n=P)).then_inc(sem("m_Cout"), 1)
        eng.tensor_copy(nst[:, :], ps[0:HM, 1, 0:P]).then_inc(sem("m_Cout"), 1)

    def pool_mlstm_out(eng):
        eng.wait_ge(sem("m_Cout"), 2)
        eng.wait_ge(sem("m_state"), PT)
        eng.dma_start(C_prompt[0].rearrange("h d e -> d h e"), Cst[:, :, :]).then_inc(sem("m_out"), 16)
        eng.dma_start(n_prompt[0], nst[:, :]).then_inc(sem("m_out"), 16)
        eng.dma_start(m_prompt, mprev[0:1, :]).then_inc(sem("m_out"), 16)


    def sp_states(eng):
        eng.wait_ge(sem("m_copied"), 3 * PT)
        eng.wait_ge(sem("m_low"), PT)
        eng.dma_start(sC[:, :, :], state_C.rearrange("b h d e -> d (b h) e")).then_inc(sem("d_C_in"), 16)
        eng.dma_start(snn[:, :], state_n.rearrange("b h e -> b (h e)")).then_inc(sem("d_n_in"), 16)

    def pool_states(eng):
        row = lambda c0: tok[0:NS, PT, c0:c0 + CH].rearrange("p (h d) -> p h d", d=DM)
        eng.wait_ge(sem("m_copied"), 3 * PT)
        eng.tensor_copy(sk[:, :, :], row(KM)).then_inc(sem("m_set"), 1)
        eng.memset(sv[:, :, DM:DM + 1], 1.0).then_inc(sem("m_set"), 1)
        eng.tensor_copy(sv[:, :, 0:DM], row(VM)).then_inc(sem("m_set"), 1)
        eng.wait_ge(sem("m_h"), PT)
        eng.memset(sqp[:, :, :], 0.0).then_inc(sem("m_set"), 1)

    def pool_keys_by_batch(eng):
        eng.wait_ge(sem("m_kw"), PT + 1)
        eng.wait_ge(sem("d_qC_ps"), HM)
        for h in range(HM):
            if h >= 2:
                eng.wait_ge(sem("m_update"), PT + h - 1)
            eng.tensor_tensor(skw[h % 2][:, :, :], sk[:, h, :].unsqueeze(1).broadcast_to([NS, B, DM]),
                              same[:, :, 0:1].broadcast_to([NS, B, DM]), ALU.mult).then_inc(sem("d_kwb"), 1)

    update_banks = [(5, 6), (7, 2), (5, 6), (7, 2)]

    def pe_sample(eng):
        eng.wait_ge(sem("m_Cout"), 2)
        eng.wait_ge(sem("m_low"), PT)
        eng.wait_ge(sem("small_in"), 64)
        eng.matmul(ps[0:NS, 2, 0:HM], sameT[:, :], smb[:, :], start=True, stop=True)
        eng.matmul(ps[0:NS, 2, 8:8 + HM], supper[:, :, :].rearrange("p b s -> p (b s)"), lf[0:NS, PT, :],
                   start=True, stop=True).then_inc(sem("m_b_ps"), 1)
        for b, c0 in ((0, QM), (1, KM)):
            for h in range(HM):
                mm = eng.transpose(ps[:, b, h * NS:(h + 1) * NS], tok[0:NS, PT, c0 + h * DM:c0 + (h + 1) * DM],
                                   ident[0:NS, 0:NS])
            mm.then_inc(sem("m_qT_ps"), 1)
        eng.wait_ge(sem("m_diag_a"), PT + 1)
        eng.matmul(ps[0:NS, 5, 0:HM * NS], ones[0:NS, 0:NS], sdg[:, :, :].rearrange("p h n -> p (h n)"),
                   start=True, stop=True).then_inc(sem("m_a_ps"), 1)
        eng.wait_ge(sem("d_n_in"), 16)
        for h in range(HM):
            mm = eng.transpose(ps[:, 6, h * B:(h + 1) * B], snn[:, h * DM:(h + 1) * DM], ident[0:B, 0:B])
        mm.then_inc(sem("m_kT_ps"), 1)
        eng.wait_ge(sem("d_C_in"), 16)
        for g in range(B):
            if g >= 2:
                eng.wait_ge(sem("d_CT"), g - 1)
            for h in range(HM):
                mm = eng.transpose(ps[:, 3 + g % 2, h * P:(h + 1) * P], sC[:, g * HM + h, :], ident[:, :])
            mm.then_inc(sem("d_CT_ps"), 1)
        eng.wait_ge(sem("m_qT"), PT + 2)
        for h in range(HM):
            mm = eng.matmul(ps[0:NS, 7, h * NS:(h + 1) * NS], skT[:, h, :], sqT[:, h, :], start=True, stop=True)
        mm.then_inc(sem("m_qk_ps"), 1)
        eng.wait_ge(sem("m_diag_M"), PT + 1)
        eng.matmul(ps[0:NS, 5, 0:HM * NS], ones[0:NS, 0:NS], sdg[:, :, :].rearrange("p h n -> p (h n)"),
                   start=True, stop=True).then_inc(sem("m_M_ps"), 1)
        eng.matmul(ps[0:NS, 2, 64:64 + 2 * HM], slast[:, :, :].rearrange("p b s -> p (b s)"),
                   mM[0:NS, :, :].rearrange("p a h -> p (a h)"), start=True, stop=True)\
           .then_inc(sem("m_last_ps"), 1)
        eng.wait_ge(sem("d_CT"), B)
        for h in range(HM):
            eng.wait_ge(sem("d_qp"), h + 1)
            for b in range(B):
                mm = eng.matmul(two(3, h, NS), sqp[:, h % 2, b * NS:(b + 1) * NS], sCT[:, b * HM + h, :],
                                start=(b == 0), stop=(b == B - 1))
            mm.then_inc(sem("d_qC_ps"), 1)
        eng.wait_ge(sem("m_A"), PT + 1)
        for h in range(HM):
            mm = eng.matmul(two(0, h, NS), sA[:, h, :], sv[:, h, :], start=True, stop=True)
        mm.then_inc(sem("m_num_ps"), 1)
        eng.wait_ge(sem("d_decb"), 1)
        eng.matmul(ps[0:B, 2, 80:80 + 2 * HM], slast[:, :, 0], mnew[:, :, :].rearrange("p a h -> p (a h)"),
                   start=True, stop=True)
        eng.matmul(ps[:, 2, 96:96 + B * HM], ones[0:NS, :], sdecb[:, :, :].rearrange("p b h -> p (b h)"),
                   start=True, stop=True).then_inc(sem("d_dec_ps"), 1)
        eng.wait_ge(sem("m_kw"), PT + 1)
        eng.matmul(ps[0:B, 7, :], same[:, :, 0], sk[:, :, :].rearrange("p h d -> p (h d)"),
                   start=True, stop=True).then_inc(sem("d_n_ps"), 1)
        for h in range(HM):
            eng.wait_ge(sem("d_kwb"), h + 1)
            if h == 1:
                eng.wait_ge(sem("d_n"), 1)
            if h >= 2:
                eng.wait_ge(sem("d_C"), h - 1)
            for k in range(2):
                mm = eng.matmul(ps[:, update_banks[h][k], :], tok[0:NS, PT, VM + h * DM:VM + (h + 1) * DM],
                                skw[h % 2][:, 4 * k:4 * k + 4, :].rearrange("p b d -> p (b d)"), start=True, stop=True)
            mm.then_inc(sem("m_update"), 1)
        eng.wait_ge(sem("m_h"), PT + 1)
        for h in range(HM):
            mm = eng.transpose(ps[:, 0, h * NS:(h + 1) * NS], sout[:, h, :], ident[0:NS, 0:NS])
        mm.then_inc(sem("m_hT_ps"), 1)

    def act_sample(eng):
        eng.wait_ge(sem("m_qT_ps"), PT + 1)
        eng.activation(sqT[:, :, :], ps[:, 0, 0:HM * NS].rearrange("p (h n) -> p h n", n=NS), ACT.Copy)\
           .then_inc(sem("m_qT"), 1)
        eng.wait_ge(sem("m_out"), 48)
        for g in range(B):
            eng.wait_ge(sem("d_CT_ps"), g + 1)
            eng.activation(sCT[:, g * HM:(g + 1) * HM, 0:DM], ps[:, 3 + g % 2, :].rearrange("p (h n) -> p h n", n=P),
                           ACT.Copy).then_inc(sem("d_CT"), 1)
        eng.wait_ge(sem("m_gap"), PT + 1)
        for h in range(HM):
            eng.activation(swgt[:, h, :], sgap[:, h, :], ACT.Exp, bias=ma[0:NS, h:h + 1]).then_inc(sem("m_wD"), 1)
        eng.wait_ge(sem("m_exponents"), PT + 1)
        eng.activation(mev[0:NS, :, :], mex[0:NS, :, :], ACT.Exp).then_inc(sem("m_exps"), 1)
        eng.wait_ge(sem("m_hT_ps"), PT + 1)
        eng.activation(mlT[0][:, :, T:NT], ps[:, 0, 0:HM * NS].rearrange("p (h n) -> p h n", n=NS), ACT.Copy)\
           .then_inc(sem("m_high"), 1)

    def dve_sample(eng):
        order = Order(eng, sem("m_steps"), Count())
        order.count.base = M_STEPS * PT
        r = slice(0, NS)
        eng.wait_ge(sem("m_out"), 48)
        eng.wait_ge(sem("m_set"), 3 + 4)
        eng.wait_ge(sem("m_b_ps"), PT + 1)
        order(eng.tensor_copy(mprev[r, :], ps[r, 2, 0:HM]))
        order(eng.tensor_copy(mM[r, 1, :], ps[r, 2, 8:8 + HM]))
        order(eng.tensor_tensor(ma[r, :], gtok[r, PT, 0:HM], mM[r, 1, :], ALU.subtract))
        idb = ident[r, 0:NS].unsqueeze(1).broadcast_to([NS, HM, NS])
        eng.tensor_tensor(sdg[:, :, :], idb, wide_of(ma[r, :], NS), ALU.mult).then_inc(sem("m_diag_a"), 1)
        eng.wait_ge(sem("m_qT_ps"), PT + 2)
        eng.tensor_copy(skT[:, :, :], ps[:, 1, 0:HM * NS].rearrange("p (h n) -> p h n", n=NS))\
           .then_inc(sem("m_qT"), 1)
        eng.wait_ge(sem("m_kT_ps"), PT + 1)
        sn = sCT[:, :, DM].rearrange("p (b h) -> p h b", h=HM)
        order(eng.tensor_copy(sn, ps[:, 6, 0:HM * B].rearrange("p (h b) -> p h b", b=B)))

        def mask3(m):
            return m[:, :, :].rearrange("p b s -> p (b s)").unsqueeze(1).broadcast_to([NS, HM, NS])

        def bank3(b):
            return ps[r, b, 0:HM * NS].rearrange("p (h n) -> p h n", n=NS)

        eng.wait_ge(sem("m_a_ps"), PT + 1)
        order(eng.tensor_tensor(sgap[:, :, :], bank3(5), mask3(scausal), ALU.add))
        order(eng.tensor_reduce(mden[r, :], sgap[:, :, :], X, ALU.max))
        order(eng.tensor_tensor(mM[r, 0, :], mden[r, :], mprev[r, :], ALU.max))
        order(eng.tensor_scalar(mnM[r, :], mM[r, 0, :], -1.0, None, ALU.mult))
        eng.tensor_tensor(sdg[:, :, :], idb, wide_of(mnM[r, :], NS), ALU.mult).then_inc(sem("m_diag_M"), 1)
        eng.wait_ge(sem("m_M_ps"), PT + 1)
        eng.tensor_tensor(sgap[:, :, :], bank3(5), mask3(scausalT), ALU.add).then_inc(sem("m_gap"), 1)
        eng.wait_ge(sem("m_qT"), PT + 2)
        for h in range(2):
            eng.tensor_copy(sqp[:, h % 2, :].rearrange("p (b k) -> p b k", k=NS + S)[:, :, 0:S], sqT[:, h, :].rearrange("p (b s) -> p b s", s=S))\
               .then_inc(sem("d_qp"), 1)
        eng.wait_ge(sem("m_last_ps"), PT + 1)
        order(eng.tensor_copy(mlast[r, :, :], ps[r, 2, 64:64 + 2 * HM].rearrange("p (a h) -> p a h", h=HM)))
        order(eng.tensor_tensor(mex[r, 0, :], mprev[r, :], mM[r, 0, :], ALU.subtract))
        order(eng.scalar_tensor_tensor(out=mex[r, 1, :], in0=mM[r, 0, :], scalar=-1.0, in1=mM[r, 1, :],
                                       op0=ALU.mult, op1=ALU.subtract))
        order(eng.tensor_tensor(mex[r, 2, :], ma[r, :], mlast[r, 0, :], ALU.subtract))
        eng.tensor_tensor(mex[r, 3, :], mprev[r, :], mlast[r, 0, :], ALU.subtract).then_inc(sem("m_exponents"), 1)
        order(eng.tensor_tensor(mnew[:, 1, :], mlast[r, 0, :], mlast[r, 1, :], ALU.add))
        eng.wait_ge(sem("m_qk_ps"), PT + 1)
        eng.wait_ge(sem("m_wD"), PT * HM + HM)
        eng.tensor_tensor(sA[:, :, :], bank3(7), swgt[:, :, :], ALU.mult).then_inc(sem("m_A"), 1)
        eng.wait_ge(sem("m_exps"), PT + 1)
        order(eng.tensor_copy(mnew[:, 0, :], mev[r, 3, :]))
        eng.tensor_tensor(sdecb[:, :, :], slast[:, :, 0:1].broadcast_to([NS, B, HM]),
                          mev[r, 3, :].unsqueeze(1).broadcast_to([NS, B, HM]), ALU.mult).then_inc(sem("d_decb"), 1)
        eng.tensor_tensor(sk[:, :, :], sk[:, :, :], wide_of(mev[r, 2, :], DM), ALU.mult).then_inc(sem("m_kw"), 1)
        for h in range(2, HM):
            eng.wait_ge(sem("d_qC_ps"), h - 1)
            eng.tensor_copy(sqp[:, h % 2, :].rearrange("p (b k) -> p b k", k=NS + S)[:, :, 0:S], sqT[:, h, :].rearrange("p (b s) -> p b s", s=S))\
               .then_inc(sem("d_qp"), 1)
        eng.wait_ge(sem("m_kw"), PT + 1)
        eng.wait_ge(sem("d_dec_ps"), 1)
        order(eng.tensor_copy(smn[:, :, :], ps[0:B, 2, 80:80 + 2 * HM].rearrange("p (a h) -> p a h", h=HM)))
        order(eng.tensor_copy(sdec[:, :], ps[:, 2, 96:96 + B * HM]))
        eng.wait_ge(sem("d_n_ps"), 1)
        for h in range(HM):
            ins = eng.scalar_tensor_tensor(out=snn[:, h * DM:(h + 1) * DM], in0=snn[:, h * DM:(h + 1) * DM],
                                           scalar=smn[:, 0, h:h + 1], in1=ps[0:B, 7, h * DM:(h + 1) * DM],
                                           op0=ALU.mult, op1=ALU.add)
        ins.then_inc(sem("d_n"), 1)
        for h in range(HM):
            eng.wait_ge(sem("m_update"), PT + h + 1)
            for b in range(B):
                j = b * HM + h
                ins = eng.scalar_tensor_tensor(out=sC[:, j, :], in0=sC[:, j, :], scalar=sdec[:, j:j + 1],
                                               in1=ps[:, update_banks[h][b // 4], (b % 4) * DM:(b % 4 + 1) * DM],
                                               op0=ALU.mult, op1=ALU.add)
            ins.then_inc(sem("d_C"), 1)
        eng.wait_ge(sem("m_num_ps"), PT + 1)
        eng.wait_ge(sem("d_qC_ps"), HM)
        for h in range(0, HM, 2):
            order(eng.tensor_copy(snum[:, h:h + 2, :], ps[r, h // 2, 0:2 * (DM + 1)]
                                  .rearrange("p (h n) -> p h n", n=DM + 1)))
        for h in range(HM):
            order(eng.scalar_tensor_tensor(out=snum[:, h, :], in0=two(3, h, NS), scalar=mev[r, 0, h:h + 1],
                                           in1=snum[:, h, :], op0=ALU.mult, op1=ALU.add))
        order(eng.scalar_tensor_tensor(out=mden[r, :], in0=snum[:, :, DM], scalar=-1.0, in1=snum[:, :, DM],
                                       op0=ALU.mult, op1=ALU.max))
        order(eng.tensor_tensor(mden[r, :], mden[r, :], mev[r, 1, :], ALU.max))
        order(eng.reciprocal(mden[r, :], mden[r, :]))
        for h in range(HM):
            ins = eng.scalar_tensor_tensor(out=sout[:, h, :], in0=snum[:, h, 0:DM], scalar=mden[r, h:h + 1],
                                           in1=tok[r, PT, OM + h * DM:OM + (h + 1) * DM],
                                           op0=ALU.mult, op1=ALU.mult)
        ins.then_inc(sem("m_h"), 1)
        eng.wait_ge(sem("m_high"), PT + 1)
        eng.tensor_tensor(mlT[1][:, :, T:NT], ps[:, 0, 0:HM * NS].rearrange("p (h n) -> p h n", n=NS),
                          mlT[0][:, :, T:NT].bitcast(F32), ALU.subtract).then_inc(sem("m_low"), 1)

    def act_states_out(eng):
        eng.wait_ge(sem("d_C"), HM)
        eng.wait_ge(sem("d_n"), 1)
        eng.dma_start(C_sample.rearrange("b h d e -> d (b h) e"), sC[:, :, :]).then_inc(sem("d_out"), 16)
        eng.dma_start(n_sample.rearrange("b h e -> b (h e)"), snn[:, :]).then_inc(sem("d_out"), 16)
        eng.dma_start(m_sample, smn[:, 1, :]).then_inc(sem("d_out"), 16)


    GROUPS = NPAGE // 4

    def pages(eng, pool, slots, arrived, free, b, before_second=None):
        flat = pool.rearrange("n p h d -> n p (h d)")
        for g in range(GROUPS):
            if g == 2 and before_second:
                before_second()
            for j in range(4):
                page = eng.value_load(pt_sb[0:1, bass.ds(b * NPAGE + g * 4 + j, 1)],
                                      min_val=0, max_val=pool.shape[0] - 1)
                h = g % len(slots)
                if j == 0:
                    eng.wait_ge(sem(free), b * GROUPS + g + 1)
                eng.dma_start(slots[h][:, j, :], flat[bass.ds(page, 1), :, :].rearrange("a p n -> (a p) n"))\
                   .then_inc(sem(f"{arrived}{h}"), 16)

    kslots = [kring[:, 4 * h:4 * h + 4, :] for h in range(2)]
    vslots = [vrings[h // 2][:, 4 * (h % 2):4 * (h % 2) + 4, :] for h in range(GROUPS)]

    def sp_keys(eng):
        eng.wait_ge(sem("small_in"), 64)
        with eng.Fori(0, B) as b:
            pages(eng, cache_k, kslots, "k_in", "k_free", b)

    def pool_values(eng):
        eng.wait_ge(sem("m_C_ps"), 1)
        for half in range(2):
            eng.memset(spow[:, half * (NS // 2):(half + 1) * (NS // 2)], 0.0).then_inc(sem("k_free"), 1)
        for part in range(4):
            eng.memset(spowT[:, part * (P // 4):(part + 1) * (P // 4)], 0.0).then_inc(sem("v_free"), 1)
        pool_keys_by_batch(eng)
        eng.wait_ge(sem("small_in"), 64)
        pages(eng, cache_v, vslots, "v_in", "v_free", 0, before_second=lambda: eng.wait_ge(sem("d_out"), 48))
        with eng.Fori(0, B - 1) as i:
            pages(eng, cache_v, vslots, "v_in", "v_free", i + 1)

    def in_turn(eng, body, order=None):
        body(0, None, None)
        body(1, 0, None)
        times = B - 2
        if order:
            c = order.count
            c.base, c.n = c.base + c.n, 0
            c.per = DVE_STEPS
        with eng.Fori(0, times) as i:
            if order:
                c.i = i
            body(i + 2, i + 1, i)
        if order:
            assert c.n == DVE_STEPS, c.n
            c.base, c.n, c.per, c.i = c.base + DVE_STEPS * times, 0, 0, None
        body(None, B - 1, B - 2)
        body(None, None, B - 1)

    DVE_STEPS = 22

    def wait(eng, name, value):
        if not isinstance(value, int) or value > 0:
            eng.wait_ge(sem(name), value)

    def sown_by(batch):
        return min(batch, B) if isinstance(batch, int) else batch

    def pe_decode(eng):
        eng.wait_ge(sem("m_low"), PT + 1)
        eng.wait_ge(sem("d_C"), HM)
        eng.wait_ge(sem("v_free"), 4)
        eng.matmul(ps[:, 6, 0:S], rep8[:, :], own8[:, :], start=True, stop=True).then_inc(sem("p_mask_ps"), 1)
        eng.wait_ge(sem("p_mask"), 1)

        def turn(k, g):
            wait(eng, f"k_in{g % 2}", k * 128 + 64 * (g // 2) + 64)
            for h in range(HP):
                wait(eng, "p_kT_act" if h % 2 == 0 else "p_kT_dve", k * 8 + max(2 * (g - 1) + h // 2 + 1, 0))
                for j in range(4):
                    mm = eng.transpose(ps[:, h, j * P:(j + 1) * P],
                                       kring[:, (g % 2) * 4 + j, h * P:(h + 1) * P], ident[:, :])
                if h < HP - 1:
                    mm.then_inc(sem("p_kT_ps"), 1)
            mm.then_inc(sem("k_free"), 1)

        def own(k):
            wait(eng, "p_q", k * 3 + 3)
            wait(eng, "p_O", k - 1)
            for h in range(HP):
                mm = eng.matmul(ps[32 * h:32 * h + 32, 7, P:P + S], qb[:, h, :], kb[:, h, :],
                                start=True, stop=True)
            mm.then_inc(sem("p_own_ps"), 1)

        def score(k, g):
            wait(eng, "p_kT_act", k * 8 + 2 * g + 2)
            wait(eng, "p_kT_dve", k * 8 + 2 * g + 2)
            wait(eng, "p_S", k * GROUPS + max(g - 1, 0))
            for h in range(HP):
                mm = eng.matmul(ps[32 * h:32 * h + 32, 4 + g % 2, :], qb[:, h, :], kT[:, g % 2, h, :],
                                start=True, stop=True)
            mm.then_inc(sem("p_S_ps"), 1)

        def turn_probs(v, g):
            wait(eng, "p_exp", v * BLOCKS + 2 * g + 2)
            wait(eng, "p_PT", v * GROUPS + g)
            for j in range(4):
                c = (4 * g + j) * P
                if g == 0 and j == 3:
                    wait(eng, "p_own", v + 1)
                    wait(eng, "p_low", v * 2)
                    wait(eng, "p_sown", sown_by(v + 2))
                mm = eng.transpose(ps[:, 6, j * P:(j + 1) * P], sS[:, c:c + P], ident[:, :])
            mm.then_inc(sem("p_PT_ps"), 1)

        def turn_own(v):
            eng.transpose(ps[0:NS, 7, 2 * P:3 * P], spow[:, :], ident[:, :]).then_inc(sem("p_ownT_ps"), 1)

        def values(v, g):
            wait(eng, f"v_in{g}", v * 64 + 64)
            wait(eng, "p_PT", v * GROUPS + g + 1)
            if g == 0:
                wait(eng, "p_ownT", v + 1)
            for j in range(4):
                for h in range(HP):
                    mm = eng.matmul(ps[32 * h:32 * h + 32, 7, 0:P], sPT[:, g % 2, j, 32 * h:32 * h + 32],
                                    vslots[g][:, j, h * P:(h + 1) * P],
                                    start=(g == 0 and j == 0), stop=False)
            mm.then_inc(sem("v_free"), 1)

        def own_values(v):
            for h in range(HP):
                mm = eng.matmul(ps[32 * h:32 * h + 32, 7, 0:P], spowT[:, 32 * h:32 * h + 32],
                                tok[0:NS, PT, VA + h * P:VA + (h + 1) * P], start=False, stop=True)
            mm.then_inc(sem("p_O_ps"), 1)

        def turn_out(o):
            wait(eng, "p_O", o + 1)
            wait(eng, "p_sown", sown_by(o + 3))
            eng.transpose(ps[:, 7, 3 * P:4 * P], sO[:, :], ident[:, :]).then_inc(sem("p_OT_ps"), 1)

        def body(k, v, o):
            plan = [(turn, k, 0), (own, k), (turn, k, 1), (turn_out, o), (score, k, 0),
                    (turn_probs, v, 0), (turn_own, v), (score, k, 1), (turn, k, 2), (values, v, 0),
                    (turn_probs, v, 1), (score, k, 2), (turn, k, 3), (values, v, 1),
                    (turn_probs, v, 2), (score, k, 3), (turn_probs, v, 3), (values, v, 2),
                    (values, v, 3), (own_values, v)]
            for step, batch, *g in plan:
                if batch is not None:
                    step(batch, *g)

        in_turn(eng, body)
        eng.wait_ge(sem("p_low"), 2 * B)

    def act_decode(eng):
        eng.wait_ge(sem("m_low"), PT + 1)
        eng.wait_ge(sem("v_free"), 4)

        def keys(k, g):
            for h in (0, 2):
                wait(eng, "p_kT_ps", k * 12 + 3 * g + h + 1)
                wait(eng, "p_S_ps", k * GROUPS + max(g - 1, 0))
                eng.activation(kT[:, g % 2, h, :], ps[:, h, :], ACT.Copy).then_inc(sem("p_kT_act"), 1)

        def scores(k, g):
            wait(eng, "p_S_ps", k * GROUPS + g + 1)
            wait(eng, "p_PT_ps", k * GROUPS + (g + 1 - GROUPS))
            eng.activation(sS[:, g * CH:(g + 1) * CH], ps[:, 4 + g % 2, :], ACT.Copy).then_inc(sem("p_S"), 1)

        def exps(v, g):
            if g == 0:
                wait(eng, "p_bias", v + 1)
            for n in (2 * g, 2 * g + 1):
                c = slice(n * 2 * PAGE, (n + 1) * 2 * PAGE)
                eng.activation(sS[:, c], sS[:, c], ACT.Exp, bias=sbias[:, n:n + 1], scale=SC,
                               accum_out=srs[:, n:n + 1]).then_inc(sem("p_exp"), 1)

        def own(v):
            eng.activation(spow[:, bass.ds(v * S, S)], sown[:, :], ACT.Exp, bias=snx[:, :], scale=SC,
                           accum_out=srs[:, BLOCKS:BLOCKS + 1]).then_inc(sem("p_own"), 1)

        def probs(v, g):
            wait(eng, "p_PT_ps", v * GROUPS + g + 1)
            if g >= 2:
                wait(eng, "v_free", v * GROUPS + g - 1 + 4)
            eng.activation(sPT[:, g % 2, :, :], ps[:, 6, :].rearrange("p (j n) -> p j n", n=P), ACT.Copy)\
               .then_inc(sem("p_PT"), 1)

        def out(o):
            wait(eng, "p_OT_ps", o + 1)
            for k in range(2):
                g = slice(k * DH, (k + 1) * DH)
                eng.activation(out_cols(attT[0], o, g), turned_out(k), ACT.Copy).then_inc(sem("p_high"), 1)

        def body(k, v, o):
            plan = [(keys, k, 0), (keys, k, 1), (out, o), (exps, v, 0), (own, v), (exps, v, 1),
                    (probs, v, 0), (scores, k, 0), (keys, k, 2), (exps, v, 2),
                    (probs, v, 1), (scores, k, 1), (keys, k, 3), (exps, v, 3),
                    (probs, v, 2), (scores, k, 2), (scores, k, 3), (probs, v, 3)]
            for step, batch, *g in plan:
                if batch is not None:
                    step(batch, *g)

        in_turn(eng, body)

    def out_cols(dst, b, g):
        return dst[g, :, bass.ds(b * S + T, S)]

    def turned_out(k):
        g = slice(k * DH, (k + 1) * DH)
        return ps[g, 7, 3 * P:4 * P].rearrange("p (h n) -> p h n", n=32)[:, :, k * S:(k + 1) * S]

    def dve_decode(eng):
        order = Order(eng, sem("p_steps"), Count())
        eng.wait_ge(sem("v_free"), 4)
        eng.wait_ge(sem("p_mask_ps"), 1)
        eng.tensor_copy(ownmask[:, :], ps[:, 6, 0:S]).then_inc(sem("p_mask"), 1)
        eng.wait_ge(sem("p_mask"), 1)

        def queries(k):
            wait(eng, "p_S_ps", k * GROUPS)
            wait(eng, "p_own_ps", k)
            for j in range(2):
                g = slice(j * DH, (j + 1) * DH)
                eng.tensor_copy(qb[g, :, j * S:(j + 1) * S], QTs[g, :, bass.ds(k * S, S)]).then_inc(sem("p_q"), 1)
            eng.tensor_copy(kb[:, :, :], KTs[:, :, bass.ds(k * S, S)]).then_inc(sem("p_q"), 1)

        def keys(k, g):
            for h in (1, 3):
                if h == 1:
                    wait(eng, "p_kT_ps", k * 12 + 3 * g + 2)
                else:
                    wait(eng, "k_free", k * GROUPS + g + 1 + 2)
                wait(eng, "p_S_ps", k * GROUPS + max(g - 1, 0))
                eng.tensor_copy(kT[:, g % 2, h, :], ps[:, h, :]).then_inc(sem("p_kT_dve"), 1)

        def own(k):
            wait(eng, "p_own_ps", k + 1)
            eng.tensor_tensor(snext[:, :], ps[:, 7, P:P + S], ownmask[:, :], ALU.add).then_inc(sem("p_sown"), 1)
            wait(eng, "p_sown", k + 1)
            order(eng.tensor_reduce(smax[:, BLOCKS:BLOCKS + 1], snext[:, :], X, ALU.max))

        def reduce(k, g):
            s = sS[:, g * CH:(g + 1) * CH].rearrange("p (n k) -> p n k", k=2 * PAGE)
            wait(eng, "p_S", k * GROUPS + g + 1)
            eng.tensor_reduce(ssum[:, 2 * g:2 * g + 2], s, X, ALU.add).then_inc(sem("p_steps"), 1)
            order.count.add()
            order(eng.tensor_reduce(smax[:, 2 * g:2 * g + 2], s, X, ALU.max))

        def choose(k):
            wait(eng, "p_own", k)
            order(eng.tensor_copy(sown[:, :], snext[:, :]))
            full = [P, BLOCKS, BLOCKS]
            of_n = ssum[:, :].unsqueeze(2).broadcast_to(full)
            of_m = ssum[:, :].unsqueeze(1).broadcast_to(full)
            order(eng.tensor_tensor(seq[:, :, :], of_m, of_n, ALU.is_equal))
            order(eng.tensor_tensor(seq[:, :, :], seq[:, :, :], earlier[:, :, :], ALU.mult))
            order(eng.tensor_tensor(scmp[:, :, :], of_m, of_n, ALU.is_gt))
            order(eng.tensor_tensor(scmp[:, :, :], scmp[:, :, :], seq[:, :, :], ALU.add))
            order(eng.tensor_reduce(srank[:, :], scmp[:, :, :], X, ALU.add))
            order(eng.tensor_scalar(sneg[:, :], srank[:, :], TOPK - 0.5, NEG, ALU.is_gt, ALU.mult))
            order(eng.tensor_tensor(smax[:, 0:BLOCKS], smax[:, 0:BLOCKS], sneg[:, :], ALU.add))
            order(eng.tensor_reduce(smx[:, :], smax[:, :], X, ALU.max))
            order(eng.tensor_scalar(snx[:, :], smx[:, :], -SC, None, ALU.mult))
            order(eng.memset(spow[:, :], 0.0))
            eng.tensor_scalar(sbias[:, :], sneg[:, :], snx[:, :], None, ALU.add).then_inc(sem("p_bias"), 1)

        def own_probs(v):
            wait(eng, "p_ownT_ps", v + 1)
            eng.tensor_copy(spowT[:, :], ps[0:NS, 7, 2 * P:3 * P]).then_inc(sem("p_ownT"), 1)

        def total(v):
            wait(eng, "p_exp", v * BLOCKS + BLOCKS)
            wait(eng, "p_own", v + 1)
            order(eng.tensor_reduce(srt[:, :], srs[:, :], X, ALU.add))
            order(eng.reciprocal(sri[:, :], srt[:, :]))

        def divide(v):
            wait(eng, "p_O_ps", v + 1)
            eng.tensor_scalar(sO[:, :], ps[:, 7, 0:P], sri[:, :], None, ALU.mult).then_inc(sem("p_O"), 1)

        def out(o):
            wait(eng, "p_high", o * 2 + 2)
            for k in range(2):
                g = slice(k * DH, (k + 1) * DH)
                eng.tensor_tensor(out_cols(attT[1], o, g), turned_out(k), out_cols(attT[0], o, g).bitcast(F32),
                                  ALU.subtract).then_inc(sem("p_low"), 1)

        def body(k, v, o):
            plan = [(queries, k), (keys, k, 0), (own, k), (keys, k, 1), (out, o), (own_probs, v),
                    (reduce, k, 0), (keys, k, 2), (reduce, k, 1), (keys, k, 3), (total, v),
                    (reduce, k, 2), (reduce, k, 3), (choose, k), (divide, v)]
            for step, batch, *g in plan:
                if batch is not None:
                    step(batch, *g)

        in_turn(eng, body, order)


    MERGE = steps(8) | banks(8, 8)

    def merge_rows(k, c):
        w = w_attn_br if k < 4 else w_mlstm_br
        return w[(k % 4) * P:(k % 4 + 1) * P, c * CH:(c + 1) * CH]

    def sp_merge_first(eng, n):
        for k in range(AHEAD):
            w_load(eng, n, merge_rows(k, 0))

    def sp_merge_rest(eng, n):
        for c in range(2):
            for k in range(AHEAD if c == 0 else 0, 8):
                w_load(eng, n, merge_rows(k, c))
        with n.loop(2, ALL8) as c:
            for k in range(KT):
                w_load(eng, n, w_out[k * P:(k + 1) * P, bass.ds(c * CH, CH)])

    def pe_merge(eng, n):
        with n.loop(2, MERGE):
            features_chunk(eng, n, attT, HP)
            features_chunk(eng, n, mlT, HM)
        eng.wait_ge(sem("u_low"), 16)
        with n.loop(2, ALL8 | banks(TILES)):
            tokens_chunk(eng, n, uT, KT)

    def u_at(dst, c, b):
        return dst[:, bass.ds(c * (4 * NT) + (b // 2) * NT + (b % 2) * HALFT, HALFT)]

    uT_flat = [a[:, :, :].rearrange("p k n -> p (k n)") for a in uT]
    u32_flat = u32[:, :, :].rearrange("p k n -> p (k n)")
    sgm = sg[:, KT * NT:2 * KT * NT]

    def act_merge(eng, n):
        for _ in range(AHEAD):
            w_high(eng, n)
        with n.loop(2, MERGE) as c:
            for _ in range(4):
                w_high(eng, n)
            for b in range(8):
                skip(n, b, b == 7)
            for _ in range(4):
                w_high(eng, n)
            for b in range(8):
                skip(n, b, b == 7)
                eng.wait_ge(sem("u_sum"), c * 8 + b + 1)
                eng.activation(u_at(uT_flat[0], c, b), u_at(u32_flat, c, b), ACT.Copy).then_inc(sem("u_high"), 1)
        with n.loop(2, ALL8 | banks(TILES)) as c:
            for _ in range(KT):
                w_high(eng, n)
            copy_tokens(eng, n, lambda t: wide[0:rows(t), t, bass.ds(c * CH, CH)], 0)
        merged_norm_act(eng, n)

    def dve_merge(eng, n):
        for _ in range(AHEAD):
            w_low(eng, n)
        with n.loop(2, MERGE) as c:
            for _ in range(4):
                w_low(eng, n)
            for b in range(8):
                drain(eng, n, b, b == 7)
                drained(eng.tensor_tensor(u_at(u32_flat, c, b), ps[:, b, 0:HALFT], u_at(sg, c, b), ALU.mult), n, b)
            for _ in range(4):
                w_low(eng, n)
            for b in range(8):
                drain(eng, n, b, b == 7)
                drained(eng.tensor_tensor(u_at(sgm, c, b), ps[:, b, 0:HALFT], u_at(sgm, c, b), ALU.mult), n, b)
                eng.wait_ge(sem(f"free{b}"), n[f"free{b}"].value())
                eng.tensor_tensor(u_at(u32_flat, c, b), u_at(u32_flat, c, b), u_at(sgm, c, b), ALU.add)\
                   .then_inc(sem("u_sum"), 1)
            for b in range(8):
                eng.wait_ge(sem("u_high"), c * 8 + b + 1)
                eng.tensor_tensor(u_at(uT_flat[1], c, b), u_at(u32_flat, c, b),
                                  u_at(uT_flat[0], c, b).bitcast(F32), ALU.subtract).then_inc(sem("u_low"), 1)
        with n.loop(2, ALL8 | banks(TILES)) as c:
            for _ in range(KT):
                w_low(eng, n)
            copy_tokens(eng, n, lambda t: wide[0:rows(t), t, bass.ds(c * CH, CH)], 1)
        merged_norm_dve(eng, n)

    def wide_whole(eng, n):
        for t in range(TILES):
            eng.wait_ge(sem(f"free{t}"), n[f"free{t}"].value())

    def merged_norm_act(eng, n):
        norm_stats(eng, 1, wide, lambda e, t: e.wait_ge(sem(f"free{t}"), n[f"free{t}"].value()))
        norm_stats(eng, 2, x, lambda e, t: e.wait_ge(sem("x_sum"), t + 1))
        turn_act(eng, n, 2, h2T)

    def merged_norm_dve(eng, n):
        wide_whole(eng, n)
        eng.wait_ge(sem("g_in"), 16)
        add_norm(eng, 1)
        eng.wait_ge(sem("g_in"), 32)
        norm_and_turn(eng, n, 2, x, h2T)
        eng.memset(wide[:, :, :], 0.0).then_inc(sem("y_zero"), 1)


    FB = FF // D
    MLP = steps(32) | banks(8, 8, TILES, TILES)
    rl = sb("rl", [P, 8, HALFT], F32, offset=R2)

    def mlp_passes(eng, n, counts, body):
        with n.loop(FB - 1, counts) as i:
            body(i, False)
        body(FB - 1, True)

    def sp_mlp(eng, n):
        def body(i, last):
            for c in range(2):
                for k in range(KT):
                    w_load(eng, n, w_up[k * P:(k + 1) * P, bass.ds(i * D + c * CH, CH)])
            for c in range(2):
                for k in range(KT):
                    w_load(eng, n, w_down[bass.ds(i * D + k * P, P), c * CH:(c + 1) * CH])
        mlp_passes(eng, n, steps(32), body)

    def pe_mlp(eng, n):
        def body(i, last):
            for c in range(2):
                features_chunk(eng, n, h2T, KT)
            tokens_chunk(eng, n, hid, KT, lambda k: eng.wait_ge(sem("hid_low"), i * 16 + 2 * k + 2))
            tokens_chunk(eng, n, hid, KT)
        all_out(eng, n)
        mlp_passes(eng, n, MLP, body)

    def act_mlp(eng, n):
        def body(i, last):
            for c in range(2):
                for _ in range(KT):
                    w_high(eng, n)
                for b in range(9):
                    if b < 8:
                        drain(eng, n, b, b == 7)
                        eng.wait_ge(sem("hid_low"), i * 16 + 8 * c)
                        drained(eng.activation(rl[:, b, :], ps[:, b, 0:HALFT], ACT.Relu), n, b)
                    if b >= 1:
                        u = b - 1
                        eng.wait_ge(sem("hid_sq"), i * 16 + 8 * c + u + 1)
                        k = 4 * c + u // 2
                        eng.activation(hid[0][:, k, (u % 2) * HALFT:(u % 2 + 1) * HALFT], rl[:, u, :], ACT.Copy)\
                           .then_inc(sem("hid_high"), 1)
            for c in range(2):
                for _ in range(KT - (AHEAD if last and c == 1 else 0)):
                    w_high(eng, n)
                for t in range(TILES):
                    skip(n, t, t == TILES - 1)
        mlp_passes(eng, n, MLP, body)

    def dve_mlp(eng, n):
        def body(i, last):
            for c in range(2):
                for _ in range(KT):
                    w_low(eng, n)
                for b in range(9):
                    if b < 8:
                        eng.wait_ge(sem(f"free{b}"), n[f"free{b}"].value(1, 1))
                        skip(n, b, b == 7)
                        eng.tensor_tensor(rl[:, b, :], rl[:, b, :], rl[:, b, :], ALU.mult).then_inc(sem("hid_sq"), 1)
                    if b >= 1:
                        u = b - 1
                        eng.wait_ge(sem("hid_high"), i * 16 + 8 * c + u + 1)
                        k = 4 * c + u // 2
                        half = slice((u % 2) * HALFT, (u % 2 + 1) * HALFT)
                        eng.tensor_tensor(hid[1][:, k, half], rl[:, u, :], hid[0][:, k, half].bitcast(F32),
                                          ALU.subtract).then_inc(sem("hid_low"), 1)
            for c in range(2):
                for _ in range(KT - (AHEAD if last and c == 1 else 0)):
                    w_low(eng, n)
                for t in range(TILES):
                    drain(eng, n, t, t == TILES - 1)
                    y = wide[0:rows(t), t, c * CH:(c + 1) * CH]
                    drained(eng.tensor_tensor(y, ps[bank_rows(t), t, :], y, ALU.add), n, t)
        eng.wait_ge(sem("y_zero"), 1)
        mlp_passes(eng, n, MLP, body)


    def act_out(eng, n):
        norm_stats(eng, 3, wide, lambda e, t: e.wait_ge(sem(f"free{t}"), n[f"free{t}"].value()))

    def dve_out(eng, n):
        wide_whole(eng, n)
        eng.wait_ge(sem("g_in"), 48)
        add_norm(eng, 3)

    def sp_out(eng):
        for t in range(PT):
            eng.wait_ge(sem("x_sum"), TILES + t + 1)
            eng.dma_start(y_prompt[0, t * P:(t + 1) * P, :], x[:, t, :]).then_inc(sem("y_out"), 16)
        eng.wait_ge(sem("x_sum"), 2 * TILES)
        eng.dma_start(y_sample.rearrange("b s d -> (b s) d"), x[0:NS, PT, :]).then_inc(sem("y_out"), 16)
        eng.wait_ge(sem("y_out"), 16 * TILES)
        eng.wait_ge(sem("kv_out"), 64)
        eng.wait_ge(sem("m_out"), 48)
        eng.wait_ge(sem("d_out"), 48)


    with stack:
        block = stack.enter_context(nc.Block())

        @block.sync
        def _(eng):
            n = Counts(eng)
            load_x(eng, "x_in")
            sp_project(eng, n)
            sp_merge_first(eng, n)
            sp_states(eng)
            sp_keys(eng)
            eng.wait_ge(sem("k_free"), 2 + B * GROUPS)
            load_x(eng, "x_in")
            sp_merge_rest(eng, n)
            sp_mlp(eng, n)
            sp_out(eng)

        @block.gpsimd
        def _(eng):
            constants(eng)
            eng.wait_ge(sem("normed"), TILES)
            load_g(eng, g_post_mix)
            pool_rotary(eng)
            pool_heads(eng)
            pool_mlstm(eng)
            pool_states(eng)
            pool_mlstm_out(eng)
            pool_values(eng)
            eng.wait_ge(sem("normed"), 2 * TILES)
            load_g(eng, g_pre_mlp)
            eng.wait_ge(sem("normed"), 3 * TILES)
            load_g(eng, g_post_mlp)

        @block.scalar
        def _(eng):
            n = Counts(eng)
            load_g(eng, g_pre_mix, "g_first")
            eng.dma_start(bif[:, :], b_if.rearrange("(p a) -> p a", a=1)).then_inc(sem("small_in"), 16)
            eng.dma_start(rot[:, :, :], rotary.rearrange("(t p) n -> p t n", p=P)).then_inc(sem("small_in"), 16)
            eng.dma_start(pt_sb[:, :], page_table.rearrange("(a b) n -> a (b n)", a=1)).then_inc(sem("small_in"), 16)
            eng.dma_start(smb[:, :], state_m).then_inc(sem("small_in"), 16)
            constants_ready(eng)
            norm_stats(eng, 0, x, lambda e, t: e.wait_ge(sem(f"x_in{t}"), 16))
            for _ in range(AHEAD):
                w_high(eng, n)
            turn_act(eng, n, 0, hT)
            act_project(eng, n)
            act_gates(eng)
            act_prompt(eng)
            act_mlstm(eng)
            act_sample(eng)
            act_states_out(eng)
            act_decode(eng)
            act_merge(eng, n)
            act_mlp(eng, n)
            act_out(eng, n)

        @block.vector
        def _(eng):
            n = Counts(eng)
            constants_ready(eng)
            eng.wait_ge(sem("g_first"), 16)
            norm_and_turn(eng, n, 0, x, hT)
            for _ in range(AHEAD):
                w_low(eng, n)
            dve_project(eng, n)
            dve_gates(eng)
            dve_prompt(eng)
            dve_mlstm(eng)
            dve_sample(eng)
            dve_decode(eng)
            dve_merge(eng, n)
            dve_mlp(eng, n)
            dve_out(eng, n)

        @block.tensor
        def _(eng):
            n = Counts(eng)
            constants_ready(eng)
            turn_pe(eng, n, 0)
            all_out(eng, n)
            pe_project(eng, n)
            all_out(eng, n)
            pe_gates(eng)
            pe_prompt(eng)
            pe_mlstm(eng)
            pe_sample(eng)
            pe_decode(eng)
            pe_merge(eng, n)
            turn_pe(eng, n, 2)
            pe_mlp(eng, n)



def rotary_table():
    import numpy as np
    half = HALF
    inv = (np.float32(500000.0) ** (-np.arange(half, dtype=np.float32) * np.float32(2.0) / np.float32(2 * half)))
    pos = np.zeros(TILES * P, np.float32)
    pos[:T] = np.arange(T)
    pos[T:NT] = PAST + np.arange(NS) % S
    ang = (pos[:, None] * inv[None, :].astype(np.float32)).astype(np.float32).astype(np.float64)
    return np.concatenate([np.cos(ang), np.sin(ang)], axis=1).astype(np.float32)


_INS = ["x_prompt", "x_sample", "cache_k", "cache_v", "state_C", "state_n", "state_m", "page_table",
        "g_pre_mix", "w_in", "b_if", "w_attn_br", "w_mlstm_br", "w_out", "g_post_mix", "g_pre_mlp",
        "w_up", "w_down", "g_post_mlp"]
_OUTS = [(1, T, D), (B, S, D), (1, T, HA, DH), (1, T, HA, DH), (1, HM, DM, DM), (1, HM, DM), (1, HM),
         (B, S, HA, DH), (B, S, HA, DH), (B, HM, DM, DM), (B, HM, DM), (B, HM)]


def kernel(**inputs):
    import numpy as _np
    import concourse.bacc as _bacc
    from concourse.bass_utils import run_bass_kernel_spmd as _run

    nc = _bacc.Bacc("TRN2", target_bir_lowering=False, num_devices=1)
    arrays, args = {}, []
    for name, a in [(k, _np.ascontiguousarray(inputs[k])) for k in _INS] + [("rotary", rotary_table())]:
        arrays[f"in_{name}_dram"] = a
        args.append(nc.dram_tensor(f"in_{name}_dram", a.shape, mybir.dt.from_np(a.dtype), kind="ExternalInput").ap())
    for i, shape in enumerate(_OUTS):
        args.append(nc.dram_tensor(f"out_{i}_dram", shape, F32, kind="ExternalOutput").ap())
    moba_mlstm_step(nc, *args)
    r = _run(nc, [arrays], core_ids=[0])
    return tuple(r.results[0][f"out_{i}_dram"] for i in range(len(_OUTS)))
```
